# Optimizing a Trainium2 kernel written in Bass

```python
import jax, jax.numpy as jnp
from jax import lax
import numpy as np
import math

D_MODEL = 1024
BATCH = 1
SEQ = 512
DEPTH = 2

GRID_W = 64
CTX_LEN = 256
HEAD_DIM = 64
N_Q_HEADS = 8
N_KV_HEADS = 2
GQA_GROUP = N_Q_HEADS // N_KV_HEADS
ATTN_WIDTH = N_Q_HEADS * HEAD_DIM
KV_WIDTH = N_KV_HEADS * HEAD_DIM
CONV_GROUPS = 4
CONV_WIDTH = CONV_GROUPS * 64
CONV_K = 3
FOURIER_GROUPS = 4
FOURIER_GROUP_DIM = 64
FOURIER_WIDTH = FOURIER_GROUPS * FOURIER_GROUP_DIM
N_BRANCHES = 3
D_FF = 4 * D_MODEL
Q_BLOCK = 128
ROPE_THETA = 10000.0
ROPE_HALF = HEAD_DIM // 2
EPS = 1e-6
N_MOD = 6

OFF_B = 0
OFF_C = OFF_B + CONV_WIDTH
OFF_X = OFF_C + CONV_WIDTH
OFF_F = OFF_X + CONV_WIDTH
OFF_Q = OFF_F + FOURIER_WIDTH
OFF_K = OFF_Q + ATTN_WIDTH
OFF_V = OFF_K + KV_WIDTH
OFF_G = OFF_V + KV_WIDTH
IN_WIDTH = OFF_G + N_BRANCHES * D_MODEL


def rms_norm(x, g):
    xf = x.astype(jnp.float32)
    y = xf * lax.rsqrt(jnp.mean(xf * xf, axis=-1, keepdims=True) + EPS)
    return (y * g.astype(jnp.float32)).astype(x.dtype)

def modulate(x, g, shift, scale):
    return rms_norm(x, g) * (1 + scale) + shift

def axial_rope_tables(rows):
    n_freq = ROPE_HALF // 2
    inv = ROPE_THETA ** (-jnp.arange(n_freq, dtype=jnp.float32) / n_freq)
    row_ang = jnp.repeat(jnp.arange(rows, dtype=jnp.float32)[:, None] * inv, GRID_W, axis=0)
    col_ang = jnp.tile(jnp.arange(GRID_W, dtype=jnp.float32)[:, None] * inv, (rows, 1))
    ang = jnp.concatenate([row_ang, col_ang], axis=-1)
    return jnp.cos(ang), jnp.sin(ang)

def apply_rope(x, cos, sin):
    xf = x.astype(jnp.float32)
    x1, x2 = xf[..., :ROPE_HALF], xf[..., ROPE_HALF:]
    c = cos[None, :, None, :]
    s = sin[None, :, None, :]
    return jnp.concatenate([x1 * c - x2 * s, x1 * s + x2 * c], axis=-1).astype(x.dtype)

def short_conv(u, w):
    L = u.shape[1]
    pad = CONV_K // 2
    up = jnp.pad(u, ((0, 0), (pad, pad), (0, 0)))
    return sum(up[:, j:j + L] * w[j] for j in range(CONV_K))

def fourier_mix(u):
    b, L, _ = u.shape
    ug = u.astype(jnp.float32).reshape(b, L, FOURIER_GROUPS, FOURIER_GROUP_DIM)
    y = jnp.fft.fft2(ug, axes=(1, 3), norm="ortho").real
    return y.reshape(b, L, FOURIER_WIDTH).astype(u.dtype)

def local_branches(z, w_conv):
    y_conv = z[..., OFF_B:OFF_C] * short_conv(z[..., OFF_C:OFF_X] * z[..., OFF_X:OFF_F], w_conv)
    y_four = fourier_mix(z[..., OFF_F:OFF_Q])
    return y_conv, y_four

def qkv_heads(z, g_q, g_k):
    b, L, _ = z.shape
    q = rms_norm(z[..., OFF_Q:OFF_K].reshape(b, L, N_Q_HEADS, HEAD_DIM), g_q)
    k = rms_norm(z[..., OFF_K:OFF_V].reshape(b, L, N_KV_HEADS, HEAD_DIM), g_k)
    v = z[..., OFF_V:OFF_G].reshape(b, L, N_KV_HEADS, HEAD_DIM)
    return q, k, v

def gqa(q, k, v):
    b, lq = q.shape[:2]
    qg = q.reshape(b, lq, N_KV_HEADS, GQA_GROUP, HEAD_DIM)
    s = jnp.einsum('bqgrd,bkgd->bgrqk', qg, k).astype(jnp.float32) * (HEAD_DIM ** -0.5)
    p = jax.nn.softmax(s, axis=-1).astype(v.dtype)
    o = jnp.einsum('bgrqk,bkgd->bqgrd', p, v)
    return o.reshape(b, lq, ATTN_WIDTH)

def blocked_gqa(q, k, v):
    b, lq = q.shape[:2]
    nb = lq // Q_BLOCK
    qb = q.reshape(b, nb, Q_BLOCK, N_Q_HEADS, HEAD_DIM).transpose(1, 0, 2, 3, 4)
    ob = lax.map(lambda qi: gqa(qi, k, v), qb)
    return ob.transpose(1, 0, 2, 3).reshape(b, lq, ATTN_WIDTH)

def merge_branches(z, y_conv, y_four, y_attn, w_conv_out, w_four_out, w_attn_out, w_o):
    gates = jax.nn.sigmoid(z[..., OFF_G:].astype(jnp.float32)).astype(z.dtype)
    g_conv, g_four, g_attn = jnp.split(gates, N_BRANCHES, axis=-1)
    m = g_conv * (y_conv @ w_conv_out) + g_four * (y_four @ w_four_out) + g_attn * (y_attn @ w_attn_out)
    return m @ w_o

def sq_relu_mlp(h, w1, w2):
    return jnp.square(jax.nn.relu(h @ w1)) @ w2

def first_inputs(seed: int = 0) -> dict:
    key = jax.random.key(seed)
    ks = jax.random.split(key, 20)
    f32 = jnp.float32
    nrm = lambda k, shape, s: jax.random.normal(k, shape, f32) * s
    return {
        "x": nrm(ks[0], (BATCH, SEQ, D_MODEL), 1.0),
        "c": nrm(ks[1], (BATCH, D_MODEL), 1.0),
        "ctx": nrm(ks[2], (BATCH, CTX_LEN, D_MODEL), 1.0),
        "c_ctx": nrm(ks[3], (D_MODEL,), 1.0),
        "w_mod": nrm(ks[4], (DEPTH, D_MODEL, N_MOD * D_MODEL), 0.5 * D_MODEL ** -0.5),
        "b_mod": nrm(ks[5], (DEPTH, N_MOD * D_MODEL), 0.01),
        "g_norm1": 1.0 + nrm(ks[6], (DEPTH, D_MODEL), 0.05),
        "g_norm2": 1.0 + nrm(ks[7], (DEPTH, D_MODEL), 0.05),
        "w_in": nrm(ks[8], (DEPTH, D_MODEL, IN_WIDTH), D_MODEL ** -0.5),
        "w_conv": nrm(ks[9], (DEPTH, CONV_K, CONV_WIDTH), CONV_K ** -0.5),
        "g_q": 1.0 + nrm(ks[10], (DEPTH, HEAD_DIM), 0.05),
        "g_k": 1.0 + nrm(ks[11], (DEPTH, HEAD_DIM), 0.05),
        "w_conv_out": nrm(ks[12], (DEPTH, CONV_WIDTH, D_MODEL), CONV_WIDTH ** -0.5),
        "w_four_out": nrm(ks[13], (DEPTH, FOURIER_WIDTH, D_MODEL), FOURIER_WIDTH ** -0.5),
        "w_attn_out": nrm(ks[14], (DEPTH, ATTN_WIDTH, D_MODEL), ATTN_WIDTH ** -0.5),
        "w_o": nrm(ks[15], (DEPTH, D_MODEL, D_MODEL), D_MODEL ** -0.5),
        "w_ff1": nrm(ks[16], (DEPTH, D_MODEL, D_FF), D_MODEL ** -0.5),
        "w_ff2": nrm(ks[17], (DEPTH, D_FF, D_MODEL), D_FF ** -0.5),
    }

def first_block(x, c, ctx, c_ctx, w_mod, b_mod, g_norm1, g_norm2, w_in, w_conv, g_q, g_k,
              w_conv_out, w_four_out, w_attn_out, w_o, w_ff1, w_ff2):
    S = x.shape[1]
    ROWS = S // GRID_W
    cos, sin = axial_rope_tables(ROWS)
    ctx_s = ctx
    for l in range(DEPTH):
        mod = (jax.nn.silu(c) @ w_mod[l] + b_mod[l])[:, None, :]
        mod_c = (jax.nn.silu(c_ctx)[None] @ w_mod[l] + b_mod[l])[:, None, :]
        sh1, sc1, gt1, sh2, sc2, gt2 = jnp.split(mod, N_MOD, axis=-1)
        csh1, csc1, cgt1, csh2, csc2, cgt2 = jnp.split(mod_c, N_MOD, axis=-1)

        hc = modulate(ctx_s, g_norm1[l], csh1, csc1)
        zc = hc @ w_in[l]
        qc, kc, vc = qkv_heads(zc, g_q[l], g_k[l])

        h = modulate(x, g_norm1[l], sh1, sc1)
        z = h @ w_in[l]
        q, k, v = qkv_heads(z, g_q[l], g_k[l])
        q = apply_rope(q, cos, sin)
        k = apply_rope(k, cos, sin)
        k_all = jnp.concatenate([k, kc], axis=1)
        v_all = jnp.concatenate([v, vc], axis=1)
        y_attn = blocked_gqa(q, k_all, v_all)
        y_conv, y_four = local_branches(z, w_conv[l])
        x = x + gt1 * merge_branches(z, y_conv, y_four, y_attn,
                                     w_conv_out[l], w_four_out[l], w_attn_out[l], w_o[l])
        x = x + gt2 * sq_relu_mlp(modulate(x, g_norm2[l], sh2, sc2), w_ff1[l], w_ff2[l])

        if l < DEPTH - 1:
            yc_attn = gqa(qc, kc, vc)
            yc_conv, yc_four = local_branches(zc, w_conv[l])
            ctx_s = ctx_s + cgt1 * merge_branches(zc, yc_conv, yc_four, yc_attn,
                                                  w_conv_out[l], w_four_out[l], w_attn_out[l], w_o[l])
            ctx_s = ctx_s + cgt2 * sq_relu_mlp(modulate(ctx_s, g_norm2[l], csh2, csc2),
                                               w_ff1[l], w_ff2[l])
    return x


N_EVEN = (DEPTH + 1) // 2
N_ODD = DEPTH // 2

CONF_WIDTH = D_MODEL // 2
CONF_KERNEL = 31
LRU_WIDTH = D_MODEL // 2
LRU_HEADS = 8
LRU_HEAD_DIM = LRU_WIDTH // LRU_HEADS
LRU_CONV = 4
LRU_C = 8.0
AB_IN = 2 * CONF_WIDTH + 2 * LRU_WIDTH
AB_OUT = CONF_WIDTH + LRU_WIDTH
ML_HEADS = 8
ML_V_DIM = D_MODEL
ML_HEAD_V = ML_V_DIM // ML_HEADS
ML_HEAD_QK = ML_HEAD_V // 2
ML_QK_DIM = ML_HEADS * ML_HEAD_QK
ML_CHUNK = 64
ML_IN = 2 * ML_QK_DIM + 2 * ML_V_DIM + 2 * ML_HEADS
D_FF_2 = int(math.ceil(8 * D_MODEL / 3 / 256)) * 256


def _rmsnorm(x, g):
    xf = x.astype(jnp.float32)
    y = xf * lax.rsqrt(jnp.mean(xf * xf, axis=-1, keepdims=True) + EPS)
    return (y * g.astype(jnp.float32)).astype(x.dtype)

def _layernorm(x, g, b):
    xf = x.astype(jnp.float32)
    mu = jnp.mean(xf, axis=-1, keepdims=True)
    var = jnp.mean(jnp.square(xf - mu), axis=-1, keepdims=True)
    y = (xf - mu) * lax.rsqrt(var + EPS)
    return (y * g.astype(jnp.float32) + b.astype(jnp.float32)).astype(x.dtype)

def _causal_dwconv(x, w, b):
    k = w.shape[0]
    c = x.shape[-1]
    y = lax.conv_general_dilated(
        x, w[:, None, :].astype(x.dtype), window_strides=(1,), padding=[(k - 1, 0)],
        dimension_numbers=('NWC', 'WIO', 'NWC'), feature_group_count=c)
    return y + b

def _conformer_conv(u, conv_w, conv_b, ln_g, ln_b):
    val, gate = jnp.split(u, 2, axis=-1)
    y = val * jax.nn.sigmoid(gate)
    y = _causal_dwconv(y, conv_w, conv_b)
    return jax.nn.silu(_layernorm(y, ln_g, ln_b))

def _lru_combine(left, right):
    a_l, b_l = left
    a_r, b_r = right
    return a_l * a_r, a_r * b_l + b_r

def _rglru_block(u, conv_w, conv_b, w_a, b_a, w_x, b_x, lam):
    bsz, seq, _ = u.shape
    gate_in, rec_in = jnp.split(u, 2, axis=-1)
    xr = _causal_dwconv(rec_in, conv_w, conv_b)
    xh = xr.reshape(bsz, seq, LRU_HEADS, LRU_HEAD_DIM)
    r = jax.nn.sigmoid(jnp.einsum('bshd,hde->bshe', xh, w_a) + b_a)
    i = jax.nn.sigmoid(jnp.einsum('bshd,hde->bshe', xh, w_x) + b_x)
    log_base = -jax.nn.softplus(-lam.astype(jnp.float32)).reshape(LRU_HEADS, LRU_HEAD_DIM)
    log_a = LRU_C * log_base * r.astype(jnp.float32)
    a = jnp.exp(log_a)
    gated_x = jnp.sqrt(-jnp.expm1(2.0 * log_a)) * (i * xh).astype(jnp.float32)
    _, h = lax.associative_scan(_lru_combine, (a, gated_x), axis=1)
    h = h.reshape(bsz, seq, LRU_WIDTH).astype(u.dtype)
    return h * jax.nn.gelu(gate_in)

def _ab_mixer(xn, w_in, b_in, conf_conv_w, conf_conv_b, conf_ln_g, conf_ln_b,
              lru_conv_w, lru_conv_b, lru_w_a, lru_b_a, lru_w_x, lru_b_x, lru_lambda, w_out):
    u = jnp.einsum('bsd,de->bse', xn, w_in) + b_in
    u_conf, u_lru = jnp.split(u, [2 * CONF_WIDTH], axis=-1)
    y_a = _conformer_conv(u_conf, conf_conv_w, conf_conv_b, conf_ln_g, conf_ln_b)
    y_b = _rglru_block(u_lru, lru_conv_w, lru_conv_b, lru_w_a, lru_b_a, lru_w_x, lru_b_x, lru_lambda)
    y = jnp.concatenate([y_a, y_b], axis=-1)
    return jnp.einsum('bse,ed->bsd', y, w_out)

def _mlstm_chunk_step(carry, inp):
    c_state, n_state, m_state = carry
    qc, kc, vc, ic, lfc = inp
    L = qc.shape[2]
    causal = jnp.tril(jnp.ones((L, L), dtype=bool))
    b = jnp.cumsum(lfc, axis=-1)
    log_d = b[..., :, None] - b[..., None, :] + ic[..., None, :]
    log_d = jnp.where(causal, log_d, -jnp.inf)
    log_inter = b + m_state[..., None]
    m_row = jnp.maximum(log_inter, jnp.max(log_d, axis=-1))
    d_w = jnp.exp(log_d - m_row[..., None])
    inter_w = jnp.exp(log_inter - m_row)
    scores = jnp.einsum('bhjd,bhsd->bhjs', qc, kc) * d_w
    num = jnp.einsum('bhjs,bhsv->bhjv', scores, vc) + inter_w[..., None] * jnp.einsum('bhjd,bhdv->bhjv', qc, c_state)
    den = jnp.sum(scores, axis=-1) + inter_w * jnp.einsum('bhjd,bhd->bhj', qc, n_state)
    h = num / jnp.maximum(jnp.abs(den), jnp.exp(-m_row))[..., None]
    b_last = b[..., -1]
    log_w = b_last[..., None] - b + ic
    m_new = jnp.maximum(b_last + m_state, jnp.max(log_w, axis=-1))
    w_s = jnp.exp(log_w - m_new[..., None])
    decay = jnp.exp(b_last + m_state - m_new)
    c_new = decay[..., None, None] * c_state + jnp.einsum('bhsd,bhsv->bhdv', w_s[..., None] * kc, vc)
    n_new = decay[..., None] * n_state + jnp.einsum('bhs,bhsd->bhd', w_s, kc)
    return (c_new, n_new, m_new), h

def _mlstm_mixer(xn, w_in, b_in, head_g, w_out):
    bsz, seq, _ = xn.shape
    nc = seq // ML_CHUNK
    u = jnp.einsum('bsd,de->bse', xn, w_in) + b_in
    q, k, v, o, ig, fg = jnp.split(
        u, [ML_QK_DIM, 2 * ML_QK_DIM, 2 * ML_QK_DIM + ML_V_DIM,
            2 * ML_QK_DIM + 2 * ML_V_DIM, 2 * ML_QK_DIM + 2 * ML_V_DIM + ML_HEADS], axis=-1)
    f32 = jnp.float32

    def to_chunks(t, d):
        return t.astype(f32).reshape(bsz, nc, ML_CHUNK, ML_HEADS, d).transpose(1, 0, 3, 2, 4)

    def gate_chunks(t):
        return t.astype(f32).reshape(bsz, nc, ML_CHUNK, ML_HEADS).transpose(1, 0, 3, 2)

    qc = to_chunks(q, ML_HEAD_QK)
    kc = to_chunks(k, ML_HEAD_QK) * (ML_HEAD_QK ** -0.5)
    vc = to_chunks(v, ML_HEAD_V)
    ic = gate_chunks(ig)
    lfc = gate_chunks(jax.nn.log_sigmoid(fg))
    init = (jnp.zeros((bsz, ML_HEADS, ML_HEAD_QK, ML_HEAD_V), f32),
            jnp.zeros((bsz, ML_HEADS, ML_HEAD_QK), f32),
            jnp.zeros((bsz, ML_HEADS), f32))
    _, h = lax.scan(_mlstm_chunk_step, init, (qc, kc, vc, ic, lfc))
    h = h.transpose(1, 0, 3, 2, 4).reshape(bsz, seq, ML_HEADS, ML_HEAD_V)
    h = h * lax.rsqrt(jnp.mean(h * h, axis=-1, keepdims=True) + EPS)
    h = (h.reshape(bsz, seq, ML_V_DIM) * head_g.astype(f32)).astype(xn.dtype)
    h = jax.nn.sigmoid(o) * h
    return jnp.einsum('bse,ed->bsd', h, w_out)

def _swiglu(xn, w_gate, w_up, w_down):
    g = jnp.einsum('bsd,df->bsf', xn, w_gate)
    up = jnp.einsum('bsd,df->bsf', xn, w_up)
    return jnp.einsum('bsf,fd->bsd', jax.nn.silu(g) * up, w_down)

def second_inputs(seed: int = 0) -> dict:
    key = jax.random.key(seed)
    ks = iter(jax.random.split(key, 40))

    def nrm(shape, scale):
        return jax.random.normal(next(ks), shape, jnp.float32) * scale

    def gain(shape):
        return 1.0 + nrm(shape, 0.05)

    lam_u = jax.random.uniform(next(ks), (N_EVEN, LRU_WIDTH), jnp.float32, minval=0.9, maxval=0.999)
    lam_base = lam_u ** (1.0 / LRU_C)
    lru_lambda = jnp.log(lam_base) - jnp.log1p(-lam_base)

    ml_b_in = nrm((N_ODD, ML_IN), 0.02)
    f_bias = jnp.linspace(3.0, 6.0, ML_HEADS, dtype=jnp.float32) + nrm((N_ODD, ML_HEADS), 0.1)
    ml_b_in = ml_b_in.at[:, ML_IN - ML_HEADS:].set(f_bias)

    return {
        'x': nrm((BATCH, SEQ, D_MODEL), 1.0),
        'pre_mix_g': gain((DEPTH, D_MODEL)),
        'post_mix_g': gain((DEPTH, D_MODEL)),
        'pre_ffn_g': gain((DEPTH, D_MODEL)),
        'post_ffn_g': gain((DEPTH, D_MODEL)),
        'ab_w_in': nrm((N_EVEN, D_MODEL, AB_IN), D_MODEL ** -0.5),
        'ab_b_in': nrm((N_EVEN, AB_IN), 0.02),
        'conf_conv_w': nrm((N_EVEN, CONF_KERNEL, CONF_WIDTH), CONF_KERNEL ** -0.5),
        'conf_conv_b': nrm((N_EVEN, CONF_WIDTH), 0.02),
        'conf_ln_g': gain((N_EVEN, CONF_WIDTH)),
        'conf_ln_b': nrm((N_EVEN, CONF_WIDTH), 0.02),
        'lru_conv_w': nrm((N_EVEN, LRU_CONV, LRU_WIDTH), LRU_CONV ** -0.5),
        'lru_conv_b': nrm((N_EVEN, LRU_WIDTH), 0.02),
        'lru_w_a': nrm((N_EVEN, LRU_HEADS, LRU_HEAD_DIM, LRU_HEAD_DIM), LRU_HEAD_DIM ** -0.5),
        'lru_b_a': nrm((N_EVEN, LRU_HEADS, LRU_HEAD_DIM), 0.02),
        'lru_w_x': nrm((N_EVEN, LRU_HEADS, LRU_HEAD_DIM, LRU_HEAD_DIM), LRU_HEAD_DIM ** -0.5),
        'lru_b_x': nrm((N_EVEN, LRU_HEADS, LRU_HEAD_DIM), 0.02),
        'lru_lambda': lru_lambda,
        'ab_w_out': nrm((N_EVEN, AB_OUT, D_MODEL), AB_OUT ** -0.5),
        'ml_w_in': nrm((N_ODD, D_MODEL, ML_IN), D_MODEL ** -0.5),
        'ml_b_in': ml_b_in,
        'ml_head_g': gain((N_ODD, ML_V_DIM)),
        'ml_w_out': nrm((N_ODD, ML_V_DIM, D_MODEL), ML_V_DIM ** -0.5),
        'ffn_w_gate': nrm((DEPTH, D_MODEL, D_FF_2), D_MODEL ** -0.5),
        'ffn_w_up': nrm((DEPTH, D_MODEL, D_FF_2), D_MODEL ** -0.5),
        'ffn_w_down': nrm((DEPTH, D_FF_2, D_MODEL), D_FF_2 ** -0.5),
    }

def second_block(x, pre_mix_g, post_mix_g, pre_ffn_g, post_ffn_g,
              ab_w_in, ab_b_in, conf_conv_w, conf_conv_b, conf_ln_g, conf_ln_b,
              lru_conv_w, lru_conv_b, lru_w_a, lru_b_a, lru_w_x, lru_b_x, lru_lambda, ab_w_out,
              ml_w_in, ml_b_in, ml_head_g, ml_w_out,
              ffn_w_gate, ffn_w_up, ffn_w_down):
    for layer in range(DEPTH):
        j = layer // 2
        h = _rmsnorm(x, pre_mix_g[layer])
        if layer % 2 == 0:
            h = _ab_mixer(h, ab_w_in[j], ab_b_in[j], conf_conv_w[j], conf_conv_b[j],
                          conf_ln_g[j], conf_ln_b[j], lru_conv_w[j], lru_conv_b[j],
                          lru_w_a[j], lru_b_a[j], lru_w_x[j], lru_b_x[j], lru_lambda[j], ab_w_out[j])
        else:
            h = _mlstm_mixer(h, ml_w_in[j], ml_b_in[j], ml_head_g[j], ml_w_out[j])
        x = x + _rmsnorm(h, post_mix_g[layer])
        h = _swiglu(_rmsnorm(x, pre_ffn_g[layer]), ffn_w_gate[layer], ffn_w_up[layer], ffn_w_down[layer])
        x = x + _rmsnorm(h, post_ffn_g[layer])
    return x


def setup_inputs(seed=0):
    out = dict(first_inputs(seed))
    for name, value in second_inputs(seed + 1).items():
        if name != "x":
            out[name + "_2"] = value
    return out


def reference(
    x, c, ctx, c_ctx, w_mod, b_mod, g_norm1, g_norm2, w_in, w_conv, g_q, g_k, w_conv_out,
    w_four_out, w_attn_out, w_o, w_ff1, w_ff2, pre_mix_g_2, post_mix_g_2, pre_ffn_g_2,
    post_ffn_g_2, ab_w_in_2, ab_b_in_2, conf_conv_w_2, conf_conv_b_2, conf_ln_g_2, conf_ln_b_2,
    lru_conv_w_2, lru_conv_b_2, lru_w_a_2, lru_b_a_2, lru_w_x_2, lru_b_x_2, lru_lambda_2,
    ab_w_out_2, ml_w_in_2, ml_b_in_2, ml_head_g_2, ml_w_out_2, ffn_w_gate_2, ffn_w_up_2,
    ffn_w_down_2,
):
    x = first_block(
        x, c, ctx, c_ctx, w_mod, b_mod, g_norm1, g_norm2, w_in, w_conv, g_q, g_k, w_conv_out,
        w_four_out, w_attn_out, w_o, w_ff1, w_ff2,
    )
    return second_block(
        x, pre_mix_g_2, post_mix_g_2, pre_ffn_g_2, post_ffn_g_2, ab_w_in_2, ab_b_in_2,
        conf_conv_w_2, conf_conv_b_2, conf_ln_g_2, conf_ln_b_2, lru_conv_w_2, lru_conv_b_2,
        lru_w_a_2, lru_b_a_2, lru_w_x_2, lru_b_x_2, lru_lambda_2, ab_w_out_2, ml_w_in_2,
        ml_b_in_2, ml_head_g_2, ml_w_out_2, ffn_w_gate_2, ffn_w_up_2, ffn_w_down_2,
    )


_drawn_inputs = setup_inputs


def setup_inputs(seed=0):
    import zlib

    import numpy as np

    out = dict(_drawn_inputs(seed))
    spreads = {}
    factors = {'ctx': 2.874,
     'g_q': 8.0,
     'g_k': 8.0,
     'conf_ln_b_2': 3.896,
     'lru_b_a_2': 22.341,
     'lru_b_x_2': 8.0}
    for name, (base, spread) in spreads.items():
        noise = np.random.default_rng([zlib.crc32(name.encode()), seed]).standard_normal(out[name].shape)
        drawn = base * np.exp(spread * noise) if base else spread * noise
        out[name] = __import__('jax').numpy.asarray(drawn.astype(out[name].dtype))
    for name, factor in factors.items():
        out[name] = (out[name] * factor).astype(out[name].dtype)
    return out
```

```python
from contextlib import ExitStack

import numpy as np
import concourse.bass as bass
from concourse import mybir

F32 = mybir.dt.float32
F32R = mybir.dt.float32r
ALU = mybir.AluOpType
ACT = mybir.ActivationFunctionType
AX_X = mybir.AxisListType.X

P = 128
D = 1024
KB = D // P
SEQ = 512
CTX = 256
DEPTH = 2
HEAD = 64
N_HEADS = 8
N_MOD = 6
FF = 4096
FF2 = 2816
EPS = 1e-6
R = 4
TILE = KB * P
LEAD = 3
FFN_GROUPS = ((0, 8), (8, 8), (16, 6))
FFN_TILES = sum(2 * n + KB for _, n in FFN_GROUPS)
KT_ALL = (SEQ + CTX) // P

Z_B, Z_C, Z_X, Z_F, Z_Q, Z_K = 0, 2, 4, 6, 8, 12


def vector_columns():
    cols, at = {}, 0
    for name, n in (
        ("c", 8), ("c_ctx", 8), ("b_mod0", 48), ("b_mod1", 48),
        ("g1_0", 8), ("g1_1", 8), ("g2_0", 8), ("g2_1", 8),
        ("w_conv0", 6), ("w_conv1", 6), ("gq0", 1), ("gq1", 1), ("gk0", 1), ("gk1", 1),
        ("pre_mix0", 8), ("pre_mix1", 8), ("post_mix0", 8), ("post_mix1", 8),
        ("pre_ffn0", 8), ("pre_ffn1", 8), ("post_ffn0", 8), ("post_ffn1", 8),
        ("ab_b", 16), ("conf_w", 31 * 4), ("conf_b", 4), ("ln_g", 4), ("ln_b", 4),
        ("lru_w", 16), ("lru_b", 4), ("lru_ba", 4), ("lru_bx", 4), ("lru_lam", 4),
        ("ml_b", 16), ("ml_bg", 1), ("head_g", 8),
    ):
        cols[name] = (at, n)
        at += n
    return cols, at


VCOL, N_VCOL = vector_columns()


def plan():
    steps, at = [], 0

    def add(kind, n, layer=0, stream="main"):
        nonlocal at
        steps.append((kind, layer, stream, at))
        at += n

    def block(layer, stream):
        add("norm1", 0, layer, stream)
        add("z", 14, layer, stream)
        add("fourier", 5 if stream == "main" else 2, layer, stream)
        add("conv", 0, layer, stream)
        add("qk", 0, layer, stream)
        add("attn", 0, layer, stream)
        add("merge", 32, layer, stream)
        add("w_o", 8, layer, stream)
        add("norm2", 0, layer, stream)
        add("ff", 64, layer, stream)

    add("mod", 48, 0)
    block(0, "ctx")
    block(0, "main")
    add("mod", 48, 1)
    add("norm1", 0, 1, "ctx")
    add("z_kv", 2, 1, "ctx")
    add("qk", 0, 1, "ctx")
    block(1, "main")
    add("pre_mix", 0, 0)
    add("ab_conf", 8)
    add("ab_lru", 8)
    add("lru_gate", 1)
    add("mix_out", 8, 0)
    add("post_mix", 0, 0)
    add("pre_ffn", 0, 0)
    add("ffn", FFN_TILES, 0)
    add("post_ffn", 0, 0)
    add("pre_mix", 0, 1)
    add("ml_qk", 16)
    add("ml_gates", 1)
    add("ml_v", 8)
    add("mlstm", 0)
    add("mix_out", 8, 1)
    add("post_mix", 0, 1)
    add("pre_ffn", 0, 1)
    add("ffn", FFN_TILES, 1)
    add("post_ffn", 0, 1)
    return steps, at


def stream_tiles(w):
    out = []

    def cols(m, first, n):
        part = m[:, first:first + n * P].reshape(KB, P, n, P)
        out.extend(part.transpose(2, 1, 0, 3).reshape(n, P, TILE))

    def fourier(length):
        k = np.arange(HEAD)
        ang = 2 * np.pi * np.outer(k, k) / HEAD
        t = np.zeros((P, TILE), np.float32)
        for i, fn in enumerate((np.cos, np.sin)):
            for g in range(2):
                t[g * HEAD:(g + 1) * HEAD, i * P + g * HEAD:i * P + (g + 1) * HEAD] = fn(ang) / 8.0
        out.append(t)
        k = np.arange(length)
        ang = 2 * np.pi * (np.outer(k, k) % length) / length
        big = np.stack([np.cos(ang), -np.sin(ang)]) / np.sqrt(length)
        big = big.astype(np.float32).reshape(2, length // P, P, length).transpose(0, 1, 2, 3)
        rows = big.reshape(2 * (length // P), P, length)
        per = TILE // length
        for i in range(0, rows.shape[0], per):
            out.append(rows[i:i + per].transpose(1, 0, 2).reshape(P, TILE))

    def ffn(gate, up, down):
        for first, n in FFN_GROUPS:
            for m in range(first, first + n):
                cols(gate, m * P, 1)
                cols(up, m * P, 1)
            for m in range(KB):
                t = np.zeros((P, TILE), np.float32)
                part = down[first * P:(first + n) * P, m * P:(m + 1) * P]
                t[:, :n * P] = part.reshape(n, P, P).transpose(1, 0, 2).reshape(P, n * P)
                out.append(t)

    for kind, layer, stream, at in plan()[0]:
        assert at == len(out), (kind, at, len(out))
        if kind == "mod":
            cols(w["w_mod"][layer], 0, 48)
        elif kind == "z":
            cols(w["w_in"][layer], 0, 14)
        elif kind == "z_kv":
            cols(w["w_in"][layer], 12 * P, 2)
        elif kind == "fourier":
            fourier(SEQ if stream == "main" else CTX)
        elif kind == "merge":
            branch = np.concatenate([w["w_conv_out"][layer], w["w_four_out"][layer], w["w_attn_out"][layer]])
            for m in range(KB):
                for g in range(3):
                    cols(w["w_in"][layer], 14 * P + g * D + m * P, 1)
                cols(branch, m * P, 1)
        elif kind == "w_o":
            cols(w["w_o"][layer], 0, 8)
        elif kind == "ff":
            for g in range(4):
                cols(w["w_ff1"][layer], g * D, 8)
                cols(w["w_ff2"][layer][g * D:(g + 1) * D], 0, 8)
        elif kind == "ab_conf":
            for b in range(4):
                cols(w["ab_w_in_2"][0], b * P, 1)
                cols(w["ab_w_in_2"][0], (4 + b) * P, 1)
        elif kind == "ab_lru":
            cols(w["ab_w_in_2"][0], 12 * P, 4)
            cols(w["ab_w_in_2"][0], 8 * P, 4)
        elif kind == "lru_gate":
            t = np.zeros((P, 2, 4, P), np.float32)
            for i, name in enumerate(("lru_w_a_2", "lru_w_x_2")):
                for h in range(8):
                    o = (h % 2) * HEAD
                    t[o:o + HEAD, i, h // 2, o:o + HEAD] = w[name][0, h]
            out.append(t.reshape(P, TILE))
        elif kind == "mix_out":
            cols(w["ml_w_out_2"][0] if layer else w["ab_w_out_2"][0], 0, 8)
        elif kind == "ffn":
            ffn(w["ffn_w_gate_2"][layer], w["ffn_w_up_2"][layer], w["ffn_w_down_2"][layer])
        elif kind == "ml_qk":
            cols(w["ml_w_in_2"][0], 0, 8)
            cols(w["ml_w_in_2"][0], 2 * D, 8)
        elif kind == "ml_gates":
            t = np.zeros((D, P), np.float32)
            t[:, 0:8] = w["ml_w_in_2"][0][:, 3 * D:3 * D + 8]
            t[:, 32:40] = w["ml_w_in_2"][0][:, 3 * D + 8:3 * D + 16]
            cols(t, 0, 1)
        elif kind == "ml_v":
            v = w["ml_w_in_2"][0][:, D:2 * D]
            for half in range(2):
                for kk in range(0, KB, 2):
                    part = v[kk * P:(kk + 2) * P, half * 512:(half + 1) * 512]
                    out.append(part.reshape(2, P, 512).transpose(1, 0, 2).reshape(P, TILE))
    return np.ascontiguousarray(np.stack(out), dtype=np.float32)


def vector_table(w):
    t = np.zeros((P, N_VCOL), np.float32)

    def put(name, v):
        at, n = VCOL[name]
        t[:, at:at + n] = np.asarray(v).reshape(n, P).T

    put("c", w["c"])
    put("c_ctx", w["c_ctx"])
    for i in range(2):
        put(f"b_mod{i}", w["b_mod"][i])
        put(f"g1_{i}", w["g_norm1"][i])
        put(f"g2_{i}", w["g_norm2"][i])
        put(f"w_conv{i}", w["w_conv"][i])
        put(f"gq{i}", np.tile(w["g_q"][i], 2))
        put(f"gk{i}", np.tile(w["g_k"][i], 2))
        for n in ("pre_mix", "post_mix", "pre_ffn", "post_ffn"):
            put(f"{n}{i}", w[f"{n}_g_2"][i])
    put("ab_b", w["ab_b_in_2"])
    put("conf_w", w["conf_conv_w_2"])
    put("conf_b", w["conf_conv_b_2"])
    put("ln_g", w["conf_ln_g_2"])
    put("ln_b", w["conf_ln_b_2"])
    put("lru_w", w["lru_conv_w_2"])
    put("lru_b", w["lru_conv_b_2"])
    put("lru_ba", w["lru_b_a_2"])
    put("lru_bx", w["lru_b_x_2"])
    put("lru_lam", w["lru_lambda_2"])
    b = w["ml_b_in_2"][0]
    put("ml_b", np.concatenate([b[:D], b[2 * D:3 * D]]))
    gb = np.zeros(P, np.float32)
    gb[0:8], gb[32:40] = b[3 * D:3 * D + 8], b[3 * D + 8:]
    put("ml_bg", gb)
    put("head_g", w["ml_head_g_2"])
    return t


def shape_tables():
    m = np.zeros((P, 5, P), np.float32)
    m[:, 0] = 1.0
    m[:, 1] = np.eye(P)
    for g in range(2):
        s = slice(g * HEAD, (g + 1) * HEAD)
        m[s, 2, s] = 1.0
    for p in range(P):
        lower = p % HEAD < HEAD // 2
        m[p + 32 if lower else p - 32, 3, p] = -1.0 if lower else 1.0
    m[:, 4] = np.where(np.arange(P)[:, None] <= np.arange(P)[None, :], 0.0, -1e30)
    n_freq = HEAD // 4
    inv = (np.float32(10000.0) ** (-np.arange(n_freq, dtype=np.float32) / n_freq)).astype(np.float32)
    t = np.arange(SEQ)
    ang = np.concatenate([(t // 64).astype(np.float32)[:, None] * inv, (t % 64).astype(np.float32)[:, None] * inv], -1)
    ang = np.tile(ang.T, (4, 1)).astype(np.float32)
    rope = np.stack([np.cos(ang), np.sin(ang)], axis=1).astype(np.float32)
    return m.reshape(P, 5 * P), rope.reshape(P, 2 * SEQ)


class Counts:

    def __init__(self):
        self.n, self.i, self.per, self.at = {}, None, {}, {}

    def now(self, sem, more=0):
        n = self.n.get(id(sem), 0) + more
        if self.i is not None and id(sem) in self.per:
            return self.i * self.per[id(sem)] + n
        assert self.i is None or n - more == self.at.get(id(sem), 0), "a count that changes in a loop"
        return n

    def next(self, sem, n=1):
        self.n[id(sem)] = self.n.get(id(sem), 0) + n
        return self.now(sem)

    def enter(self, i, per):
        self.at = dict(self.n)
        self.i, self.per = i, {id(k): n for k, n in per.items()}

    def leave(self, turns):
        for k, n in self.n.items():
            one = n - self.at.get(k, 0)
            assert one == self.per.get(k, 0), ("increments of one turn", one, self.per.get(k, 0))
            self.n[k] = self.at.get(k, 0) + turns * one
        self.i, self.per = None, {}


def build(nc, ws, vecs, mats, ropes, x_in, ctx_in, bv_in, out, upto=None):
    steps, n_tiles = plan()
    if upto is not None:
        n_tiles = steps[upto][3]
        steps = steps[:upto]

    with ExitStack() as stack:
        def sb(name, shape, dt=F32):
            return stack.enter_context(nc.sbuf_tensor(name, shape, dt))

        def sem(name):
            return stack.enter_context(nc.semaphore(name))

        raw = sb("raw", [P, R, TILE])
        w_hi = sb("w_hi", [P, R, TILE], F32R)
        w_lo = sb("w_lo", [P, R, TILE], F32R)
        x = sb("x", [P, KB, SEQ])
        xc = sb("xc", [P, KB, CTX])
        h_hi = sb("h_hi", [P, KB, SEQ], F32R)
        h_lo = sb("h_lo", [P, KB, SEQ], F32R)
        y_hi = sb("y_hi", [P, KB, SEQ], F32R)
        y_lo = sb("y_lo", [P, KB, SEQ], F32R)
        z = sb("z", [P, 16, SEQ])
        kv = sb("kv", [P, 12, SEQ], F32R)
        scr = sb("scr", [P, 4, SEQ])
        vec = sb("vec", [P, N_VCOL])
        mat = sb("mat", [P, 5 * P])
        mod = sb("mod", [P, DEPTH, N_MOD * KB, 2])
        gain = sb("gain", [P, DEPTH, 2, 2, KB])
        c_act = sb("c_act", [P, 16])
        c_hi = sb("c_hi", [P, KB, 2], F32R)
        c_lo = sb("c_lo", [P, KB, 2], F32R)
        mx = sb("mx", [P, 2, 4])
        small = sb("small", [P, 64])
        eps = sb("eps", [P, 1])
        decay = sb("decay", [P, 4])
        ones_r = sb("ones_r", [P, P], F32R)
        bank = [stack.enter_context(nc.psum_tensor(f"bank{i}", [P, SEQ], F32)) for i in range(4, 8)]
        ring = stack.enter_context(nc.psum_tensor("ring", [P, R, SEQ], F32))

        ones, ident, head_ones, rot = (mat[:, i * P:(i + 1) * P] for i in range(4))
        causal = mat[:, 4 * P:5 * P]
        kvf = kv[:, :, :].rearrange("p a b -> p (a b)")
        nk = SEQ + CTX
        k_pair = kvf[:, 0:2 * nk].rearrange("p (g k) -> p g k", g=2)
        k_one = kvf[:, 2 * nk:4 * nk].rearrange("p (g k) -> p g k", g=2)
        v_hi = kvf[:, 4 * nk:6 * nk].rearrange("p (k g d) -> p k g d", k=KT_ALL, g=2)
        v_lo = kvf[:, 6 * nk:8 * nk].rearrange("p (k g d) -> p k g d", k=KT_ALL, g=2)


        xv = xc[:, :, :].rearrange("p a b -> p (a b)").rearrange("p (a b) -> p a b", b=SEQ)
        gate_rows = slice(32, 40)
        row = (xv[gate_rows, 2, :], xv[gate_rows, 3, :])

        def head_out(h):
            return z[:, h // 2 + 4 * (h % 2), :]

        def v(name, i=0):
            return vec[:, VCOL[name][0] + i:VCOL[name][0] + i + 1]

        loaded = [sem(f"loaded{i}") for i in range(R)]
        s_in = sem("inputs_loaded")
        s_ctx = sem("ctx_loaded")
        s_rope = sem("rope_loaded")
        s_bv = sem("v_bias_loaded")
        w_hi_ready = sem("w_hi_ready")
        w_ready = sem("w_ready")
        tile_done = sem("tile_done")
        post = sem("post")
        evac = sem("evac")
        sq_ready = sem("sq_ready")
        ss_ready = sem("ss_ready")
        root_ready = sem("root_ready")
        t_ready = sem("t_ready")
        hi_ready = sem("hi_ready")
        lo_ready = sem("lo_ready")
        consts = sem("constants_ready")
        dve_own = sem("vector_own")
        act_own = sem("scalar_own")
        s_score = sem("scores_ready")
        s_max = sem("max_ready")
        s_mrow = sem("max_row_ready")
        s_shift = sem("shift_ready")
        s_q = sem("q_ready")
        s_st = sem("scores_t_ready")
        s_exp = sem("exp_ready")
        s_p = sem("p_ready")
        s_pv = sem("pv_done")
        s_o = sem("o_ready")
        s_on = sem("o_read")
        s_vec = sem("vectors_loaded")
        s_silu = sem("conditions_activated")
        s_free = sem("scratch_free")
        s_qn = sem("q_normed")
        s_rot = sem("rotated")
        s_x = sem("residual_ready")
        s_conv = sem("conv_ready")
        s_gate = sem("lru_gates_ready")
        s_gread = sem("lru_gates_read")
        s_act = sem("activated")
        s_lam = sem("decay_ready")
        s_row = sem("gate_rows_ready")
        s_col = sem("gate_columns_ready")
        s_bc = sem("row_spread")
        s_diag = sem("diagonal_ready")
        s_thr = sem("threshold_ready")
        s_final = sem("result_ready")
        s_out = sem("stored")

        block = stack.enter_context(nc.Block())

        def length(stream):
            return SEQ if stream == "main" else CTX

        def x_of(stream):
            return x if stream == "main" else xc

        turn = [None]

        def grouped(eng, n, first, body, C, per=None, size=R):
            turns = n // size
            turn[0] = None
            if first + turns * size + LEAD > n_tiles:
                turns -= 1
            if turns > 1:
                with eng.Fori(0, turns, 1) as i:
                    C.enter(i, per or {})
                    turn[0] = i
                    for u in range(size):
                        body(first + u, u, i * size)
                    C.leave(turns)
                turn[0] = None
            else:
                turns = 0
            for u in range(turns * size, n):
                body(first + u, u, 0)

        def at(ap, block, off):
            if isinstance(off, int):
                return ap[:, block, :]
            return ap[:, bass.ds(off + block, 1), :].rearrange("p o n -> p (o n)")

        @block.sync
        def _(sp):
            sp.dma_start(vec[:, :], vecs).then_inc(s_vec, 16)
            for t in range(R):
                sp.dma_start(raw[:, t, :], ws[t]).then_inc(loaded[t], 16)
            sp.dma_start(mat[:, :], mats).then_inc(s_in, 16)
            sp.dma_start(xc[:, :, :], ctx_in.rearrange("(k p) t -> p k t", p=P)).then_inc(s_ctx, 16)
            sp.dma_start(x[:, :, :], x_in.rearrange("(k p) t -> p k t", p=P)).then_inc(s_in, 16)
            groups = n_tiles // R - 1
            with sp.Fori(0, groups, 1) as i:
                for u in range(R):
                    sp.wait_ge(w_ready, i * R + (u + 1))
                    sp.dma_start(raw[:, u, :], ws[bass.ds(i * R + (R + u), 1)].rearrange("o p n -> (o p) n"))\
                        .then_inc(loaded[u], 16)
            for t in range((groups + 1) * R, n_tiles):
                sp.wait_ge(w_ready, t - R + 1)
                sp.dma_start(raw[:, t % R, :], ws[t]).then_inc(loaded[t % R], 16)
            sp.wait_ge(s_final, 1)
            sp.dma_start(out.rearrange("(k p) t -> p k t", p=P), x[:, :, :]).then_inc(s_out, 16)
            sp.wait_ge(s_out, 16)

        @block.gpsimd
        def _(pool):
            def lower(u, n):
                pool.wait_ge(w_hi_ready, n)
                nc.gpsimd.tensor_tensor(w_lo[:, u, :], raw[:, u, :], w_hi[:, u, :].bitcast(F32),
                                        ALU.subtract).then_inc(w_ready, 1)

            with pool.Fori(0, n_tiles // R, 1) as i:
                for u in range(R):
                    lower(u, i * R + (u + 1))
            for t in range(n_tiles // R * R, n_tiles):
                lower(t % R, t + 1)

        @block.scalar
        def _(act):
            C = Counts()

            def split(c, off=0):
                t = c + LEAD
                if isinstance(off, int) and t >= n_tiles:
                    return
                act.wait_ge(loaded[t % R], off * (16 // R) + 16 * (t // R + 1))
                act.wait_ge(tile_done, off + (t + 1))
                nc.scalar.activation(w_hi[:, t % R, :], raw[:, t % R, :], ACT.Copy).then_inc(w_hi_ready, 1)

            def done(c, off=0):
                act.wait_ge(tile_done, off + (c + 1 + R))

            def begun(at_tile):
                act.wait_ge(post, at_tile + R)

            def squares(src, n, T):
                for k in range(n):
                    if k >= 2:
                        act.wait_ge(ss_ready, C.next(ss_ready))
                    nc.scalar.activation(scr[:, k % 2, :T], src(k), ACT.Square).then_inc(sq_ready, 1)
                act.wait_ge(ss_ready, C.next(ss_ready, min(n, 2)))

            def root(ps, T, count):
                nc.scalar.activation(scr[:, 2, :T], ps[:, :T], ACT.Sqrt, bias=eps[:, 0:1], scale=1.0 / count)\
                    .then_inc(root_ready, 1)

            def upper(n, src, dst, bias=None):
                for k in range(n):
                    act.wait_ge(t_ready, C.next(t_ready))
                    if bias is None:
                        nc.scalar.activation(dst(k), src(k), ACT.Copy).then_inc(hi_ready, 1)
                    else:
                        nc.scalar.activation(dst(k), src(k), ACT.Identity, bias=bias(k)).then_inc(hi_ready, 1)

            def gain_norm(first, residual=True):
                begun(first)
                if residual:
                    act.wait_ge(s_x, C.next(s_x))
                squares(lambda k: x[:, k, :], KB, SEQ)
                root(bank[0], SEQ, D)
                upper(KB, lambda k: scr[:, k % 2, :], lambda k: h_hi[:, k, :])

            def post_norm(first):
                begun(first)
                squares(lambda k: z[:, k, :], KB, SEQ)
                root(bank[0], SEQ, D)

            def biased(c, off, o, func, column):
                b = column if isinstance(off, int) else column
                nc.scalar.activation(o, ring[:, c % R, :], func, bias=b).then_inc(evac, 1)

            def col(name, i, off):
                at0 = VCOL[name][0] + i
                return vec[:, at0:at0 + 1] if isinstance(off, int) else vec[:, bass.ds(off + at0, 1)]

            def ab_conf(first):
                for n in range(8):
                    c, b = first + n, n // 2
                    split(c)
                    done(c)
                    if n % 2 == 0:
                        biased(c, 0, z[:, b, :], ACT.Identity, col("ab_b", b, 0))
                    else:
                        act.wait_ge(post, c - 3 + R)
                        biased(c, 0, scr[:, b % 2, :], ACT.Sigmoid, col("ab_b", 4 + b, 0))

            def ab_lru(first):
                for n in range(8):
                    split(first + n)
                    done(first + n)
                    if n < 4:
                        biased(first + n, 0, z[:, 8 + n, :], ACT.Identity, col("ab_b", 12 + n, 0))
                    else:
                        biased(first + n, 0, z[:, 8 + n, :], ACT.Gelu_apprx_tanh, col("ab_b", 8 + n - 4, 0))

            def lru(first):
                split(first)
                act.wait_ge(ss_ready, C.next(ss_ready, 4))
                nc.scalar.activation(scr[:, 2, :], bank[0][:, :], ACT.Copy, scale=1.0 / (4 * P)).then_inc(root_ready, 1)
                act.wait_ge(t_ready, C.next(t_ready, 4))
                squares(lambda k: z[:, 4 + k, :], 4, SEQ)
                root(bank[0], SEQ, 4 * P)
                for b in range(4):
                    act.wait_ge(t_ready, C.next(t_ready))
                    nc.scalar.activation(z[:, 4 + b, :], z[:, 4 + b, :], ACT.Silu, bias=v("ln_b", b)).then_inc(s_act, 1)
                for b in range(4):
                    act.wait_ge(s_gate, C.next(s_gate))
                    nc.scalar.activation(z[:, 8 + b, :], bank[2][:, :], ACT.Sigmoid, bias=v("lru_ba", b))\
                        .then_inc(s_gread, 1)
                    nc.scalar.activation(z[:, b, :], bank[3][:, :], ACT.Sigmoid, bias=v("lru_bx", b))\
                        .then_inc(s_gread, 1)
                act.wait_ge(s_free, C.next(s_free))
                act.wait_ge(s_gread, C.next(s_gread, 8))
                for b in range(4):
                    nc.scalar.activation(scr[:, b, :], z[:, 8 + b, :], ACT.Tanh, scale=decay[:, b:b + 1])\
                        .then_inc(s_act, 1)
                for b in range(4):
                    act.wait_ge(s_act, 5 + b)
                    nc.scalar.activation(z[:, 8 + b, :], z[:, 8 + b, :], ACT.Exp, scale=decay[:, b:b + 1])\
                        .then_inc(s_act, 1)
                for b in range(4):
                    act.wait_ge(t_ready, C.next(t_ready))
                    nc.scalar.activation(scr[:, b, :], scr[:, b, :], ACT.Sqrt).then_inc(s_act, 1)

            def mix_out(first):
                def body(c, u, off):
                    split(c, off)
                    done(c, off)
                    nc.scalar.activation(at(z, u, off), ring[:, c % R, :], ACT.Copy).then_inc(evac, 1)
                grouped(act, KB, first, body, C)

            def ffn(first):
                def body(c, u, off):
                    pos, n = (u % 24, 8) if u < 48 else (u - 48, 6)
                    split(c, off)
                    if pos >= 2 * n or pos % 2:
                        return
                    done(c, off)
                    act.wait_ge(post, off + (c - 2 + R))
                    nc.scalar.activation(scr[:, pos // 2 % 2, :], ring[:, c % R, :], ACT.Silu).then_inc(evac, 1)
                grouped(act, FFN_TILES, first, body, C, size=24)

            def ml_qk(first):
                act.dma_start(xv[0:1, 0:2, :], bv_in.rearrange("o (a n) -> o a n", a=2)).then_inc(s_bv, 16)

                def qk_body(c, u, off):
                    split(c, off)
                    done(c, off)
                    biased(c, off, at(z, u, off), ACT.Identity, col("ml_b", u, off))

                def o_body(c, u, off):
                    split(c, off)
                    done(c, off)
                    biased(c, off, at(z, 8 + u, off), ACT.Sigmoid, col("ml_b", 8 + u, off))
                grouped(act, 8, first, qk_body, C)
                grouped(act, 8, first + 8, o_body, C)

            def ml_gates(first):
                split(first)
                done(first)
                biased(first, 0, scr[:, 0, :], ACT.Identity, v("ml_bg"))
                own_wait()
                f_rows = slice(32, 40)
                step(nc.scalar.activation(scr[f_rows, 1, :], scr[f_rows, 0, :], ACT.Abs))
                step(nc.scalar.activation(scr[f_rows, 1, :], scr[f_rows, 1, :], ACT.Exp, scale=-1.0))
                nc.scalar.activation(scr[f_rows, 1, :], scr[f_rows, 1, :], ACT.Ln, bias=mat[f_rows, 0:1])\
                    .then_inc(s_act, 1)

            def own_wait():
                act.wait_ge(s_row, C.next(s_row))

            def step(ins):
                ins.then_inc(act_own, 1)
                act.wait_ge(act_own, C.next(act_own))

            def ml_v(first):
                for half in range(2):
                    for n in range(4):
                        split(first + 4 * half + n)
                    done(first + 4 * half + 3)
                    for tt in range(4):
                        nc.scalar.activation(y_hi[:, 2 * tt + half, :], bank[tt][:, :], ACT.Copy).then_inc(hi_ready, 1)

            def mlstm():
                for h in range(N_HEADS):
                    act.wait_ge(s_bc, C.next(s_bc))
                    spread = bank[2 * (h % 2)]
                    nc.scalar.activation(xv[:, h % 2, :], spread[:, :], ACT.Copy).then_inc(s_act, 1)
                    for sb_ in range(4):
                        act.wait_ge(s_diag, C.next(s_diag))
                        j = sb_ * P
                        a_col = small[:, sb_ * 8 + h:sb_ * 8 + h + 1]
                        e = scr[:, sb_ % 2, :]
                        m = nc.scalar.activation(e[:, j:j + P], e[:, j:j + P], ACT.Exp, bias=a_col)
                        if sb_ < 3:
                            m.then_inc(act_own, 1)
                            C.next(act_own)
                            m = nc.scalar.activation(e[:, j + P:], spread[:, j + P:], ACT.Exp, bias=a_col)
                        m.then_inc(s_exp, 1)
                    if h:
                        act.wait_ge(s_on, C.next(s_on))
                    nc.scalar.activation(scr[:, 3, :], bank[2 * (h % 2) + 1][:, :], ACT.Exp).then_inc(s_thr, 1)
                act.wait_ge(s_on, C.next(s_on))
                ss0 = C.now(ss_ready)

                def square(n):
                    if n >= 2:
                        act.wait_ge(ss_ready, ss0 + n - 1)
                    nc.scalar.activation(scr[:, n % 2, :], head_out(n), ACT.Square).then_inc(sq_ready, 1)

                square(0)
                for n in range(N_HEADS):
                    if n + 1 < N_HEADS:
                        square(n + 1)
                    act.wait_ge(ss_ready, ss0 + n + 1)
                    if n:
                        act.wait_ge(s_qn, C.next(s_qn))
                    root(bank[n % 2], SEQ, P)
                C.next(ss_ready, N_HEADS)
                C.next(s_qn)

            def norm(layer, stream, first, part):
                T, src, s = length(stream), x_of(stream), int(stream == "ctx")
                begun(first)
                if part == 0 and stream == "main":
                    act.dma_start(z[:, 14:16, :], ropes.rearrange("p (a t) -> p a t", a=2)).then_inc(s_rope, 16)
                if part == 0 and stream == "ctx" and layer == 0:
                    act.wait_ge(s_ctx, 16)
                if part == 0 and stream == "main" and layer == 0:
                    act.wait_ge(s_in, 32)
                squares(lambda k: src[:, k, :T], KB, T)
                root(bank[0], T, D)
                upper(KB, lambda k: scr[:, k % 2, :T], lambda k: h_hi[:, k, :T],
                      lambda k: mod[:, layer, part * KB + k, s:s + 1])

            def mod_tiles(layer, first):
                def body(c, u, off):
                    split(c, off)
                    done(c, off)
                    col = VCOL[f"b_mod{layer}"][0]
                    b = vec[:, col + u:col + u + 1] if isinstance(off, int) else vec[:, bass.ds(off + (col + u), 1)]
                    o = at(mod[:, layer, :, :], u, off)
                    nc.scalar.activation(o, ring[:, c % R, 0:2], ACT.Identity, bias=b).then_inc(evac, 1)
                grouped(act, 48, first, body, C)

            def z_tiles(layer, stream, first, n):
                T = length(stream)

                def body(c, u, off):
                    split(c, off)
                    done(c, off)
                    nc.scalar.activation(at(z[:, :, :T], (Z_K if n == 0 else 0) + u, off), ring[:, c % R, :T],
                                         ACT.Copy).then_inc(evac, 1)
                grouped(act, max(n, 1), first, body, C)
                c = first + max(n, 1)
                split(c)
                done(c)
                kt = 0 if stream == "main" else SEQ // P
                nc.scalar.activation(v_hi[:, kt:kt + T // P, :, 0:HEAD].rearrange("p k g d -> p (k g) d"),
                                     ring[:, c % R, :T].rearrange("p (k d) -> p k d", d=HEAD),
                                     ACT.Copy).then_inc(evac, 1)

            def fourier(layer, stream, first):
                T = length(stream)
                split(first)
                done(first)
                for tt in range(T // P):
                    nc.scalar.activation(y_hi[:, 4 + tt, :], bank[tt][:, :], ACT.Copy).then_inc(hi_ready, 1)
                n = 4 if T == SEQ else 1
                for c in range(first + 1, first + 1 + n):
                    split(c)
                done(first + n)
                for fb in range(2):
                    nc.scalar.activation(y_hi[:, 2 + fb, :T], bank[fb][:, :T], ACT.Copy).then_inc(hi_ready, 1)

            def qk(layer, stream, blocks, first):
                T = length(stream)
                begun(first)
                if len(blocks) > 1:
                    act.wait_ge(s_free, C.next(s_free))

                def square(n):
                    if n >= 2:
                        act.wait_ge(ss_ready, ss0 + n - 1)
                    nc.scalar.activation(scr[:, n % 2, :T], z[:, blocks[n], :T], ACT.Square).then_inc(sq_ready, 1)

                ss0 = C.now(ss_ready)
                square(0)
                for n in range(len(blocks)):
                    if n + 1 < len(blocks):
                        square(n + 1)
                    act.wait_ge(ss_ready, ss0 + n + 1)
                    if n:
                        act.wait_ge(s_qn, C.next(s_qn))
                    root(bank[n % 2], T, HEAD)
                C.next(ss_ready, len(blocks))
                C.next(s_qn)

            def attention(layer, stream):
                T = length(stream)
                kts = range(0 if stream == "main" else SEQ // P, KT_ALL)
                st0 = C.now(s_st)
                for h in range(N_HEADS):
                    act.wait_ge(s_mrow, C.next(s_mrow))
                    act.wait_ge(s_q, C.next(s_q))
                    nc.scalar.activation(y_lo[HEAD:HEAD + 1, 6 + h % 2, :T], bank[3][0:1, :T], ACT.Copy,
                                         scale=-1.0).then_inc(s_shift, 1)
                    for n, kt in enumerate(kts):
                        act.wait_ge(s_st, C.next(s_st))
                        k = C.now(s_st) - 1
                        if k >= 2:
                            act.wait_ge(s_p, k - 1)
                        nc.scalar.activation(z[:, 13 + k % 2, :T], bank[k % 2][:, :T], ACT.Exp,
                                             scale=HEAD ** -0.5).then_inc(s_exp, 1)
                C.next(s_on, N_HEADS)
                upper(4, lambda k: z[:, Z_Q + k, :T], lambda k: y_hi[:, 4 + k, :T])

            def merge(layer, stream, first):
                T = length(stream)

                def body(c, u, off):
                    split(c, off)
                    if u % R == 3:
                        return
                    done(c, off)
                    g = u % R
                    act.wait_ge(post, off + (c - g + R))
                    nc.scalar.activation(scr[:, g, :T], ring[:, c % R, :T], ACT.Sigmoid).then_inc(evac, 1)
                grouped(act, 32, first, body, C)
                upper(KB, lambda k: z[:, k, :T], lambda k: h_hi[:, k, :T])

            def ff(layer, stream, first):
                T = length(stream)

                def body(c, u, off):
                    split(c, off)
                    if u % 16 >= KB:
                        return
                    done(c, off)
                    act.wait_ge(post, off + (c - 1 + R))
                    nc.scalar.activation(scr[:, u % 2, :T], ring[:, c % R, :T], ACT.Relu).then_inc(evac, 1)
                grouped(act, 64, first, body, C, size=16)

            act.wait_ge(s_vec, 16)
            act.wait_ge(consts, 1)
            nc.scalar.activation(c_act[:, :], vec[:, 0:16], ACT.Silu).then_inc(s_silu, 1)
            for t in range(-LEAD, 0):
                split(t)
            lam = vec[:, VCOL["lru_lam"][0]:VCOL["lru_lam"][0] + 4]
            step(nc.scalar.activation(small[:, 0:4], lam, ACT.Abs))
            nc.scalar.activation(small[:, 4:8], small[:, 0:4], ACT.Exp, scale=-1.0).then_inc(s_lam, 1)
            for n, (kind, layer, stream, first) in enumerate(steps):
                if kind == "mod":
                    mod_tiles(layer, first)
                elif kind == "norm1":
                    norm(layer, stream, first, 0)
                elif kind == "z":
                    z_tiles(layer, stream, first, 13)
                elif kind == "z_kv":
                    z_tiles(layer, stream, first, 0)
                elif kind == "fourier":
                    fourier(layer, stream, first)
                elif kind == "qk":
                    qk(layer, stream, [Z_K] if (layer, stream) == (1, "ctx") else list(range(Z_Q, Z_K + 1)), first)
                    if stream == "main":
                        pass
                elif kind == "attn":
                    attention(layer, stream)
                elif kind == "merge":
                    merge(layer, stream, first)
                elif kind == "w_o":
                    for c in range(first, first + KB):
                        split(c)
                elif kind == "norm2":
                    norm(layer, stream, first, 3)
                elif kind == "pre_mix":
                    gain_norm(first, residual=layer > 0)
                elif kind == "pre_ffn":
                    gain_norm(first)
                elif kind in ("post_mix", "post_ffn"):
                    post_norm(first)
                elif kind == "ab_conf":
                    ab_conf(first)
                elif kind == "ab_lru":
                    ab_lru(first)
                elif kind == "lru_gate":
                    lru(first)
                elif kind == "mix_out":
                    mix_out(first)
                elif kind == "ffn":
                    ffn(first)
                elif kind == "ml_qk":
                    ml_qk(first)
                elif kind == "ml_gates":
                    ml_gates(first)
                elif kind == "ml_v":
                    ml_v(first)
                elif kind == "mlstm":
                    mlstm()
                elif kind == "ff":
                    ff(layer, stream, first)

        @block.tensor
        def _(pe):
            C = Counts()

            def three(o, a_hi, a_lo, b_hi, b_lo, start, stop):
                nc.tensor.matmul(o, a_hi, b_hi, start=start, stop=False)
                nc.tensor.matmul(o, a_hi, b_lo, start=False, stop=False)
                return nc.tensor.matmul(o, a_lo, b_hi, start=False, stop=stop)

            def ready(c, off=0):
                pe.wait_ge(w_ready, off + (c + 1))
                pe.wait_ge(post, off + (c + 1))

            def w(c, k, n=P):
                return w_hi[:, c % R, k * n:(k + 1) * n], w_lo[:, c % R, k * n:(k + 1) * n]

            def product(c, T, a_hi, a_lo, blocks=range(KB), o=None, last=True, first_k=0, before=None):
                o = ring[:, c % R, :T] if o is None else o
                for n, k in enumerate(blocks):
                    if before:
                        before(k)
                    m = three(o, *w(c, k), a_hi[:, k, :T], a_lo[:, k, :T], n == 0, n == len(blocks) - 1)
                if last:
                    m.then_inc(tile_done, 1)

            def sums(n, T, lhs, ps):
                for k in range(n):
                    pe.wait_ge(sq_ready, C.next(sq_ready))
                    nc.tensor.matmul(ps(k)[:, :T], lhs, scr[:, k % 2, :T], start=(k == 0), stop=(k == n - 1))\
                        .then_inc(ss_ready, 1)

            def blocks_ready(k0):
                return lambda k: pe.wait_ge(lo_ready, k0 + k + 1)

            def mod_tiles(first):
                def body(c, u, off):
                    ready(c, off)
                    o = ring[:, c % R, 0:2]
                    for k in range(KB):
                        m = three(o, *w(c, k), c_hi[:, k, :], c_lo[:, k, :], k == 0, k == KB - 1)
                    m.then_inc(tile_done, 1)
                grouped(pe, 48, first, body, C)

            def z_tiles(stream, first, n):
                T = length(stream)
                k0 = C.now(lo_ready)
                C.next(lo_ready, KB)

                def body(c, u, off):
                    ready(c, off)
                    product(c, T, h_hi, h_lo, before=blocks_ready(k0) if u == 0 else None)
                grouped(pe, n, first, body, C)
                c = first + n
                ready(c)
                for tt in range(T // P):
                    s = slice(tt * P, (tt + 1) * P)
                    for k in range(KB):
                        m = three(ring[:, c % R, s], h_hi[:, k, s], h_lo[:, k, s], *w(c, k), k == 0, k == KB - 1)
                m.then_inc(tile_done, 1)

            def fourier(stream, first):
                T = length(stream)
                pe.wait_ge(lo_ready, C.next(lo_ready, 2))
                ready(first)
                for tt in range(T // P):
                    s = slice(tt * P, (tt + 1) * P)
                    for fb in range(2):
                        m = three(bank[tt][:, fb * 256:(fb + 1) * 256], y_hi[:, 2 + fb, s], y_lo[:, 2 + fb, s],
                                  *w(first, 0, 256), True, True)
                m.then_inc(tile_done, 1)
                pe.wait_ge(lo_ready, C.next(lo_ready, T // P))
                per, nkt = TILE // T, T // P
                total = 2 * nkt
                for idx in range(total):
                    c = first + 1 + idx // per
                    cs, kt = divmod(idx, nkt)
                    if idx % per == 0:
                        ready(c)
                    for fb in range(2):
                        a = slice(fb * 256 + cs * P, fb * 256 + (cs + 1) * P)
                        m = three(bank[fb][:, :T], y_hi[:, 4 + kt, a], y_lo[:, 4 + kt, a],
                                  *w(c, idx % per, T), idx == 0, idx == total - 1)
                    if idx % per == per - 1:
                        m.then_inc(tile_done, 1)

            def qk(stream, n_blocks):
                T = length(stream)

                def total(n):
                    pe.wait_ge(sq_ready, C.next(sq_ready))
                    if n >= 2:
                        pe.wait_ge(root_ready, root0 + n - 1)
                    nc.tensor.matmul(bank[n % 2][:, :T], head_ones, scr[:, n % 2, :T], start=True, stop=True)\
                        .then_inc(ss_ready, 1)

                if n_blocks > 1:
                    pe.wait_ge(lo_ready, C.now(lo_ready, 2))
                root0 = C.now(root_ready)
                C.next(root_ready, n_blocks)
                total(0)
                for n in range(n_blocks):
                    if n + 1 < n_blocks:
                        total(n + 1)
                    pe.wait_ge(s_qn, C.next(s_qn))
                    if stream == "main":
                        b = n if n_blocks > 1 else Z_K - Z_Q
                        nc.tensor.matmul(bank[2 + n % 2][:, :T], rot, z[:, Z_Q + b, :T], start=True, stop=True)\
                            .then_inc(s_rot, 1)

            def attention(stream, first):
                T = length(stream)
                pe.wait_ge(post, first + R)
                kts = list(range(0 if stream == "main" else SEQ // P, KT_ALL))
                c0, n_k = kts[0] * P, len(kts) * P
                nq = T // P

                def scores(h):
                    g, s = h // 4, 6 + h % 2
                    pe.wait_ge(s_q, C.next(s_q))
                    for qt in range(nq):
                        n = C.next(s_score)
                        if n > 2:
                            pe.wait_ge(s_max, n - 2)
                        q = slice(qt * P, (qt + 1) * P)
                        slot = (n - 1) % 2
                        for a in range(0, n_k, SEQ):
                            e = min(a + SEQ, n_k)
                            o = ring[:, 2 * slot + a // SEQ, 0:e - a]
                            nc.tensor.matmul(o, y_hi[:, s, q], k_pair[:, g, c0 + a:c0 + e], start=True, stop=False)
                            m = nc.tensor.matmul(o, y_lo[0:HEAD, s, q], k_one[0:HEAD, g, c0 + a:c0 + e],
                                                 start=False, stop=True)
                        m.then_inc(s_score, 1)

                def max_row(h):
                    if C.now(s_shift):
                        pe.wait_ge(s_shift, C.now(s_shift))
                    for qt in range(nq):
                        pe.wait_ge(s_max, C.next(s_max))
                        m = nc.tensor.matmul(bank[3][0:1, qt * P:(qt + 1) * P], mx[:, h % 2, qt:qt + 1], ident,
                                             start=True, stop=True)
                    m.then_inc(s_mrow, 1)

                def score_t(h, n):
                    g, s = h // 4, 6 + h % 2
                    if n == 0:
                        pe.wait_ge(s_shift, C.next(s_shift))
                    k = C.next(s_st) - 1
                    if k >= 2:
                        pe.wait_ge(s_exp, k - 1)
                    keys = slice(kts[n] * P, (kts[n] + 1) * P)
                    nc.tensor.matmul(bank[k % 2][:, :T], k_pair[:, g, keys], y_hi[:, s, :T], start=True, stop=False)
                    nc.tensor.matmul(bank[k % 2][:, :T], k_one[0:HEAD + 1, g, keys], y_lo[0:HEAD + 1, s, :T],
                                     start=False, stop=True).then_inc(s_st, 1)

                def values(h, n):
                    g = h // 4
                    k = C.next(s_p)
                    pe.wait_ge(s_p, k)
                    if n == 0 and C.now(s_on):
                        pe.wait_ge(s_on, C.now(s_on))
                    b = 4 + (k - 1) % 2
                    m = three(bank[2][:, :T], v_hi[:, kts[n], g, :], v_lo[:, kts[n], g, :],
                              y_hi[:, b, :T], y_lo[:, b, :T], n == 0, n == len(kts) - 1)
                    m.then_inc(s_pv, 1)
                    if n == len(kts) - 1:
                        C.next(s_on)

                scores(0)
                max_row(0)
                for h in range(N_HEADS):
                    score_t(h, 0)
                    score_t(h, 1)
                    if h + 1 < N_HEADS:
                        scores(h + 1)
                    for n in range(len(kts)):
                        values(h, n)
                        if n + 2 < len(kts):
                            score_t(h, n + 2)
                    if h + 1 < N_HEADS:
                        max_row(h + 1)

            def merge(stream, first):
                T = length(stream)
                y_all = C.next(lo_ready, 2 + 2 + 4)

                def body(c, u, off):
                    ready(c, off)
                    if u % R < 3:
                        product(c, T, h_hi, h_lo)
                        return
                    pe.wait_ge(lo_ready, y_all)
                    product(c, T, y_hi, y_lo, range(0, 2), last=False)
                    product(c, T, y_hi, y_lo, range(2, 4), o=bank[0][:, :T], last=False)
                    product(c, T, y_hi, y_lo, range(4, 8), o=bank[1][:, :T])
                grouped(pe, 32, first, body, C)

            def w_o(T, first):
                k0 = C.now(lo_ready)
                C.next(lo_ready, KB)

                def body(c, u, off):
                    ready(c, off)
                    product(c, T, h_hi, h_lo, before=blocks_ready(k0) if u == 0 else None)
                grouped(pe, KB, first, body, C)

            def ff(stream, first):
                T = length(stream)
                k0 = C.now(lo_ready)
                C.next(lo_ready, KB)

                def body(c, u, off):
                    ready(c, off)
                    if u % 16 < KB:
                        product(c, T, h_hi, h_lo, before=blocks_ready(k0) if u % 16 == 0 else None)
                    else:
                        def hidden(k):
                            if u % 16 == KB and k > KB - R:
                                pe.wait_ge(post, off + (c - KB + k + 1 + R))
                        product(c, T, y_hi, y_lo, before=hidden)
                grouped(pe, 64, first, body, C, size=16)

            def plain(n, first, a_hi, a_lo, split_first=KB):
                k0 = C.now(lo_ready)
                C.next(lo_ready, split_first)

                def body(c, u, off):
                    ready(c, off)
                    product(c, SEQ, a_hi, a_lo, before=blocks_ready(k0) if u == 0 and split_first else None)
                grouped(pe, n, first, body, C)

            def lru(first):
                for b in range(4):
                    pe.wait_ge(s_conv, C.next(s_conv))
                    nc.tensor.matmul(bank[0][:, :], ones, z[:, 4 + b, :], start=b == 0, stop=b == 3)\
                        .then_inc(ss_ready, 1)
                pe.wait_ge(root_ready, C.next(root_ready))
                sums(4, SEQ, ones, lambda k: bank[0])
                C.next(root_ready)
                pe.wait_ge(lo_ready, C.next(lo_ready, 4))
                ready(first)
                for b in range(4):
                    if b:
                        pe.wait_ge(s_gread, C.next(s_gread, 2))
                    for i in range(2):
                        m = three(bank[2 + i][:, :], *w(first, 4 * i + b), y_hi[:, 4 + b, :], y_lo[:, 4 + b, :],
                                  True, True)
                    m.then_inc(s_gate, 1)
                pe.wait_ge(s_gread, C.next(s_gread, 2))
                pe.sem_inc(tile_done, 1)

            def ffn(first):
                k0 = C.now(lo_ready)
                C.next(lo_ready, KB)

                def body(c, u, off):
                    pos, n = (u % 24, 8) if u < 48 else (u - 48, 6)
                    ready(c, off)
                    if pos < 2 * n:
                        product(c, SEQ, h_hi, h_lo, before=blocks_ready(k0) if u == 0 else None)
                        return

                    def hidden(k):
                        if pos == 2 * n and k >= n - 2:
                            pe.wait_ge(post, off + (c - 2 * (n - k) + 2 + R))
                    product(c, SEQ, y_hi, y_lo, range(n), before=hidden)
                grouped(pe, FFN_TILES, first, body, C, size=24)

            def ml_v(first):
                pe.wait_ge(s_bv, 16)
                for half in range(2):
                    if half:
                        pe.wait_ge(lo_ready, C.next(lo_ready, 4))
                    for n in range(4):
                        c = first + 4 * half + n
                        ready(c)
                        for tt in range(4):
                            s = slice(tt * P, (tt + 1) * P)
                            if n == 0:
                                nc.tensor.matmul(bank[tt][:, :], ones[0:1, :], xv[0:1, half, :], start=True, stop=False)
                            for r in range(2):
                                m = three(bank[tt][:, :], h_hi[:, 2 * n + r, s], h_lo[:, 2 * n + r, s],
                                          *w(c, r, SEQ), False, n == 3 and r == 1)
                        m.then_inc(tile_done, 1)

            def mlstm(first):
                pe.wait_ge(lo_ready, C.next(lo_ready, 4))
                pe.wait_ge(post, first + R)
                pe.wait_ge(s_row, C.next(s_row, 2))
                for tt in range(4):
                    m = nc.tensor.matmul(bank[0][:, tt * 8:tt * 8 + 8], xv[0:8, 3, tt * P:(tt + 1) * P],
                                         ident[0:8, 0:8], start=True, stop=True)
                m.then_inc(s_col, 1)
                pe.wait_ge(s_col, C.next(s_col, 2))

                def spread(h):
                    if h >= 2:
                        pe.wait_ge(s_thr, C.next(s_thr))
                    for i in range(2):
                        m = nc.tensor.matmul(bank[2 * (h % 2) + i][:, :],
                                             ident[gate_rows, 32 + h:33 + h].to_broadcast([8, P]), row[i], start=True, stop=True)
                    m.then_inc(s_bc, 1)

                def score_t(h, n):
                    b = 4 * (h % 2)
                    if n == 0:
                        pe.wait_ge(s_q, C.next(s_q))
                    k = C.next(s_st) - st0 - 1
                    if k >= 2:
                        pe.wait_ge(s_p, p0 + k - 1)
                    keys, o = slice(n * P, (n + 1) * P), ring[:, k % 2, n * P:]
                    nc.tensor.matmul(o, kv[:, b + 2, keys], kv[:, b, n * P:], start=True, stop=False)
                    nc.tensor.matmul(o, kv[0:HEAD, b + 3, keys], kv[0:HEAD, b + 1, n * P:], start=False, stop=True)\
                        .then_inc(s_st, 1)

                def values(h, n):
                    k = C.next(s_p)
                    pe.wait_ge(s_p, k)
                    if n == 0 and h:
                        pe.wait_ge(s_on, C.next(s_on))
                    b = 8 + 2 * ((k - p0 - 1) % 2)
                    vb, vc = 2 * n + h // 4, slice(h % 4 * P, (h % 4 + 1) * P)
                    j = slice(n * P, SEQ)
                    three(ring[:, 2, j], y_hi[:, vb, vc], y_lo[:, vb, vc], kv[:, b, j], kv[:, b + 1, j], n == 0, n == 3)
                    nc.tensor.matmul(ring[:, 3, j], ones_r[:, :], kv[:, b, j], start=n == 0, stop=False)
                    nc.tensor.matmul(ring[:, 3, j], ones_r[:, :], kv[:, b + 1, j], start=False, stop=n == 3)\
                        .then_inc(s_pv, 1)

                st0, p0 = C.now(s_st), C.now(s_p)
                spread(0)
                for h in range(N_HEADS):
                    score_t(h, 0)
                    score_t(h, 1)
                    if h + 1 < N_HEADS:
                        spread(h + 1)
                    for n in range(4):
                        values(h, n)
                        if n + 2 < 4:
                            score_t(h, n + 2)
                C.next(s_thr, 2)
                C.next(s_on)

                def total(n):
                    pe.wait_ge(sq_ready, C.next(sq_ready))
                    if n >= 2:
                        pe.wait_ge(root_ready, root0 + n - 1)
                    nc.tensor.matmul(bank[n % 2][:, :], ones, scr[:, n % 2, :], start=True, stop=True)\
                        .then_inc(ss_ready, 1)

                root0 = C.now(root_ready)
                C.next(root_ready, N_HEADS)
                for n in range(N_HEADS):
                    total(n)
                C.next(s_qn, N_HEADS)

            pe.sem_inc(tile_done, R)
            pe.wait_ge(s_in, 32)
            pe.wait_ge(lo_ready, C.next(lo_ready))
            for kind, layer, stream, first in steps:
                if kind == "mod":
                    mod_tiles(first)
                elif kind in ("norm1", "norm2"):
                    sums(KB, length(stream), ones, lambda k: bank[0])
                    C.next(root_ready)
                elif kind == "z":
                    z_tiles(stream, first, 13)
                elif kind == "z_kv":
                    z_tiles(stream, first, 1)
                elif kind == "fourier":
                    fourier(stream, first)
                elif kind == "conv":
                    pass
                elif kind == "qk":
                    qk(stream, 1 if (layer, stream) == (1, "ctx") else 5)
                elif kind == "attn":
                    attention(stream, first)
                elif kind == "merge":
                    merge(stream, first)
                elif kind == "w_o":
                    w_o(length(stream), first)
                elif kind in ("pre_mix", "pre_ffn", "post_mix", "post_ffn"):
                    sums(KB, SEQ, ones, lambda k: bank[0])
                    C.next(root_ready)
                elif kind == "ab_conf":
                    plain(8, first, h_hi, h_lo)
                elif kind == "ab_lru":
                    plain(8, first, h_hi, h_lo, 0)
                elif kind == "lru_gate":
                    lru(first)
                elif kind == "mix_out":
                    plain(8, first, *((h_hi, h_lo) if layer else (y_hi, y_lo)))
                elif kind == "ffn":
                    ffn(first)
                elif kind == "ml_qk":
                    plain(8, first, h_hi, h_lo)
                    plain(8, first + 8, h_hi, h_lo, 0)
                elif kind == "ml_gates":
                    plain(1, first, h_hi, h_lo, 0)
                elif kind == "ml_v":
                    ml_v(first)
                elif kind == "mlstm":
                    mlstm(first)
                elif kind == "ff":
                    ff(stream, first)

        @block.vector
        def _(dve):
            C = Counts()

            def step(ins, sem=dve_own):
                ins.then_inc(sem, 1)
                dve.wait_ge(sem, C.next(sem))

            def posted():
                dve.sem_inc(post, 1)
                C.next(post)

            def done(c, off=0):
                dve.wait_ge(tile_done, off + (c + 1 + R))

            def f(ap):
                return ap.bitcast(F32)

            def lower(n, src, dst, hi, bias=None, before=None):
                if before:
                    before(0)
                for k in range(n):
                    if before and k + 1 < n:
                        before(k + 1)
                    dve.wait_ge(hi_ready, C.next(hi_ready))
                    step(nc.vector.scalar_tensor_tensor(dst(k), src(k), bias(k) if bias else 0.0, f(hi(k)),
                                                   ALU.add, ALU.subtract), lo_ready)

            def both(src, hi, lo):
                step(nc.vector.tensor_copy(hi, src))
                step(nc.vector.tensor_tensor(lo, src, f(hi), ALU.subtract), lo_ready)

            def norm(layer, stream, part):
                T, src, s = length(stream), x_of(stream), int(stream == "ctx")
                dve.wait_ge(root_ready, C.next(root_ready))
                step(nc.vector.reciprocal(scr[:, 3, :T], scr[:, 2, :T]))

                def scaled(k):
                    step(nc.vector.scalar_tensor_tensor(scr[:, k % 2, :T], src[:, k, :T],
                                                   gain[:, layer, part // 3, s, k:k + 1], scr[:, 3, :T],
                                                   ALU.mult, ALU.mult), t_ready)
                lower(KB, lambda k: scr[:, k % 2, :T], lambda k: h_lo[:, k, :T], lambda k: h_hi[:, k, :T],
                      lambda k: mod[:, layer, part * KB + k, s:s + 1], before=scaled)

            def mod_tiles(layer, first):
                def body(c, u, off):
                    dve.wait_ge(evac, C.next(evac))
                    posted()
                grouped(dve, 48, first, body, C, {evac: R, post: R})
                for half in range(2):
                    for s in range(2):
                        sc = (3 * half + 1) * KB
                        g = VCOL[f"g{half + 1}_{layer}"][0]
                        step(nc.vector.scalar_tensor_tensor(gain[:, layer, half, s, :], mod[:, layer, sc:sc + KB, s],
                                                           1.0, vec[:, g:g + KB], ALU.add, ALU.mult))

            def z_tiles(stream, first, n):
                T = length(stream)

                def body(c, u, off):
                    dve.wait_ge(evac, C.next(evac))
                    posted()
                grouped(dve, n, first, body, C, {evac: R, post: R})
                c = first + n
                kt = 0 if stream == "main" else SEQ // P
                dve.wait_ge(evac, C.next(evac))
                step(nc.vector.tensor_tensor(v_lo[:, kt:kt + T // P, :, 0:HEAD].rearrange("p k g d -> p (k g) d"),
                                        ring[:, c % R, :T].rearrange("p (k d) -> p k d", d=HEAD),
                                        f(v_hi[:, kt:kt + T // P, :, 0:HEAD].rearrange("p k g d -> p (k g) d")),
                                        ALU.subtract), post)

            def fourier(stream, first):
                T = length(stream)
                for fb in range(2):
                    both(z[:, Z_F + fb, :T], y_hi[:, 2 + fb, :T], y_lo[:, 2 + fb, :T])
                for tt in range(T // P):
                    dve.wait_ge(hi_ready, C.next(hi_ready))
                    step(nc.vector.tensor_tensor(y_lo[:, 4 + tt, :], bank[tt][:, :], f(y_hi[:, 4 + tt, :]),
                                            ALU.subtract), lo_ready)
                posted()
                n = 4 if T == SEQ else 1
                for c in range(first + 1, first + 1 + n):
                    done(c)
                    posted()
                for fb in range(2):
                    dve.wait_ge(hi_ready, C.next(hi_ready))
                    step(nc.vector.tensor_tensor(y_lo[:, 2 + fb, :T], bank[fb][:, :T], f(y_hi[:, 2 + fb, :T]),
                                            ALU.subtract), lo_ready)

            def conv(layer, stream):
                T = length(stream)
                for b in range(2):
                    step(nc.vector.tensor_tensor(z[:, Z_C + b, :T], z[:, Z_C + b, :T], z[:, Z_X + b, :T], ALU.mult))
                wv = lambda j, b: v(f"w_conv{layer}", 2 * j + b)
                for b in range(2):
                    step(nc.vector.tensor_scalar(scr[:, b, :T], z[:, Z_C + b, :T], wv(1, b), None, ALU.mult))
                for b in range(2):
                    step(nc.vector.scalar_tensor_tensor(scr[:, b, 1:T], z[:, Z_C + b, 0:T - 1], wv(0, b),
                                                       scr[:, b, 1:T], ALU.mult, ALU.add))
                for b in range(2):
                    step(nc.vector.scalar_tensor_tensor(scr[:, b, 0:T - 1], z[:, Z_C + b, 1:T], wv(2, b),
                                                       scr[:, b, 0:T - 1], ALU.mult, ALU.add))
                for b in range(2):
                    step(nc.vector.tensor_tensor(scr[:, b, :T], scr[:, b, :T], z[:, Z_B + b, :T], ALU.mult))
                for b in range(2):
                    both(scr[:, b, :T], y_hi[:, b, :T], y_lo[:, b, :T])
                dve.sem_inc(s_free, 1)

            def qk(layer, stream, blocks):
                T = length(stream)
                if stream == "main":
                    dve.wait_ge(s_rope, C.next(s_rope, 16))
                for n, b in enumerate(blocks):
                    g = v(f"gk{layer}" if b == Z_K else f"gq{layer}")
                    dve.wait_ge(root_ready, C.next(root_ready))
                    step(nc.vector.reciprocal(scr[:, 3, :T], scr[:, 2, :T]))
                    step(nc.vector.scalar_tensor_tensor(z[:, b, :T], z[:, b, :T], g, scr[:, 3, :T],
                                                   ALU.mult, ALU.mult), s_qn)
                    if stream == "main":
                        dve.wait_ge(s_rot, C.next(s_rot))
                        step(nc.vector.tensor_tensor(z[:, 13, :T], bank[2 + n % 2][:, :T], z[:, 15, :T], ALU.mult))
                        step(nc.vector.tensor_tensor(z[:, b, :T], z[:, b, :T], z[:, 14, :T], ALU.mult))
                        step(nc.vector.tensor_tensor(z[:, b, :T], z[:, b, :T], z[:, 13, :T], ALU.add))
                c0 = 0 if stream == "main" else SEQ
                cols = slice(c0, c0 + T)
                step(nc.vector.tensor_copy(y_hi[:, 4, :T], z[:, Z_K, :T]))
                step(nc.vector.tensor_tensor(y_lo[:, 4, :T], z[:, Z_K, :T], f(y_hi[:, 4, :T]), ALU.subtract))
                for g in range(2):
                    s = slice(g * HEAD, (g + 1) * HEAD)
                    step(nc.vector.tensor_copy(k_pair[0:HEAD, g, cols], f(y_hi[s, 4, :T])))
                    step(nc.vector.tensor_copy(k_one[0:HEAD, g, cols], f(y_hi[s, 4, :T])))
                    step(nc.vector.tensor_copy(k_pair[HEAD:P, g, cols], f(y_lo[s, 4, :T])))

            def attention(stream):
                T = length(stream)
                n_kt = KT_ALL if stream == "main" else CTX // P
                nq = T // P

                def queries(h):
                    b, s = h // 2, slice(h % 2 * HEAD, (h % 2 + 1) * HEAD)
                    other = slice(HEAD - h % 2 * HEAD, P - h % 2 * HEAD)
                    src, slot = z[s, Z_Q + b, :T], 6 + h % 2
                    step(nc.vector.tensor_copy(y_hi[s, slot, :T], src))
                    step(nc.vector.tensor_copy(y_hi[other, slot, :T], f(y_hi[s, slot, :T])))
                    step(nc.vector.tensor_tensor(y_lo[0:HEAD, slot, :T], src, f(y_hi[s, slot, :T]), ALU.subtract), s_q)

                def maxima(h):
                    for qt in range(nq):
                        n = C.next(s_score)
                        dve.wait_ge(s_score, n)
                        slot = (n - 1) % 2
                        view = ring[:, 2 * slot:2 * slot + 2, :].rearrange("p a b -> p (a b)")[:, 0:n_kt * P]
                        step(nc.vector.reduce_max(mx[:, h % 2, qt:qt + 1], view, AX_X), s_max)

                def parts():
                    k = C.next(s_exp)
                    dve.wait_ge(s_exp, k)
                    if k > 2:
                        dve.wait_ge(s_pv, k - 2)
                    src, b = z[:, 13 + (k - 1) % 2, :T], 4 + (k - 1) % 2
                    step(nc.vector.tensor_copy(y_hi[:, b, :T], src))
                    step(nc.vector.tensor_tensor(y_lo[:, b, :T], src, f(y_hi[:, b, :T]), ALU.subtract), s_p)

                queries(0)
                maxima(0)
                for h in range(N_HEADS):
                    if h + 1 < N_HEADS:
                        queries(h + 1)
                    parts()
                    parts()
                    if h + 1 < N_HEADS:
                        maxima(h + 1)
                    for n in range(2, n_kt):
                        parts()
                    dve.wait_ge(s_pv, C.next(s_pv, n_kt))
                    b, s = h // 2, slice(h % 2 * HEAD, (h % 2 + 1) * HEAD)
                    step(nc.vector.reciprocal(scr[0:HEAD, 0, :T], bank[2][HEAD:P, :T]))
                    step(nc.vector.tensor_tensor(z[s, Z_Q + b, :T], bank[2][0:HEAD, :T], scr[0:HEAD, 0, :T],
                                            ALU.mult), s_on)
                C.next(s_st, N_HEADS * n_kt)
                dve.sem_inc(t_ready, 4)
                C.next(t_ready, 4)
                lower(4, lambda k: z[:, Z_Q + k, :T], lambda k: y_lo[:, 4 + k, :T], lambda k: y_hi[:, 4 + k, :T])

            def merge(stream, first):
                T = length(stream)

                def body(c, u, off):
                    if u % R < 3:
                        dve.wait_ge(evac, C.next(evac))
                        posted()
                        return
                    done(c, off)
                    for g, ps in enumerate((ring[:, c % R, :T], bank[0][:, :T], bank[1][:, :T])):
                        step(nc.vector.tensor_tensor(scr[:, g, :T], ps, scr[:, g, :T], ALU.mult))
                    step(nc.vector.tensor_tensor(scr[:, 0, :T], scr[:, 0, :T], scr[:, 1, :T], ALU.add))
                    m = u // R
                    o = z[:, m, :T] if isinstance(off, int) else at(z[:, :, :T], m, turn[0])
                    step(nc.vector.tensor_tensor(o, scr[:, 0, :T], scr[:, 2, :T], ALU.add), post)
                grouped(dve, 32, first, body, C, {evac: 3, dve_own: 4, post: R})
                dve.sem_inc(t_ready, KB)
                C.next(t_ready, KB)
                lower(KB, lambda k: z[:, k, :T], lambda k: h_lo[:, k, :T], lambda k: h_hi[:, k, :T])

            def residual(c, m, off, m_off, layer, stream, part):
                T, xs, s = length(stream), x_of(stream), int(stream == "ctx")
                done(c, off)
                g = part * KB + m
                g = mod[:, layer, g, s:s + 1] if isinstance(m_off, int) else \
                    mod[:, layer, bass.ds(m_off + g, 1), s:s + 1].rearrange("p o n -> p (o n)")
                o = at(xs[:, :, :T], m, m_off)
                return nc.vector.scalar_tensor_tensor(o, ring[:, c % R, :T], g, o, ALU.mult, ALU.add)

            def w_o(layer, stream, first):
                def body(c, u, off):
                    step(residual(c, u, off, off, layer, stream, 2), post)
                grouped(dve, KB, first, body, C, {post: R})

            def ff(layer, stream, first):
                T = length(stream)

                def body(c, u, off):
                    m = u % 16
                    if m < KB:
                        dve.wait_ge(evac, C.next(evac))
                        step(nc.vector.tensor_tensor(z[:, m % 2, :T], scr[:, m % 2, :T], scr[:, m % 2, :T], ALU.mult))
                        step(nc.vector.tensor_copy(y_hi[:, m, :T], z[:, m % 2, :T]))
                        step(nc.vector.tensor_tensor(y_lo[:, m, :T], z[:, m % 2, :T], f(y_hi[:, m, :T]),
                                                ALU.subtract), post)
                    else:
                        step(residual(c, m - KB, off, 0, layer, stream, 5), post)
                grouped(dve, 64, first, body, C, {evac: KB, dve_own: 2 * KB, post: 2 * KB}, size=16)

            def rms(part_gain, n=KB):
                dve.wait_ge(root_ready, C.next(root_ready))
                step(nc.vector.reciprocal(scr[:, 3, :], scr[:, 2, :]))

                def scaled(k):
                    step(nc.vector.scalar_tensor_tensor(scr[:, k % 2, :], x[:, k, :], part_gain(k), scr[:, 3, :],
                                                        ALU.mult, ALU.mult), t_ready)
                lower(n, lambda k: scr[:, k % 2, :], lambda k: h_lo[:, k, :], lambda k: h_hi[:, k, :], before=scaled)

            def post_norm(gain_of):
                dve.wait_ge(root_ready, C.next(root_ready))
                step(nc.vector.reciprocal(scr[:, 3, :], scr[:, 2, :]))
                for k in range(KB):
                    step(nc.vector.scalar_tensor_tensor(z[:, k, :], z[:, k, :], gain_of(k), scr[:, 3, :],
                                                        ALU.mult, ALU.mult))
                    step(nc.vector.tensor_tensor(x[:, k, :], x[:, k, :], z[:, k, :], ALU.add))
                dve.sem_inc(s_x, 1)

            def passed(n, first):
                def body(c, u, off):
                    dve.wait_ge(evac, C.next(evac))
                    posted()
                grouped(dve, n, first, body, C, {evac: R, post: R})

            def ab_conf(first):
                for n in range(8):
                    dve.wait_ge(evac, C.next(evac))
                    if n % 2 == 0:
                        posted()
                    else:
                        b = n // 2
                        step(nc.vector.tensor_tensor(z[:, b, :], z[:, b, :], scr[:, b % 2, :], ALU.mult), post)

            def ab_lru(first):
                width = 31
                n = 0
                for b in range(4):
                    o = z[:, 4 + b, :]
                    for j in range(width - 1, -1, -1):
                        w_col = v("conf_w", 4 * j + b)
                        back = width - 1 - j
                        if back == 0:
                            ins = nc.vector.tensor_scalar(o, z[:, b, :], w_col, v("conf_b", b), ALU.mult, ALU.add)
                        else:
                            ins = nc.vector.scalar_tensor_tensor(o[:, back:], z[:, b, 0:SEQ - back], w_col, o[:, back:],
                                                                 ALU.mult, ALU.add)
                        step(ins, s_conv if j == 0 else dve_own)
                        if j % 8 == 0 and n < 8:
                            n += 1
                            dve.wait_ge(evac, C.next(evac))
                            posted()
                assert n == 8

            def lru(first):
                for b in range(4):
                    o = xv[:, b, :]
                    for back in range(4):
                        w_col = v("lru_w", 4 * (3 - back) + b)
                        if back == 0:
                            step(nc.vector.tensor_scalar(o, z[:, 8 + b, :], w_col, v("lru_b", b), ALU.mult, ALU.add))
                        else:
                            step(nc.vector.scalar_tensor_tensor(o[:, back:], z[:, 8 + b, 0:SEQ - back], w_col,
                                                                o[:, back:], ALU.mult, ALU.add))
                    both(o, y_hi[:, 4 + b, :], y_lo[:, 4 + b, :])
                dve.wait_ge(root_ready, C.next(root_ready))
                for b in range(4):
                    step(nc.vector.tensor_tensor(z[:, 4 + b, :], z[:, 4 + b, :], scr[:, 2, :], ALU.subtract), t_ready)
                dve.wait_ge(root_ready, C.next(root_ready))
                step(nc.vector.reciprocal(scr[:, 3, :], scr[:, 2, :]))
                for b in range(4):
                    step(nc.vector.scalar_tensor_tensor(z[:, 4 + b, :], z[:, 4 + b, :], v("ln_g", b), scr[:, 3, :],
                                                        ALU.mult, ALU.mult), t_ready)
                for b in range(4):
                    dve.wait_ge(s_act, C.next(s_act))
                    both(z[:, 4 + b, :], y_hi[:, b, :], y_lo[:, b, :])
                dve.sem_inc(s_free, 1)
                for b in range(4):
                    dve.wait_ge(s_act, C.next(s_act))
                    step(nc.vector.tensor_scalar(z[:, 4 + b, :], scr[:, b, :], -1.0, 1.0, ALU.mult, ALU.add))
                    step(nc.vector.reciprocal(z[:, 4 + b, :], z[:, 4 + b, :]))
                    step(nc.vector.scalar_tensor_tensor(scr[:, b, :], scr[:, b, :], -2.0, z[:, 4 + b, :],
                                                        ALU.mult, ALU.mult), t_ready)
                dve.wait_ge(s_act, C.next(s_act, 4))
                for b in range(4):
                    step(nc.vector.tensor_tensor(z[:, b, :], z[:, b, :], xv[:, b, :], ALU.mult))
                    dve.wait_ge(s_act, C.next(s_act))
                    step(nc.vector.tensor_tensor(z[:, b, :], z[:, b, :], scr[:, b, :], ALU.mult))
                    step(nc.vector.tensor_tensor_scan(xv[:, b, :], z[:, 8 + b, :], z[:, b, :], 0.0, ALU.mult, ALU.add))
                    step(nc.vector.tensor_tensor(xv[:, b, :], xv[:, b, :], z[:, 12 + b, :], ALU.mult))
                    if b == 0:
                        done(first)
                    both(xv[:, b, :], y_hi[:, 4 + b, :], y_lo[:, 4 + b, :])
                posted()

            def ffn(first):
                step(nc.vector.memset(z[:, 0:KB, :], 0.0))

                def body(c, u, off):
                    pos, n = (u % 24, 8) if u < 48 else (u - 48, 6)
                    if pos < 2 * n:
                        if pos % 2 == 0:
                            dve.wait_ge(evac, C.next(evac))
                            posted()
                            return
                        m = pos // 2
                        done(c, off)
                        step(nc.vector.tensor_tensor(z[:, 8 + m % 2, :], ring[:, c % R, :], scr[:, m % 2, :], ALU.mult))
                        step(nc.vector.tensor_copy(y_hi[:, m, :], z[:, 8 + m % 2, :]))
                        step(nc.vector.tensor_tensor(y_lo[:, m, :], z[:, 8 + m % 2, :], f(y_hi[:, m, :]),
                                                     ALU.subtract), post)
                    else:
                        m = pos - 2 * n
                        done(c, off)
                        step(nc.vector.tensor_tensor(z[:, m, :], z[:, m, :], ring[:, c % R, :], ALU.add), post)
                grouped(dve, FFN_TILES, first, body, C, {evac: 8, dve_own: 16, post: 24}, size=24)

            def ml_gates(first):
                dve.wait_ge(evac, C.next(evac))
                posted()
                dve.sem_inc(s_row, 1)
                dve.wait_ge(s_act, C.next(s_act))
                g, low, run = scr[0:8, 0, :], scr[32:40, :, :], xv[0:8, 2, :]
                step(nc.vector.memset(scr[0:8, 3, :], 0.0))
                step(nc.vector.scalar_tensor_tensor(scr[0:8, 2, :], low[:, 0, :], 0.0, low[:, 1, :],
                                                    ALU.min, ALU.subtract))
                step(nc.vector.tensor_tensor_scan(run, scr[0:8, 2, :], scr[0:8, 3, :], 0.0, ALU.add, ALU.add))
                step(nc.vector.tensor_tensor(xv[0:8, 3, :], g, run, ALU.subtract))
                step(nc.vector.tensor_tensor_scan(scr[0:8, 2, :], scr[0:8, 3, :], xv[0:8, 3, :], 0.0, ALU.add, ALU.max))
                step(nc.vector.tensor_scalar(row[0], scr[0:8, 2, :], -1.0, None, ALU.mult))
                step(nc.vector.scalar_tensor_tensor(row[1], scr[0:8, 2, :], -1.0, run, ALU.mult, ALU.subtract))
                dve.sem_inc(s_row, 1)

            def ml_v(first):
                for half in range(2):
                    for tt in range(4):
                        dve.wait_ge(hi_ready, C.next(hi_ready))
                        b = 2 * tt + half
                        step(nc.vector.tensor_tensor(y_lo[:, b, :], bank[tt][:, :], f(y_hi[:, b, :]), ALU.subtract),
                             lo_ready)
                    for n in range(4):
                        posted()

            def mlstm():
                dve.wait_ge(s_col, C.next(s_col))
                step(nc.vector.tensor_copy(small[:, 0:32], bank[0][:, 0:32]), s_col)

                def queries_keys(h):
                    b, lo0 = 4 * (h % 2), h % 2 * HEAD
                    s, other = slice(lo0, lo0 + HEAD), slice(HEAD - lo0, P - lo0)
                    q, k = z[s, h // 2, :], z[s, 4 + h // 2, :]
                    step(nc.vector.tensor_copy(kv[s, b, :], q))
                    step(nc.vector.tensor_copy(kv[other, b, :], f(kv[s, b, :])))
                    step(nc.vector.tensor_tensor(kv[0:HEAD, b + 1, :], q, f(kv[s, b, :]), ALU.subtract))
                    step(nc.vector.tensor_scalar(kv[s, b + 2, :], k, HEAD ** -0.5, None, ALU.mult))
                    step(nc.vector.scalar_tensor_tensor(kv[other, b + 2, :], k, HEAD ** -0.5, f(kv[s, b + 2, :]),
                                                        ALU.mult, ALU.subtract))
                    step(nc.vector.tensor_copy(kv[0:HEAD, b + 3, :], f(kv[s, b + 2, :])), s_q)

                def diagonal(h, n):
                    if n == 0:
                        dve.wait_ge(s_act, C.next(s_act))
                    j = slice(n * P, (n + 1) * P)
                    step(nc.vector.tensor_tensor(scr[:, n % 2, j], xv[:, h % 2, j], causal, ALU.add), s_diag)

                def parts(h, n):
                    dve.wait_ge(s_exp, C.next(s_exp))
                    dve.wait_ge(s_st, C.next(s_st))
                    j = slice(n * P, SEQ)
                    k = C.now(s_st) - st0
                    step(nc.vector.tensor_tensor(scr[:, 2, j], ring[:, (k - 1) % 2, j], scr[:, n % 2, j], ALU.mult))
                    if k > 2:
                        dve.wait_ge(s_pv, pv0 + k - 2)
                    b = 8 + 2 * ((k - 1) % 2)
                    step(nc.vector.tensor_copy(kv[:, b, j], scr[:, 2, j]))
                    step(nc.vector.tensor_tensor(kv[:, b + 1, j], scr[:, 2, j], f(kv[:, b, j]), ALU.subtract), s_p)

                st0, pv0 = C.now(s_st), C.now(s_pv)
                queries_keys(0)
                for h in range(N_HEADS):
                    diagonal(h, 0)
                    diagonal(h, 1)
                    if h + 1 < N_HEADS:
                        queries_keys(h + 1)
                    for n in range(4):
                        parts(h, n)
                        if n + 2 < 4:
                            diagonal(h, n + 2)
                    dve.wait_ge(s_pv, C.next(s_pv, 4))
                    dve.wait_ge(s_thr, C.next(s_thr))
                    step(nc.vector.tensor_tensor(scr[:, 3, :], ring[:, 3, :], scr[:, 3, :], ALU.max))
                    step(nc.vector.scalar_tensor_tensor(scr[:, 3, :], ring[:, 3, :], -1.0, scr[:, 3, :],
                                                        ALU.mult, ALU.max))
                    step(nc.vector.reciprocal(scr[:, 3, :], scr[:, 3, :]))
                    step(nc.vector.tensor_tensor(head_out(h), ring[:, 2, :], scr[:, 3, :], ALU.mult), s_on)
                for h in range(N_HEADS):
                    dve.wait_ge(root_ready, C.next(root_ready))
                    step(nc.vector.reciprocal(scr[:, 3, :], scr[:, 2, :]))
                    step(nc.vector.scalar_tensor_tensor(head_out(h), head_out(h), v("head_g", h), scr[:, 3, :],
                                                        ALU.mult, ALU.mult), s_qn)
                    step(nc.vector.tensor_tensor(head_out(h), head_out(h), z[:, 8 + h, :], ALU.mult))
                    both(head_out(h), h_hi[:, h, :], h_lo[:, h, :])

            dve.sem_inc(post, R)
            C.next(post, R)
            step(nc.vector.memset(eps[:, :], EPS), consts)
            step(nc.vector.memset(f(k_one[HEAD:HEAD + 1, :, :]), 1.0))
            step(nc.vector.memset(f(v_hi[:, :, :, HEAD:P]), 1.0))
            step(nc.vector.memset(f(v_lo[:, :, :, HEAD:P]), 0.0))
            dve.wait_ge(s_silu, 1)
            c_in = c_act[:, :].rearrange("p (s k) -> p k s", s=2)
            both(c_in, c_hi[:, :, :], c_lo[:, :, :])
            dve.wait_ge(s_vec, 16)
            dve.wait_ge(s_lam, 1)
            lam = vec[:, VCOL["lru_lam"][0]:VCOL["lru_lam"][0] + 4]
            e_, r_, q_, a_ = (small[:, i:i + 4] for i in (4, 8, 12, 16))
            step(nc.vector.tensor_scalar(r_, e_, 2.0, None, ALU.add))
            step(nc.vector.reciprocal(r_, r_))
            step(nc.vector.tensor_tensor(r_, r_, e_, ALU.mult))
            step(nc.vector.tensor_tensor(q_, r_, r_, ALU.mult))
            step(nc.vector.tensor_scalar(a_, q_, 1.0 / 17, 1.0 / 15, ALU.mult, ALU.add))
            for odd in (13, 11, 9, 7, 5, 3, 1):
                step(nc.vector.tensor_tensor(a_, a_, q_, ALU.mult))
                step(nc.vector.tensor_scalar(a_, a_, 1.0 / odd, None, ALU.add))
            step(nc.vector.scalar_tensor_tensor(a_, a_, 2.0, r_, ALU.mult, ALU.mult))
            step(nc.vector.tensor_scalar(r_, lam, -1.0, 0.0, ALU.mult, ALU.max))
            step(nc.vector.tensor_tensor(a_, a_, r_, ALU.add))
            step(nc.vector.tensor_scalar(decay[:, :], a_, -8.0, None, ALU.mult))
            dve.wait_ge(s_in, 32)
            step(nc.vector.tensor_copy(ones_r[:, :], ones))
            for kind, layer, stream, first in steps:
                if kind == "mod":
                    mod_tiles(layer, first)
                    dve.wait_ge(s_in, 32)
                    dve.wait_ge(s_ctx, 16)
                elif kind == "norm1":
                    norm(layer, stream, 0)
                elif kind == "norm2":
                    norm(layer, stream, 3)
                elif kind == "z":
                    z_tiles(stream, first, 13)
                elif kind == "z_kv":
                    z_tiles(stream, first, 1)
                elif kind == "fourier":
                    fourier(stream, first)
                elif kind == "conv":
                    conv(layer, stream)
                elif kind == "qk":
                    qk(layer, stream, [Z_K] if (layer, stream) == (1, "ctx") else list(range(Z_Q, Z_K + 1)))
                elif kind == "attn":
                    attention(stream)
                elif kind == "merge":
                    merge(stream, first)
                elif kind == "w_o":
                    w_o(layer, stream, first)
                elif kind == "pre_mix":
                    rms(lambda k: v(f"pre_mix{layer}", k))
                elif kind == "pre_ffn":
                    rms(lambda k: v(f"pre_ffn{layer}", k))
                elif kind == "post_mix":
                    post_norm(lambda k: v(f"post_mix{layer}", k))
                elif kind == "post_ffn":
                    post_norm(lambda k: v(f"post_ffn{layer}", k))
                elif kind == "ab_conf":
                    ab_conf(first)
                elif kind == "ab_lru":
                    ab_lru(first)
                elif kind == "lru_gate":
                    lru(first)
                elif kind == "mix_out":
                    passed(KB, first)
                elif kind == "ffn":
                    ffn(first)
                elif kind == "ml_qk":
                    passed(8, first)
                    passed(8, first + 8)
                elif kind == "ml_gates":
                    ml_gates(first)
                elif kind == "ml_v":
                    ml_v(first)
                elif kind == "mlstm":
                    mlstm()
                elif kind == "ff":
                    ff(layer, stream, first)
            dve.sem_inc(s_final, 1)


def arrays_of(inputs):
    w = {k: np.asarray(a) for k, a in inputs.items()}
    mats, ropes = shape_tables()
    return {
        "ws": stream_tiles(w), "vecs": vector_table(w), "mats": mats, "ropes": ropes,
        "x_t": np.ascontiguousarray(w["x"][0].T), "ctx_t": np.ascontiguousarray(w["ctx"][0].T),
        "bv": np.ascontiguousarray(w["ml_b_in_2"][:, D:2 * D]),
    }


def kernel(**inputs):
    import concourse.bacc as bacc
    from concourse.bass_utils import run_bass_kernel_spmd

    nc = bacc.Bacc("TRN2", target_bir_lowering=False, num_devices=1)
    arrays = arrays_of(inputs)
    aps = [nc.dram_tensor(n, a.shape, mybir.dt.from_np(a.dtype), kind="ExternalInput").ap() for n, a in arrays.items()]
    out = nc.dram_tensor("out_t", (D, SEQ), F32, kind="ExternalOutput").ap()
    build(nc, *aps, out)
    r = run_bass_kernel_spmd(nc, [arrays], core_ids=[0])
    return np.ascontiguousarray(r.results[0]["out_t"].T).reshape(1, SEQ, D)
```

```python
from contextlib import ExitStack

import numpy as np
import concourse.bass as bass
from concourse import mybir

F32 = mybir.dt.float32
F32R = mybir.dt.float32r
ALU = mybir.AluOpType
ACT = mybir.ActivationFunctionType
AX_X = mybir.AxisListType.X

P = 128
D = 1024
KB = D // P
SEQ = 512
CTX = 256
DEPTH = 2
HEAD = 64
N_HEADS = 8
N_MOD = 6
FF = 4096
FF2 = 2816
EPS = 1e-6
R = 4
TILE = KB * P
LEAD = 3
FFN_GROUPS = ((0, 8), (8, 8), (16, 6))
FFN_TILES = sum(2 * n + KB for _, n in FFN_GROUPS)
KT_ALL = (SEQ + CTX) // P

Z_B, Z_C, Z_X, Z_F, Z_Q, Z_K = 0, 2, 4, 6, 8, 12

MOD_GROUPS = {
    ("mod", 0, "main"): (0, 0, 4), ("attn", 0, "ctx"): (0, 4, 8),
    ("qk", 0, "main"): (1, 0, 6), ("qk", 1, "ctx"): (1, 6, 1), ("qk", 1, "main"): (1, 7, 5),
}


def vector_columns():
    cols, at = {}, 0
    for name, n in (
        ("c", 8), ("c_ctx", 8), ("b_mod0", 48), ("b_mod1", 48),
        ("g1_0", 8), ("g1_1", 8), ("g2_0", 8), ("g2_1", 8),
        ("w_conv0", 6), ("w_conv1", 6), ("gq0", 1), ("gq1", 1), ("gk0", 1), ("gk1", 1),
        ("pre_mix0", 8), ("pre_mix1", 8), ("post_mix0", 8), ("post_mix1", 8),
        ("pre_ffn0", 8), ("pre_ffn1", 8), ("post_ffn0", 8), ("post_ffn1", 8),
        ("ab_b", 16), ("conf_w", 31 * 4), ("conf_b", 4), ("ln_g", 4), ("ln_b", 4),
        ("lru_w", 16), ("lru_b", 4), ("lru_ba", 4), ("lru_bx", 4), ("lru_lam", 4),
        ("ml_b", 16), ("ml_bg", 1), ("head_g", 8),
    ):
        cols[name] = (at, n)
        at += n
    return cols, at


VCOL, N_VCOL = vector_columns()


def plan():
    steps, at = [], 0

    def add(kind, n, layer=0, stream="main"):
        nonlocal at
        steps.append((kind, layer, stream, at))
        at += n + 4 * MOD_GROUPS.get((kind, layer, stream), (0, 0, 0))[2]

    def block(layer, stream):
        add("norm1", 0, layer, stream)
        add("z", 14, layer, stream)
        add("fourier", 5 if stream == "main" else 2, layer, stream)
        add("conv", 0, layer, stream)
        add("qk", 0, layer, stream)
        add("attn", 0, layer, stream)
        add("merge", 32, layer, stream)
        add("w_o", 8, layer, stream)
        add("norm2", 0, layer, stream)
        add("ff", 64, layer, stream)

    add("mod", 0, 0)
    block(0, "ctx")
    block(0, "main")
    add("norm1", 0, 1, "ctx")
    add("z_kv", 2, 1, "ctx")
    add("qk", 0, 1, "ctx")
    block(1, "main")
    add("pre_mix", 0, 0)
    add("ab_conf", 8)
    add("ab_lru", 8)
    add("lru_gate", 1)
    add("mix_out", 8, 0)
    add("post_mix", 0, 0)
    add("pre_ffn", 0, 0)
    add("ffn", FFN_TILES, 0)
    add("post_ffn", 0, 0)
    add("pre_mix", 0, 1)
    add("ml_qk", 16)
    add("ml_gates", 1)
    add("ml_v", 8)
    add("mlstm", 0)
    add("mix_out", 8, 1)
    add("post_mix", 0, 1)
    add("pre_ffn", 0, 1)
    add("ffn", FFN_TILES, 1)
    add("post_ffn", 0, 1)
    return steps, at


def stream_tiles(w):
    out = []

    def cols(m, first, n):
        part = m[:, first:first + n * P].reshape(KB, P, n, P)
        out.extend(part.transpose(2, 1, 0, 3).reshape(n, P, TILE))

    def fourier(length):
        k = np.arange(HEAD)
        ang = 2 * np.pi * np.outer(k, k) / HEAD
        t = np.zeros((P, TILE), np.float32)
        for i, fn in enumerate((np.cos, np.sin)):
            for g in range(2):
                t[g * HEAD:(g + 1) * HEAD, i * P + g * HEAD:i * P + (g + 1) * HEAD] = fn(ang) / 8.0
        out.append(t)
        k = np.arange(length)
        ang = 2 * np.pi * (np.outer(k, k) % length) / length
        big = np.stack([np.cos(ang), -np.sin(ang)]) / np.sqrt(length)
        big = big.astype(np.float32).reshape(2, length // P, P, length).transpose(0, 1, 2, 3)
        rows = big.reshape(2 * (length // P), P, length)
        per = TILE // length
        for i in range(0, rows.shape[0], per):
            out.append(rows[i:i + per].transpose(1, 0, 2).reshape(P, TILE))

    def ffn(gate, up, down):
        for first, n in FFN_GROUPS:
            for m in range(first, first + n):
                cols(gate, m * P, 1)
                cols(up, m * P, 1)
            for m in range(KB):
                t = np.zeros((P, TILE), np.float32)
                part = down[first * P:(first + n) * P, m * P:(m + 1) * P]
                t[:, :n * P] = part.reshape(n, P, P).transpose(1, 0, 2).reshape(P, n * P)
                out.append(t)

    for kind, layer, stream, at in plan()[0]:
        assert at == len(out), (kind, at, len(out))
        if (kind, layer, stream) in MOD_GROUPS:
            of, g0, n = MOD_GROUPS[kind, layer, stream]
            for g in range(g0, g0 + n):
                for kk in range(0, KB, 2):
                    part = w["w_mod"][of][kk * P:(kk + 2) * P, g * 512:(g + 1) * 512]
                    out.append(part.reshape(2, P, 512).transpose(1, 0, 2).reshape(P, TILE))
        if kind == "z":
            cols(w["w_in"][layer], 0, 14)
        elif kind == "z_kv":
            cols(w["w_in"][layer], 12 * P, 2)
        elif kind == "fourier":
            fourier(SEQ if stream == "main" else CTX)
        elif kind == "merge":
            branch = np.concatenate([w["w_conv_out"][layer], w["w_four_out"][layer], w["w_attn_out"][layer]])
            for m in range(KB):
                for g in range(3):
                    cols(w["w_in"][layer], 14 * P + g * D + m * P, 1)
                cols(branch, m * P, 1)
        elif kind == "w_o":
            cols(w["w_o"][layer], 0, 8)
        elif kind == "ff":
            for g in range(4):
                cols(w["w_ff1"][layer], g * D, 8)
                cols(w["w_ff2"][layer][g * D:(g + 1) * D], 0, 8)
        elif kind == "ab_conf":
            for b in range(4):
                cols(w["ab_w_in_2"][0], b * P, 1)
                cols(w["ab_w_in_2"][0], (4 + b) * P, 1)
        elif kind == "ab_lru":
            cols(w["ab_w_in_2"][0], 12 * P, 4)
            cols(w["ab_w_in_2"][0], 8 * P, 4)
        elif kind == "lru_gate":
            t = np.zeros((P, 2, 4, P), np.float32)
            for i, name in enumerate(("lru_w_a_2", "lru_w_x_2")):
                for h in range(8):
                    o = (h % 2) * HEAD
                    t[o:o + HEAD, i, h // 2, o:o + HEAD] = w[name][0, h]
            out.append(t.reshape(P, TILE))
        elif kind == "mix_out":
            cols(w["ml_w_out_2"][0] if layer else w["ab_w_out_2"][0], 0, 8)
        elif kind == "ffn":
            ffn(w["ffn_w_gate_2"][layer], w["ffn_w_up_2"][layer], w["ffn_w_down_2"][layer])
        elif kind == "ml_qk":
            cols(w["ml_w_in_2"][0], 0, 8)
            cols(w["ml_w_in_2"][0], 2 * D, 8)
        elif kind == "ml_gates":
            t = np.zeros((D, P), np.float32)
            t[:, 0:8] = w["ml_w_in_2"][0][:, 3 * D:3 * D + 8]
            t[:, 32:40] = w["ml_w_in_2"][0][:, 3 * D + 8:3 * D + 16]
            cols(t, 0, 1)
        elif kind == "ml_v":
            v = w["ml_w_in_2"][0][:, D:2 * D]
            for half in range(2):
                for kk in range(0, KB, 2):
                    part = v[kk * P:(kk + 2) * P, half * 512:(half + 1) * 512]
                    out.append(part.reshape(2, P, 512).transpose(1, 0, 2).reshape(P, TILE))
    return np.ascontiguousarray(np.stack(out), dtype=np.float32)


def vector_table(w):
    t = np.zeros((P, N_VCOL), np.float32)

    def put(name, v):
        at, n = VCOL[name]
        t[:, at:at + n] = np.asarray(v).reshape(n, P).T

    put("c", w["c"])
    put("c_ctx", w["c_ctx"])
    for i in range(2):
        put(f"b_mod{i}", w["b_mod"][i])
        put(f"g1_{i}", w["g_norm1"][i])
        put(f"g2_{i}", w["g_norm2"][i])
        put(f"w_conv{i}", w["w_conv"][i])
        put(f"gq{i}", np.tile(w["g_q"][i], 2))
        put(f"gk{i}", np.tile(w["g_k"][i], 2))
        for n in ("pre_mix", "post_mix", "pre_ffn", "post_ffn"):
            put(f"{n}{i}", w[f"{n}_g_2"][i])
    put("ab_b", w["ab_b_in_2"])
    put("conf_w", w["conf_conv_w_2"])
    put("conf_b", w["conf_conv_b_2"])
    put("ln_g", w["conf_ln_g_2"])
    put("ln_b", w["conf_ln_b_2"])
    put("lru_w", w["lru_conv_w_2"])
    put("lru_b", w["lru_conv_b_2"])
    put("lru_ba", w["lru_b_a_2"])
    put("lru_bx", w["lru_b_x_2"])
    put("lru_lam", w["lru_lambda_2"])
    b = w["ml_b_in_2"][0]
    put("ml_b", np.concatenate([b[:D], b[2 * D:3 * D]]))
    gb = np.zeros(P, np.float32)
    gb[0:8], gb[32:40] = b[3 * D:3 * D + 8], b[3 * D + 8:]
    put("ml_bg", gb)
    put("head_g", w["ml_head_g_2"])
    return t


def shape_tables():
    m = np.zeros((P, 5, P), np.float32)
    m[:, 0] = 1.0
    m[:, 1] = np.eye(P)
    for g in range(2):
        s = slice(g * HEAD, (g + 1) * HEAD)
        m[s, 2, s] = 1.0
    for p in range(P):
        lower = p % HEAD < HEAD // 2
        m[p + 32 if lower else p - 32, 3, p] = -1.0 if lower else 1.0
    m[:, 4] = np.where(np.arange(P)[:, None] <= np.arange(P)[None, :], 0.0, -1e30)
    n_freq = HEAD // 4
    inv = (np.float32(10000.0) ** (-np.arange(n_freq, dtype=np.float32) / n_freq)).astype(np.float32)
    t = np.arange(SEQ)
    ang = np.concatenate([(t // 64).astype(np.float32)[:, None] * inv, (t % 64).astype(np.float32)[:, None] * inv], -1)
    ang = np.tile(ang.T, (4, 1)).astype(np.float32)
    rope = np.stack([np.cos(ang), np.sin(ang)], axis=1).astype(np.float32)
    return m.reshape(P, 5 * P), rope.reshape(P, 2 * SEQ)


class Counts:

    def __init__(self):
        self.n, self.i, self.per, self.at = {}, None, {}, {}

    def now(self, sem, more=0):
        n = self.n.get(id(sem), 0) + more
        if self.i is not None and id(sem) in self.per:
            return self.i * self.per[id(sem)] + n
        assert self.i is None or n - more == self.at.get(id(sem), 0), "a count that changes in a loop"
        return n

    def next(self, sem, n=1):
        self.n[id(sem)] = self.n.get(id(sem), 0) + n
        return self.now(sem)

    def enter(self, i, per):
        self.at = dict(self.n)
        self.i, self.per = i, {id(k): n for k, n in per.items()}

    def leave(self, turns):
        for k, n in self.n.items():
            one = n - self.at.get(k, 0)
            assert one == self.per.get(k, 0), ("increments of one turn", one, self.per.get(k, 0))
            self.n[k] = self.at.get(k, 0) + turns * one
        self.i, self.per = None, {}


def build(nc, ws, vecs, mats, ropes, x_in, ctx_in, bv_in, out, upto=None):
    steps, n_tiles = plan()
    if upto is not None:
        n_tiles = steps[upto][3]
        steps = steps[:upto]

    with ExitStack() as stack:
        def sb(name, shape, dt=F32):
            return stack.enter_context(nc.sbuf_tensor(name, shape, dt))

        def sem(name):
            return stack.enter_context(nc.semaphore(name))

        raw = sb("raw", [P, R, TILE])
        w_hi = sb("w_hi", [P, R, TILE], F32R)
        w_lo = sb("w_lo", [P, R, TILE], F32R)
        x = sb("x", [P, KB, SEQ])
        xc = sb("xc", [P, KB, CTX])
        h_hi = sb("h_hi", [P, KB, SEQ], F32R)
        h_lo = sb("h_lo", [P, KB, SEQ], F32R)
        y_hi = sb("y_hi", [P, KB, SEQ], F32R)
        y_lo = sb("y_lo", [P, KB, SEQ], F32R)
        z = sb("z", [P, 16, SEQ])
        kv = sb("kv", [P, 12, SEQ], F32R)
        scr = sb("scr", [P, 4, SEQ])
        vec = sb("vec", [P, N_VCOL])
        mat = sb("mat", [P, 5 * P])
        mod = sb("mod", [P, DEPTH, N_MOD * KB, 2])
        gain = sb("gain", [P, DEPTH, 2, 2, KB])
        c_act = sb("c_act", [P, 16])
        c_parts = sb("c_parts", [P, KB, 4], F32R)
        pair = sb("pair", [4, 2])
        mx = sb("mx", [P, 2, 4])
        small = sb("small", [P, 64])
        eps = sb("eps", [P, 1])
        decay = sb("decay", [P, 4])
        ones_r = sb("ones_r", [P, P], F32R)
        bank = [stack.enter_context(nc.psum_tensor(f"bank{i}", [P, SEQ], F32)) for i in range(4, 8)]
        ring = stack.enter_context(nc.psum_tensor("ring", [P, R, SEQ], F32))

        ones, ident, head_ones, rot = (mat[:, i * P:(i + 1) * P] for i in range(4))
        causal = mat[:, 4 * P:5 * P]
        kvf = kv[:, :, :].rearrange("p a b -> p (a b)")
        nk = SEQ + CTX
        k_pair = kvf[:, 0:2 * nk].rearrange("p (g k) -> p g k", g=2)
        k_one = kvf[:, 2 * nk:4 * nk].rearrange("p (g k) -> p g k", g=2)
        v_hi = kvf[:, 4 * nk:6 * nk].rearrange("p (k g d) -> p k g d", k=KT_ALL, g=2)
        v_lo = kvf[:, 6 * nk:8 * nk].rearrange("p (k g d) -> p k g d", k=KT_ALL, g=2)


        xv = xc[:, :, :].rearrange("p a b -> p (a b)").rearrange("p (a b) -> p a b", b=SEQ)
        gate_rows = slice(32, 40)
        row = (xv[gate_rows, 2, :], xv[gate_rows, 3, :])

        def head_out(h):
            return z[:, h // 2 + 4 * (h % 2), :]

        def v(name, i=0):
            return vec[:, VCOL[name][0] + i:VCOL[name][0] + i + 1]

        loaded = [sem(f"loaded{i}") for i in range(R)]
        s_mat = sem("matrices_loaded")
        s_in = sem("x_loaded")
        s_ctx = sem("ctx_loaded")
        s_rope = sem("rope_loaded")
        s_bv = sem("v_bias_loaded")
        w_hi_ready = sem("w_hi_ready")
        w_ready = sem("w_ready")
        tile_done = sem("tile_done")
        post = sem("post")
        evac = sem("evac")
        sq_ready = sem("sq_ready")
        ss_ready = sem("ss_ready")
        root_ready = sem("root_ready")
        t_ready = sem("t_ready")
        hi_ready = sem("hi_ready")
        lo_ready = sem("lo_ready")
        consts = sem("constants_ready")
        dve_own = sem("vector_own")
        act_own = sem("scalar_own")
        s_score = sem("scores_ready")
        s_max = sem("max_ready")
        s_mrow = sem("max_row_ready")
        s_shift = sem("shift_ready")
        s_q = sem("q_ready")
        s_st = sem("scores_t_ready")
        s_exp = sem("exp_ready")
        s_p = sem("p_ready")
        s_pv = sem("pv_done")
        s_on = sem("o_read")
        s_recip = sem("reciprocals_ready")
        s_spread = sem("reciprocals_spread")
        s_vec = sem("vectors_loaded")
        s_silu = sem("conditions_activated")
        s_free = sem("scratch_free")
        s_qn = sem("q_normed")
        s_rot = sem("rotated")
        s_x = sem("residual_ready")
        s_conv = sem("conv_ready")
        s_gate = sem("lru_gates_ready")
        s_gread = sem("lru_gates_read")
        s_act = sem("activated")
        s_lam = sem("decay_ready")
        s_row = sem("gate_rows_ready")
        s_col = sem("gate_columns_ready")
        s_bc = sem("row_spread")
        s_diag = sem("diagonal_ready")
        s_thr = sem("threshold_ready")
        s_mod_rows = sem("mod_rows_ready")
        s_mod_cols = sem("mod_columns_ready")
        s_mod = sem("mod_ready")
        s_final = sem("result_ready")
        s_out = sem("stored")

        block = stack.enter_context(nc.Block())

        def length(stream):
            return SEQ if stream == "main" else CTX

        def x_of(stream):
            return x if stream == "main" else xc

        class ModGroups:

            def __init__(self, kind, layer, stream, first):
                self.layer, self.g0, self.n = MOD_GROUPS.get((kind, layer, stream), (0, 0, 0))
                self.first, self.tiles = first, 4 * self.n
                self.free = (2, 3) if kind == "attn" else (0, 1, 2, 3)
                self.stored = 0

            def share(self, i, of):
                return range(self.tiles * i // of, self.tiles * (i + 1) // of)

            def bank(self, g):
                return ring[:, self.free[g % len(self.free)], :]

            def rows(self, g):
                return z[0:4, Z_X + g % 2, :]

        def max_rows(stream):
            n, per = (2, 2) if stream == "main" else (1, 1)
            return ring[0:1, per - 1:n * per:per, CTX:SEQ]

        turn = [None]

        def grouped(eng, n, first, body, C, per=None, size=R):
            turns = n // size
            turn[0] = None
            if first + turns * size + LEAD > n_tiles:
                turns -= 1
            if turns > 1:
                with eng.Fori(0, turns, 1) as i:
                    C.enter(i, per or {})
                    turn[0] = i
                    for u in range(size):
                        body(first + u, u, i * size)
                    C.leave(turns)
                turn[0] = None
            else:
                turns = 0
            for u in range(turns * size, n):
                body(first + u, u, 0)

        def at(ap, block, off):
            if isinstance(off, int):
                return ap[:, block, :]
            return ap[:, bass.ds(off + block, 1), :].rearrange("p o n -> p (o n)")

        @block.sync
        def _(sp):
            sp.dma_start(vec[:, :], vecs).then_inc(s_vec, 16)
            sp.dma_start(raw[:, 0, :], ws[0]).then_inc(loaded[0], 16)
            sp.dma_start(mat[:, :], mats).then_inc(s_mat, 16)
            for t in range(1, R):
                sp.dma_start(raw[:, t, :], ws[t]).then_inc(loaded[t], 16)
            sp.dma_start(xc[:, :, :], ctx_in.rearrange("(k p) t -> p k t", p=P)).then_inc(s_ctx, 16)
            sp.dma_start(x[:, :, :], x_in.rearrange("(k p) t -> p k t", p=P)).then_inc(s_in, 16)
            groups = n_tiles // R - 1
            with sp.Fori(0, groups, 1) as i:
                for u in range(R):
                    sp.wait_ge(w_ready, i * R + (u + 1))
                    sp.dma_start(raw[:, u, :], ws[bass.ds(i * R + (R + u), 1)].rearrange("o p n -> (o p) n"))\
                        .then_inc(loaded[u], 16)
            for t in range((groups + 1) * R, n_tiles):
                sp.wait_ge(w_ready, t - R + 1)
                sp.dma_start(raw[:, t % R, :], ws[t]).then_inc(loaded[t % R], 16)
            sp.wait_ge(s_final, 1)
            sp.dma_start(out.rearrange("(k p) t -> p k t", p=P), x[:, :, :]).then_inc(s_out, 16)
            sp.wait_ge(s_out, 16)

        @block.gpsimd
        def _(pool):
            def lower(u, n):
                pool.wait_ge(w_hi_ready, n)
                nc.gpsimd.tensor_tensor(w_lo[:, u, :], raw[:, u, :], w_hi[:, u, :].bitcast(F32),
                                        ALU.subtract).then_inc(w_ready, 1)

            with pool.Fori(0, n_tiles // R, 1) as i:
                for u in range(R):
                    lower(u, i * R + (u + 1))
            for t in range(n_tiles // R * R, n_tiles):
                lower(t % R, t + 1)

        @block.scalar
        def _(act):
            C = Counts()

            def split(c, off=0):
                t = c + LEAD
                if isinstance(off, int) and t >= n_tiles:
                    return
                act.wait_ge(loaded[t % R], off * (16 // R) + 16 * (t // R + 1))
                act.wait_ge(tile_done, off + (t + 1))
                nc.scalar.activation(w_hi[:, t % R, :], raw[:, t % R, :], ACT.Copy).then_inc(w_hi_ready, 1)

            def done(c, off=0):
                act.wait_ge(tile_done, off + (c + 1 + R))

            def begun(at_tile):
                act.wait_ge(post, at_tile + R)

            def squares(src, n, T):
                for k in range(n):
                    if k >= 2:
                        act.wait_ge(ss_ready, C.next(ss_ready))
                    nc.scalar.activation(scr[:, k % 2, :T], src(k), ACT.Square).then_inc(sq_ready, 1)
                act.wait_ge(ss_ready, C.next(ss_ready, min(n, 2)))

            def root(ps, T, count):
                nc.scalar.activation(scr[:, 2, :T], ps[:, :T], ACT.Sqrt, bias=eps[:, 0:1], scale=1.0 / count)\
                    .then_inc(root_ready, 1)

            def upper(n, src, dst, bias=None):
                for k in range(n):
                    act.wait_ge(t_ready, C.next(t_ready))
                    if bias is None:
                        nc.scalar.activation(dst(k), src(k), ACT.Copy).then_inc(hi_ready, 1)
                    else:
                        nc.scalar.activation(dst(k), src(k), ACT.Identity, bias=bias(k)).then_inc(hi_ready, 1)

            def gain_norm(first, residual=True):
                begun(first)
                if residual:
                    act.wait_ge(s_x, C.next(s_x))
                squares(lambda k: x[:, k, :], KB, SEQ)
                root(bank[0], SEQ, D)
                upper(KB, lambda k: scr[:, k % 2, :], lambda k: h_hi[:, k, :])

            def post_norm(first):
                begun(first)
                squares(lambda k: z[:, k, :], KB, SEQ)
                root(bank[0], SEQ, D)

            def biased(c, off, o, func, column):
                b = column if isinstance(off, int) else column
                nc.scalar.activation(o, ring[:, c % R, :], func, bias=b).then_inc(evac, 1)

            def col(name, i, off):
                at0 = VCOL[name][0] + i
                return vec[:, at0:at0 + 1] if isinstance(off, int) else vec[:, bass.ds(off + at0, 1)]

            def ab_conf(first):
                for n in range(8):
                    c, b = first + n, n // 2
                    split(c)
                    done(c)
                    if n % 2 == 0:
                        biased(c, 0, z[:, b, :], ACT.Identity, col("ab_b", b, 0))
                    else:
                        act.wait_ge(post, c - 3 + R)
                        biased(c, 0, scr[:, b % 2, :], ACT.Sigmoid, col("ab_b", 4 + b, 0))

            def ab_lru(first):
                for n in range(8):
                    split(first + n)
                    done(first + n)
                    if n < 4:
                        biased(first + n, 0, z[:, 8 + n, :], ACT.Identity, col("ab_b", 12 + n, 0))
                    else:
                        biased(first + n, 0, z[:, 8 + n, :], ACT.Gelu_apprx_tanh, col("ab_b", 8 + n - 4, 0))

            def lru(first):
                split(first)
                act.wait_ge(ss_ready, C.next(ss_ready, 4))
                nc.scalar.activation(scr[:, 2, :], bank[0][:, :], ACT.Copy, scale=1.0 / (4 * P)).then_inc(root_ready, 1)
                act.wait_ge(t_ready, C.next(t_ready, 4))
                squares(lambda k: z[:, 4 + k, :], 4, SEQ)
                root(bank[0], SEQ, 4 * P)
                for b in range(4):
                    act.wait_ge(t_ready, C.next(t_ready))
                    nc.scalar.activation(z[:, 4 + b, :], z[:, 4 + b, :], ACT.Silu, bias=v("ln_b", b)).then_inc(s_act, 1)
                for b in range(4):
                    act.wait_ge(s_gate, C.next(s_gate))
                    nc.scalar.activation(z[:, 8 + b, :], bank[2][:, :], ACT.Sigmoid, bias=v("lru_ba", b))\
                        .then_inc(s_gread, 1)
                    nc.scalar.activation(z[:, b, :], bank[3][:, :], ACT.Sigmoid, bias=v("lru_bx", b))\
                        .then_inc(s_gread, 1)
                act.wait_ge(s_free, C.next(s_free))
                act.wait_ge(s_gread, C.next(s_gread, 8))
                for b in range(4):
                    nc.scalar.activation(scr[:, b, :], z[:, 8 + b, :], ACT.Tanh, scale=decay[:, b:b + 1])\
                        .then_inc(s_act, 1)
                for b in range(4):
                    act.wait_ge(s_act, 5 + b)
                    nc.scalar.activation(z[:, 8 + b, :], z[:, 8 + b, :], ACT.Exp, scale=decay[:, b:b + 1])\
                        .then_inc(s_act, 1)
                for b in range(4):
                    act.wait_ge(t_ready, C.next(t_ready))
                    nc.scalar.activation(scr[:, b, :], scr[:, b, :], ACT.Sqrt).then_inc(s_act, 1)

            def mix_out(first):
                def body(c, u, off):
                    split(c, off)
                    done(c, off)
                    nc.scalar.activation(at(z, u, off), ring[:, c % R, :], ACT.Copy).then_inc(evac, 1)
                grouped(act, KB, first, body, C)

            def ffn(first):
                def body(c, u, off):
                    pos, n = (u % 24, 8) if u < 48 else (u - 48, 6)
                    split(c, off)
                    if pos >= 2 * n or pos % 2:
                        return
                    done(c, off)
                    act.wait_ge(post, off + (c - 2 + R))
                    nc.scalar.activation(scr[:, pos // 2 % 2, :], ring[:, c % R, :], ACT.Silu).then_inc(evac, 1)
                grouped(act, FFN_TILES, first, body, C, size=24)

            def ml_qk(first):
                act.dma_start(xv[0:1, 0:2, :], bv_in.rearrange("o (a n) -> o a n", a=2)).then_inc(s_bv, 16)

                def qk_body(c, u, off):
                    split(c, off)
                    done(c, off)
                    biased(c, off, at(z, u, off), ACT.Identity, col("ml_b", u, off))

                def o_body(c, u, off):
                    split(c, off)
                    done(c, off)
                    biased(c, off, at(z, 8 + u, off), ACT.Sigmoid, col("ml_b", 8 + u, off))
                grouped(act, 8, first, qk_body, C)
                grouped(act, 8, first + 8, o_body, C)

            def ml_gates(first):
                split(first)
                done(first)
                biased(first, 0, scr[:, 0, :], ACT.Identity, v("ml_bg"))
                own_wait()
                f_rows = slice(32, 40)
                step(nc.scalar.activation(scr[f_rows, 1, :], scr[f_rows, 0, :], ACT.Abs))
                step(nc.scalar.activation(scr[f_rows, 1, :], scr[f_rows, 1, :], ACT.Exp, scale=-1.0))
                nc.scalar.activation(scr[f_rows, 1, :], scr[f_rows, 1, :], ACT.Ln, bias=mat[f_rows, 0:1])\
                    .then_inc(s_act, 1)

            def own_wait():
                act.wait_ge(s_row, C.next(s_row))

            def step(ins):
                ins.then_inc(act_own, 1)
                act.wait_ge(act_own, C.next(act_own))

            def ml_v(first):
                for half in range(2):
                    for n in range(4):
                        split(first + 4 * half + n)
                    done(first + 4 * half + 3)
                    for tt in range(4):
                        nc.scalar.activation(y_hi[:, 2 * tt + half, :], bank[tt][:, :], ACT.Copy).then_inc(hi_ready, 1)

            def mlstm():
                for h in range(N_HEADS):
                    act.wait_ge(s_bc, C.next(s_bc))
                    spread = bank[2 * (h % 2)]
                    nc.scalar.activation(xv[:, h % 2, :], spread[:, :], ACT.Copy).then_inc(s_act, 1)
                    for sb_ in range(4):
                        act.wait_ge(s_diag, C.next(s_diag))
                        j = sb_ * P
                        a_col = small[:, sb_ * 8 + h:sb_ * 8 + h + 1]
                        e = scr[:, sb_ % 2, :]
                        m = nc.scalar.activation(e[:, j:j + P], e[:, j:j + P], ACT.Exp, bias=a_col)
                        if sb_ < 3:
                            m.then_inc(act_own, 1)
                            C.next(act_own)
                            m = nc.scalar.activation(e[:, j + P:], spread[:, j + P:], ACT.Exp, bias=a_col)
                        m.then_inc(s_exp, 1)
                    if h:
                        act.wait_ge(s_on, C.next(s_on))
                    nc.scalar.activation(scr[:, 3, :], bank[2 * (h % 2) + 1][:, :], ACT.Exp).then_inc(s_thr, 1)
                act.wait_ge(s_on, C.next(s_on))
                ss0 = C.now(ss_ready)

                def square(n):
                    if n >= 2:
                        act.wait_ge(ss_ready, ss0 + n - 1)
                    nc.scalar.activation(scr[:, n % 2, :], head_out(n), ACT.Square).then_inc(sq_ready, 1)

                square(0)
                for n in range(N_HEADS):
                    if n + 1 < N_HEADS:
                        square(n + 1)
                    act.wait_ge(ss_ready, ss0 + n + 1)
                    if n:
                        act.wait_ge(s_qn, C.next(s_qn))
                    root(bank[n % 2], SEQ, P)
                C.next(ss_ready, N_HEADS)
                C.next(s_qn)

            def norm(layer, stream, first, part):
                T, src, s = length(stream), x_of(stream), int(stream == "ctx")
                begun(first)
                if part == 0 and stream == "main":
                    act.dma_start(z[:, 14:16, :], ropes.rearrange("p (a t) -> p a t", a=2)).then_inc(s_rope, 16)
                if part == 0 and stream == "ctx" and layer == 0:
                    act.wait_ge(s_ctx, 16)
                if part == 0 and stream == "main" and layer == 0:
                    act.wait_ge(s_in, 16)
                squares(lambda k: src[:, k, :T], KB, T)
                root(bank[0], T, D)
                upper(KB, lambda k: scr[:, k % 2, :T], lambda k: h_hi[:, k, :T],
                      lambda k: mod[:, layer, part * KB + k, s:s + 1])

            def mod_tiles(mg, numbers):
                for i in numbers:
                    split(mg.first + i)
                    if i % 4 == 0 and i:
                        mod_rows(mg, i // 4 - 1)
                if mg.tiles in (numbers.stop,) and len(numbers):
                    mod_rows(mg, mg.n - 1)

            def mod_rows(mg, g):
                done(mg.first + 4 * g + 3)
                if g >= 2:
                    act.wait_ge(s_mod_cols, C.now(s_mod_rows) - 1)
                nc.scalar.activation(mg.rows(g), mg.bank(g)[0:4, :], ACT.Copy).then_inc(s_mod_rows, 1)
                C.next(s_mod_rows)

            def z_tiles(layer, stream, first, n):
                T = length(stream)

                def body(c, u, off):
                    split(c, off)
                    done(c, off)
                    nc.scalar.activation(at(z[:, :, :T], (Z_K if n == 0 else 0) + u, off), ring[:, c % R, :T],
                                         ACT.Copy).then_inc(evac, 1)
                grouped(act, max(n, 1), first, body, C)
                c = first + max(n, 1)
                split(c)
                done(c)
                kt = 0 if stream == "main" else SEQ // P
                nc.scalar.activation(v_hi[:, kt:kt + T // P, :, 0:HEAD].rearrange("p k g d -> p (k g) d"),
                                     ring[:, c % R, :T].rearrange("p (k d) -> p k d", d=HEAD),
                                     ACT.Copy).then_inc(evac, 1)

            def fourier(layer, stream, first):
                T = length(stream)
                split(first)
                done(first)
                for tt in range(T // P):
                    nc.scalar.activation(y_hi[:, 4 + tt, :], bank[tt][:, :], ACT.Copy).then_inc(hi_ready, 1)
                n = 4 if T == SEQ else 1
                for c in range(first + 1, first + 1 + n):
                    split(c)
                done(first + n)
                for fb in range(2):
                    nc.scalar.activation(y_hi[:, 2 + fb, :T], bank[fb][:, :T], ACT.Copy).then_inc(hi_ready, 1)

            def qk(layer, stream, blocks, first):
                T = length(stream)
                mg = ModGroups("qk", layer, stream, first)
                begun(first)
                if len(blocks) > 1:
                    act.wait_ge(s_free, C.next(s_free))

                def square(n):
                    if n >= 2:
                        act.wait_ge(ss_ready, ss0 + n - 1)
                    nc.scalar.activation(scr[:, n % 2, :T], z[:, blocks[n], :T], ACT.Square).then_inc(sq_ready, 1)

                ss0 = C.now(ss_ready)
                square(0)
                for n in range(len(blocks)):
                    if n + 1 < len(blocks):
                        square(n + 1)
                    act.wait_ge(ss_ready, ss0 + n + 1)
                    if n:
                        act.wait_ge(s_qn, C.next(s_qn))
                    root(bank[n % 2], T, HEAD)
                    if n:
                        mod_tiles(mg, mg.share(2 * n - 1, 2 * len(blocks)))
                    mod_tiles(mg, mg.share(2 * n, 2 * len(blocks)))
                mod_tiles(mg, mg.share(2 * len(blocks) - 1, 2 * len(blocks)))
                C.next(ss_ready, len(blocks))
                C.next(s_qn)

            def attention(layer, stream, first):
                T = length(stream)
                mg = ModGroups("attn", layer, stream, first)
                kts = range(0 if stream == "main" else SEQ // P, KT_ALL)
                pv0 = C.now(s_st)

                def unnormed(h):
                    b, s = h // 2, slice(h % 2 * HEAD, (h % 2 + 1) * HEAD)
                    act.wait_ge(s_pv, pv0 + (h + 1) * len(kts))
                    r, ps = h % 4 * 32, bank[2 + h % 2]
                    nc.scalar.activation(z[s, Z_Q + b, :T], ps[0:HEAD, :T], ACT.Copy).then_inc(s_on, 1)
                    nc.scalar.activation(scr[r:r + 1, 2 + h // 4, :T], ps[HEAD:HEAD + 1, :T], ACT.Copy)\
                        .then_inc(s_on, 1)

                def shift(h):
                    act.wait_ge(s_mrow, C.next(s_mrow))
                    act.wait_ge(s_q, C.next(s_q, 2))
                    nc.scalar.activation(y_lo[HEAD:HEAD + 1, 6 + h % 2, :T].rearrange("p (a b) -> p a b", b=CTX),
                                         max_rows(stream), ACT.Copy, scale=-1.0).then_inc(s_shift, 1)

                if stream == "main":
                    shift(0)
                for h in range(N_HEADS):
                    if stream == "ctx":
                        shift(h)
                    for n, kt in enumerate(kts):
                        act.wait_ge(s_st, C.next(s_st))
                        k = C.now(s_st) - 1
                        if k >= 2:
                            act.wait_ge(s_p, k - 1)
                        nc.scalar.activation(z[:, 13 + k % 2, :T], bank[k % 2][:, :T], ACT.Exp, scale=HEAD ** -0.5)\
                            .then_inc(s_exp, 1)
                        if k >= 2:
                            act.wait_ge(s_pv, k - 1)
                        nc.scalar.activation(y_hi[:, 4 + k % 2, :T], bank[k % 2][:, :T], ACT.Exp, scale=HEAD ** -0.5)\
                            .then_inc(s_exp, 1)
                        if n == 1 and h:
                            unnormed(h - 1)
                        if stream == "main" and n == len(kts) - 2 and h + 1 < N_HEADS:
                            shift(h + 1)
                    if h:
                        mod_tiles(mg, mg.share(2 * h - 1, 2 * N_HEADS))
                    mod_tiles(mg, mg.share(2 * h, 2 * N_HEADS))
                mod_tiles(mg, mg.share(2 * N_HEADS - 1, 2 * N_HEADS))
                unnormed(N_HEADS - 1)
                C.next(s_on, 2 * N_HEADS)
                upper(4, lambda k: z[:, Z_Q + k, :T], lambda k: y_hi[:, 4 + k, :T])

            def merge(layer, stream, first):
                T = length(stream)

                def body(c, u, off):
                    split(c, off)
                    if u % R == 3:
                        return
                    done(c, off)
                    g = u % R
                    act.wait_ge(post, off + (c - g + R))
                    nc.scalar.activation(scr[:, g, :T], ring[:, c % R, :T], ACT.Sigmoid).then_inc(evac, 1)
                grouped(act, 32, first, body, C)
                upper(KB, lambda k: z[:, k, :T], lambda k: h_hi[:, k, :T])

            def ff(layer, stream, first):
                T = length(stream)

                def body(c, u, off):
                    split(c, off)
                    if u % 16 >= KB:
                        return
                    done(c, off)
                    act.wait_ge(post, off + (c - 1 + R))
                    nc.scalar.activation(scr[:, u % 2, :T], ring[:, c % R, :T], ACT.Relu).then_inc(evac, 1)
                grouped(act, 64, first, body, C, size=16)

            act.wait_ge(s_vec, 16)
            act.wait_ge(consts, 1)
            nc.scalar.activation(c_act[:, :], vec[:, 0:16], ACT.Silu).then_inc(s_silu, 1)
            for t in range(-LEAD, 0):
                split(t)
            lam = vec[:, VCOL["lru_lam"][0]:VCOL["lru_lam"][0] + 4]
            step(nc.scalar.activation(small[:, 0:4], lam, ACT.Abs))
            nc.scalar.activation(small[:, 4:8], small[:, 0:4], ACT.Exp, scale=-1.0).then_inc(s_lam, 1)
            for n, (kind, layer, stream, first) in enumerate(steps):
                if kind == "mod":
                    mg = ModGroups(kind, layer, stream, first)
                    mod_tiles(mg, mg.share(0, 1))
                elif kind == "norm1":
                    norm(layer, stream, first, 0)
                elif kind == "z":
                    z_tiles(layer, stream, first, 13)
                elif kind == "z_kv":
                    z_tiles(layer, stream, first, 0)
                elif kind == "fourier":
                    fourier(layer, stream, first)
                elif kind == "qk":
                    qk(layer, stream, [Z_K] if (layer, stream) == (1, "ctx") else list(range(Z_Q, Z_K + 1)), first)
                    if stream == "main":
                        pass
                elif kind == "attn":
                    attention(layer, stream, first)
                elif kind == "merge":
                    merge(layer, stream, first)
                elif kind == "w_o":
                    for c in range(first, first + KB):
                        split(c)
                elif kind == "norm2":
                    norm(layer, stream, first, 3)
                elif kind == "pre_mix":
                    gain_norm(first, residual=layer > 0)
                elif kind == "pre_ffn":
                    gain_norm(first)
                elif kind in ("post_mix", "post_ffn"):
                    post_norm(first)
                elif kind == "ab_conf":
                    ab_conf(first)
                elif kind == "ab_lru":
                    ab_lru(first)
                elif kind == "lru_gate":
                    lru(first)
                elif kind == "mix_out":
                    mix_out(first)
                elif kind == "ffn":
                    ffn(first)
                elif kind == "ml_qk":
                    ml_qk(first)
                elif kind == "ml_gates":
                    ml_gates(first)
                elif kind == "ml_v":
                    ml_v(first)
                elif kind == "mlstm":
                    mlstm()
                elif kind == "ff":
                    ff(layer, stream, first)

        @block.tensor
        def _(pe):
            C = Counts()

            def three(o, a_hi, a_lo, b_hi, b_lo, start, stop):
                nc.tensor.matmul(o, a_hi, b_hi, start=start, stop=False)
                nc.tensor.matmul(o, a_hi, b_lo, start=False, stop=False)
                return nc.tensor.matmul(o, a_lo, b_hi, start=False, stop=stop)

            def ready(c, off=0):
                pe.wait_ge(w_ready, off + (c + 1))
                pe.wait_ge(post, off + (c + 1))

            def w(c, k, n=P):
                return w_hi[:, c % R, k * n:(k + 1) * n], w_lo[:, c % R, k * n:(k + 1) * n]

            def product(c, T, a_hi, a_lo, blocks=range(KB), o=None, last=True, first_k=0, before=None):
                o = ring[:, c % R, :T] if o is None else o
                for n, k in enumerate(blocks):
                    if before:
                        before(k)
                    m = three(o, *w(c, k), a_hi[:, k, :T], a_lo[:, k, :T], n == 0, n == len(blocks) - 1)
                if last:
                    m.then_inc(tile_done, 1)

            def sums(n, T, lhs, ps):
                for k in range(n):
                    pe.wait_ge(sq_ready, C.next(sq_ready))
                    nc.tensor.matmul(ps(k)[:, :T], lhs, scr[:, k % 2, :T], start=(k == 0), stop=(k == n - 1))\
                        .then_inc(ss_ready, 1)

            def blocks_ready(k0):
                return lambda k: pe.wait_ge(lo_ready, k0 + k + 1)

            def mod_tiles(mg, numbers):
                for i in numbers:
                    g, c = i // 4, mg.first + i
                    pe.wait_ge(w_ready, c + 1)
                    if i == 0:
                        pe.wait_ge(post, c + R)
                        mod0[0] = C.now(s_mod)
                    if i % 4 == 0 and g >= len(mg.free):
                        pe.wait_ge(s_mod, mod0[0] + g - len(mg.free) + 1)
                    o = mg.bank(g)[0:4, :]
                    for r in range(2):
                        a = c_parts[:, 2 * (i % 4) + r, :]
                        hi, lo = w(c, r, SEQ)
                        nc.tensor.matmul(o, a, hi, start=i % 4 == 0 and r == 0, stop=False)
                        m = nc.tensor.matmul(o, a, lo, start=False, stop=i % 4 == 3 and r == 1)
                    m.then_inc(tile_done, 1)
                    if i % 4 == 1 and g:
                        mod_columns(mg, g - 1)
                if len(numbers) and numbers.stop == mg.tiles:
                    mod_columns(mg, mg.n - 1)
                    C.next(s_mod, mg.n)

            def mod_columns(mg, g):
                pe.wait_ge(s_mod_rows, C.next(s_mod_rows))
                for j in range(4):
                    m = nc.tensor.matmul(mg.bank(g)[:, 2 * j:2 * j + 2], mg.rows(g)[:, j * P:(j + 1) * P], pair[:, :],
                                         start=True, stop=True)
                m.then_inc(s_mod_cols, 1)

            mod0 = [0]

            def z_tiles(stream, first, n):
                T = length(stream)
                k0 = C.now(lo_ready)
                C.next(lo_ready, KB)

                def body(c, u, off):
                    ready(c, off)
                    product(c, T, h_hi, h_lo, before=blocks_ready(k0) if u == 0 else None)
                grouped(pe, n, first, body, C)
                c = first + n
                ready(c)
                for tt in range(T // P):
                    s = slice(tt * P, (tt + 1) * P)
                    for k in range(KB):
                        m = three(ring[:, c % R, s], h_hi[:, k, s], h_lo[:, k, s], *w(c, k), k == 0, k == KB - 1)
                m.then_inc(tile_done, 1)

            def fourier(stream, first):
                T = length(stream)
                pe.wait_ge(lo_ready, C.next(lo_ready, 2))
                ready(first)
                for tt in range(T // P):
                    s = slice(tt * P, (tt + 1) * P)
                    for fb in range(2):
                        m = three(bank[tt][:, fb * 256:(fb + 1) * 256], y_hi[:, 2 + fb, s], y_lo[:, 2 + fb, s],
                                  *w(first, 0, 256), True, True)
                m.then_inc(tile_done, 1)
                pe.wait_ge(lo_ready, C.next(lo_ready, T // P))
                per, nkt = TILE // T, T // P
                total = 2 * nkt
                for idx in range(total):
                    c = first + 1 + idx // per
                    cs, kt = divmod(idx, nkt)
                    if idx % per == 0:
                        ready(c)
                    for fb in range(2):
                        a = slice(fb * 256 + cs * P, fb * 256 + (cs + 1) * P)
                        m = three(bank[fb][:, :T], y_hi[:, 4 + kt, a], y_lo[:, 4 + kt, a],
                                  *w(c, idx % per, T), idx == 0, idx == total - 1)
                    if idx % per == per - 1:
                        m.then_inc(tile_done, 1)

            def qk(layer, stream, n_blocks, first):
                T = length(stream)
                mg = ModGroups("qk", layer, stream, first)

                def total(n):
                    pe.wait_ge(sq_ready, C.next(sq_ready))
                    if n >= 2:
                        pe.wait_ge(root_ready, root0 + n - 1)
                    nc.tensor.matmul(bank[n % 2][:, :T], head_ones, scr[:, n % 2, :T], start=True, stop=True)\
                        .then_inc(ss_ready, 1)

                if n_blocks > 1:
                    pe.wait_ge(lo_ready, C.now(lo_ready, 2))
                root0 = C.now(root_ready)
                C.next(root_ready, n_blocks)
                total(0)
                for n in range(n_blocks):
                    if n + 1 < n_blocks:
                        total(n + 1)
                    mod_tiles(mg, mg.share(2 * n, 2 * n_blocks))
                    pe.wait_ge(s_qn, C.next(s_qn))
                    if stream == "main":
                        b = n if n_blocks > 1 else Z_K - Z_Q
                        nc.tensor.matmul(bank[2 + n % 2][:, :T], rot, z[:, Z_Q + b, :T], start=True, stop=True)\
                            .then_inc(s_rot, 1)
                    mod_tiles(mg, mg.share(2 * n + 1, 2 * n_blocks))

            def attention(layer, stream, first):
                T = length(stream)
                mg = ModGroups("attn", layer, stream, first)
                step_banks = 2 if stream == "main" else 1
                pe.wait_ge(post, first + R)
                kts = list(range(0 if stream == "main" else SEQ // P, KT_ALL))
                c0, n_k = kts[0] * P, len(kts) * P
                nq = T // P
                e0, e1 = C.now(s_exp), C.now(s_st)

                def scores(h, qts):
                    g, s = h // 4, 6 + h % 2
                    for qt in qts:
                        if qt == 0:
                            pe.wait_ge(s_q, C.next(s_q, 2))
                        n = C.next(s_score)
                        if n > 2:
                            pe.wait_ge(s_max, n - 2)
                        q = slice(qt * P, (qt + 1) * P)
                        slot = (n - 1) % 2
                        for a in range(0, n_k, SEQ):
                            e = min(a + SEQ, n_k)
                            o = ring[:, step_banks * slot + a // SEQ, 0:e - a]
                            nc.tensor.matmul(o, y_hi[:, s, q], k_pair[:, g, c0 + a:c0 + e], start=True, stop=False)
                            m = nc.tensor.matmul(o, y_lo[0:HEAD, s, q], k_one[0:HEAD, g, c0 + a:c0 + e],
                                                 start=False, stop=True)
                        m.then_inc(s_score, 1)

                def max_row(h):
                    pe.wait_ge(s_max, C.next(s_max, nq))
                    for qt in range(nq):
                        m = nc.tensor.matmul(max_rows(stream)[:, qt // 2, qt % 2 * P:(qt % 2 + 1) * P],
                                             mx[:, h % 2, qt:qt + 1], ident, start=True, stop=True)
                    m.then_inc(s_mrow, 1)

                def score_t(h, n):
                    g, s = h // 4, 6 + h % 2
                    if n == 0:
                        pe.wait_ge(s_shift, C.next(s_shift))
                    k = C.next(s_st) - 1
                    if k >= 2:
                        pe.wait_ge(s_exp, e0 + 2 * (k - e1 - 1))
                    keys = slice(kts[n] * P, (kts[n] + 1) * P)
                    nc.tensor.matmul(bank[k % 2][:, :T], k_pair[:, g, keys], y_hi[:, s, :T], start=True, stop=False)
                    nc.tensor.matmul(bank[k % 2][:, :T], k_one[0:HEAD + 1, g, keys], y_lo[0:HEAD + 1, s, :T],
                                     start=False, stop=True).then_inc(s_st, 1)

                def values(h, n):
                    g = h // 4
                    k = C.next(s_p)
                    pe.wait_ge(s_p, k)
                    if n == 0 and h >= 2:
                        pe.wait_ge(s_on, C.next(s_on, 2))
                    b = 4 + (k - 1) % 2
                    m = three(bank[2 + h % 2][:, :T], v_hi[:, kts[n], g, :], v_lo[:, kts[n], g, :],
                              y_hi[:, b, :T], y_lo[:, b, :T], n == 0, n == len(kts) - 1)
                    m.then_inc(s_pv, 1)

                scores(0, range(nq))
                max_row(0)
                score_t(0, 0)
                score_t(0, 1)
                for h in range(N_HEADS):
                    more = h + 1 < N_HEADS
                    if stream == "ctx":
                        if more:
                            scores(h + 1, range(nq))
                        mod_tiles(mg, mg.share(2 * h, 2 * N_HEADS))
                        values(h, 0)
                        values(h, 1)
                        if more:
                            max_row(h + 1)
                        mod_tiles(mg, mg.share(2 * h + 1, 2 * N_HEADS))
                        if more:
                            score_t(h + 1, 0)
                            score_t(h + 1, 1)
                        continue
                    for n in range(len(kts)):
                        if n + 2 < len(kts):
                            score_t(h, n + 2)
                        elif more:
                            if n + 2 == len(kts):
                                max_row(h + 1)
                            score_t(h + 1, n + 2 - len(kts))
                        if more:
                            scores(h + 1, ((), (0, 1), (2,), (3,), (), ())[n])
                        values(h, n)
                C.next(s_on, 4)
                C.next(s_exp, 2 * N_HEADS * len(kts))
                for b in range(4):
                    if b % 2 == 0:
                        pe.wait_ge(s_recip, C.next(s_recip))
                    for i in range(2):
                        r = (2 * b + i) % 4 * 32
                        m = nc.tensor.matmul(bank[b][i * HEAD:(i + 1) * HEAD, :T],
                                             ident[:, r:r + 1].to_broadcast([P, HEAD]), scr[:, 2 + b // 2, :T],
                                             start=True, stop=True)
                    m.then_inc(s_spread, 1)

            def merge(stream, first):
                T = length(stream)
                y_all = C.next(lo_ready, 2 + 2 + 4)

                def body(c, u, off):
                    ready(c, off)
                    if u % R < 3:
                        product(c, T, h_hi, h_lo)
                        return
                    pe.wait_ge(lo_ready, y_all)
                    product(c, T, y_hi, y_lo, range(0, 2), last=False)
                    product(c, T, y_hi, y_lo, range(2, 4), o=bank[0][:, :T], last=False)
                    product(c, T, y_hi, y_lo, range(4, 8), o=bank[1][:, :T])
                grouped(pe, 32, first, body, C)

            def w_o(T, first):
                k0 = C.now(lo_ready)
                C.next(lo_ready, KB)

                def body(c, u, off):
                    ready(c, off)
                    product(c, T, h_hi, h_lo, before=blocks_ready(k0) if u == 0 else None)
                grouped(pe, KB, first, body, C)

            def ff(stream, first):
                T = length(stream)
                k0 = C.now(lo_ready)
                C.next(lo_ready, KB)

                def body(c, u, off):
                    ready(c, off)
                    if u % 16 < KB:
                        product(c, T, h_hi, h_lo, before=blocks_ready(k0) if u % 16 == 0 else None)
                    else:
                        def hidden(k):
                            if u % 16 == KB and k > KB - R:
                                pe.wait_ge(post, off + (c - KB + k + 1 + R))
                        product(c, T, y_hi, y_lo, before=hidden)
                grouped(pe, 64, first, body, C, size=16)

            def plain(n, first, a_hi, a_lo, split_first=KB):
                k0 = C.now(lo_ready)
                C.next(lo_ready, split_first)

                def body(c, u, off):
                    ready(c, off)
                    product(c, SEQ, a_hi, a_lo, before=blocks_ready(k0) if u == 0 and split_first else None)
                grouped(pe, n, first, body, C)

            def lru(first):
                for b in range(4):
                    pe.wait_ge(s_conv, C.next(s_conv))
                    nc.tensor.matmul(bank[0][:, :], ones, z[:, 4 + b, :], start=b == 0, stop=b == 3)\
                        .then_inc(ss_ready, 1)
                pe.wait_ge(root_ready, C.next(root_ready))
                sums(4, SEQ, ones, lambda k: bank[0])
                C.next(root_ready)
                pe.wait_ge(lo_ready, C.next(lo_ready, 4))
                ready(first)
                for b in range(4):
                    if b:
                        pe.wait_ge(s_gread, C.next(s_gread, 2))
                    for i in range(2):
                        m = three(bank[2 + i][:, :], *w(first, 4 * i + b), y_hi[:, 4 + b, :], y_lo[:, 4 + b, :],
                                  True, True)
                    m.then_inc(s_gate, 1)
                pe.wait_ge(s_gread, C.next(s_gread, 2))
                pe.sem_inc(tile_done, 1)

            def ffn(first):
                k0 = C.now(lo_ready)
                C.next(lo_ready, KB)

                def body(c, u, off):
                    pos, n = (u % 24, 8) if u < 48 else (u - 48, 6)
                    ready(c, off)
                    if pos < 2 * n:
                        product(c, SEQ, h_hi, h_lo, before=blocks_ready(k0) if u == 0 else None)
                        return

                    def hidden(k):
                        if pos == 2 * n and k >= n - 2:
                            pe.wait_ge(post, off + (c - 2 * (n - k) + 2 + R))
                    product(c, SEQ, y_hi, y_lo, range(n), before=hidden)
                grouped(pe, FFN_TILES, first, body, C, size=24)

            def ml_v(first):
                pe.wait_ge(s_bv, 16)
                for half in range(2):
                    if half:
                        pe.wait_ge(lo_ready, C.next(lo_ready, 4))
                    for n in range(4):
                        c = first + 4 * half + n
                        ready(c)
                        for tt in range(4):
                            s = slice(tt * P, (tt + 1) * P)
                            if n == 0:
                                nc.tensor.matmul(bank[tt][:, :], ones[0:1, :], xv[0:1, half, :], start=True, stop=False)
                            for r in range(2):
                                m = three(bank[tt][:, :], h_hi[:, 2 * n + r, s], h_lo[:, 2 * n + r, s],
                                          *w(c, r, SEQ), False, n == 3 and r == 1)
                        m.then_inc(tile_done, 1)

            def mlstm(first):
                pe.wait_ge(lo_ready, C.next(lo_ready, 4))
                pe.wait_ge(post, first + R)
                pe.wait_ge(s_row, C.next(s_row, 2))
                for tt in range(4):
                    m = nc.tensor.matmul(bank[0][:, tt * 8:tt * 8 + 8], xv[0:8, 3, tt * P:(tt + 1) * P],
                                         ident[0:8, 0:8], start=True, stop=True)
                m.then_inc(s_col, 1)
                pe.wait_ge(s_col, C.next(s_col, 2))

                def spread(h):
                    if h >= 2:
                        pe.wait_ge(s_thr, C.next(s_thr))
                    for i in range(2):
                        m = nc.tensor.matmul(bank[2 * (h % 2) + i][:, :],
                                             ident[gate_rows, 32 + h:33 + h].to_broadcast([8, P]), row[i], start=True, stop=True)
                    m.then_inc(s_bc, 1)

                def score_t(h, n):
                    b = 4 * (h % 2)
                    if n == 0:
                        pe.wait_ge(s_q, C.next(s_q))
                    k = C.next(s_st) - st0 - 1
                    if k >= 2:
                        pe.wait_ge(s_p, p0 + k - 1)
                    keys, o = slice(n * P, (n + 1) * P), ring[:, k % 2, n * P:]
                    nc.tensor.matmul(o, kv[:, b + 2, keys], kv[:, b, n * P:], start=True, stop=False)
                    nc.tensor.matmul(o, kv[0:HEAD, b + 3, keys], kv[0:HEAD, b + 1, n * P:], start=False, stop=True)\
                        .then_inc(s_st, 1)

                def values(h, n):
                    k = C.next(s_p)
                    pe.wait_ge(s_p, k)
                    if n == 0 and h:
                        pe.wait_ge(s_on, C.next(s_on))
                    b = 8 + 2 * ((k - p0 - 1) % 2)
                    vb, vc = 2 * n + h // 4, slice(h % 4 * P, (h % 4 + 1) * P)
                    j = slice(n * P, SEQ)
                    three(ring[:, 2, j], y_hi[:, vb, vc], y_lo[:, vb, vc], kv[:, b, j], kv[:, b + 1, j], n == 0, n == 3)
                    nc.tensor.matmul(ring[:, 3, j], ones_r[:, :], kv[:, b, j], start=n == 0, stop=False)
                    nc.tensor.matmul(ring[:, 3, j], ones_r[:, :], kv[:, b + 1, j], start=False, stop=n == 3)\
                        .then_inc(s_pv, 1)

                st0, p0 = C.now(s_st), C.now(s_p)
                spread(0)
                for h in range(N_HEADS):
                    score_t(h, 0)
                    score_t(h, 1)
                    if h + 1 < N_HEADS:
                        spread(h + 1)
                    for n in range(4):
                        values(h, n)
                        if n + 2 < 4:
                            score_t(h, n + 2)
                C.next(s_thr, 2)
                C.next(s_on)

                def total(n):
                    pe.wait_ge(sq_ready, C.next(sq_ready))
                    if n >= 2:
                        pe.wait_ge(root_ready, root0 + n - 1)
                    nc.tensor.matmul(bank[n % 2][:, :], ones, scr[:, n % 2, :], start=True, stop=True)\
                        .then_inc(ss_ready, 1)

                root0 = C.now(root_ready)
                C.next(root_ready, N_HEADS)
                for n in range(N_HEADS):
                    total(n)
                C.next(s_qn, N_HEADS)

            pe.sem_inc(tile_done, R)
            pe.wait_ge(s_mat, 16)
            pe.wait_ge(lo_ready, C.next(lo_ready))
            pe.wait_ge(consts, 2)
            for kind, layer, stream, first in steps:
                if kind == "mod":
                    mg = ModGroups(kind, layer, stream, first)
                    mod_tiles(mg, mg.share(0, 1))
                elif kind in ("norm1", "norm2"):
                    sums(KB, length(stream), ones, lambda k: bank[0])
                    C.next(root_ready)
                elif kind == "z":
                    z_tiles(stream, first, 13)
                elif kind == "z_kv":
                    z_tiles(stream, first, 1)
                elif kind == "fourier":
                    fourier(stream, first)
                elif kind == "conv":
                    pass
                elif kind == "qk":
                    qk(layer, stream, 1 if (layer, stream) == (1, "ctx") else 5, first)
                elif kind == "attn":
                    attention(layer, stream, first)
                elif kind == "merge":
                    merge(stream, first)
                elif kind == "w_o":
                    w_o(length(stream), first)
                elif kind in ("pre_mix", "pre_ffn", "post_mix", "post_ffn"):
                    sums(KB, SEQ, ones, lambda k: bank[0])
                    C.next(root_ready)
                elif kind == "ab_conf":
                    plain(8, first, h_hi, h_lo)
                elif kind == "ab_lru":
                    plain(8, first, h_hi, h_lo, 0)
                elif kind == "lru_gate":
                    lru(first)
                elif kind == "mix_out":
                    plain(8, first, *((h_hi, h_lo) if layer else (y_hi, y_lo)))
                elif kind == "ffn":
                    ffn(first)
                elif kind == "ml_qk":
                    plain(8, first, h_hi, h_lo)
                    plain(8, first + 8, h_hi, h_lo, 0)
                elif kind == "ml_gates":
                    plain(1, first, h_hi, h_lo, 0)
                elif kind == "ml_v":
                    ml_v(first)
                elif kind == "mlstm":
                    mlstm(first)
                elif kind == "ff":
                    ff(stream, first)

        @block.vector
        def _(dve):
            C = Counts()

            def step(ins, sem=dve_own):
                ins.then_inc(sem, 1)
                dve.wait_ge(sem, C.next(sem))

            def posted():
                dve.sem_inc(post, 1)
                C.next(post)

            def done(c, off=0):
                dve.wait_ge(tile_done, off + (c + 1 + R))

            def f(ap):
                return ap.bitcast(F32)

            def lower(n, src, dst, hi, bias=None, before=None):
                if before:
                    before(0)
                for k in range(n):
                    if before and k + 1 < n:
                        before(k + 1)
                    dve.wait_ge(hi_ready, C.next(hi_ready))
                    step(nc.vector.scalar_tensor_tensor(dst(k), src(k), bias(k) if bias else 0.0, f(hi(k)),
                                                   ALU.add, ALU.subtract), lo_ready)

            def both(src, hi, lo):
                step(nc.vector.tensor_copy(hi, src))
                step(nc.vector.tensor_tensor(lo, src, f(hi), ALU.subtract), lo_ready)

            def norm(layer, stream, part):
                T, src, s = length(stream), x_of(stream), int(stream == "ctx")
                dve.wait_ge(root_ready, C.next(root_ready))
                step(nc.vector.reciprocal(scr[:, 3, :T], scr[:, 2, :T]))

                def scaled(k):
                    step(nc.vector.scalar_tensor_tensor(scr[:, k % 2, :T], src[:, k, :T],
                                                   gain[:, layer, part // 3, s, k:k + 1], scr[:, 3, :T],
                                                   ALU.mult, ALU.mult), t_ready)
                lower(KB, lambda k: scr[:, k % 2, :T], lambda k: h_lo[:, k, :T], lambda k: h_hi[:, k, :T],
                      lambda k: mod[:, layer, part * KB + k, s:s + 1], before=scaled)

            def mod_store(mg, tiles):
                if not mg.n:
                    return
                last = tiles >= mg.tiles
                while mg.stored < mg.n and (last or 4 * mg.stored + 5 < tiles):
                    g = mg.stored
                    dve.wait_ge(s_mod_cols, C.next(s_mod_cols))
                    b0 = VCOL[f"b_mod{mg.layer}"][0] + 4 * (mg.g0 + g)
                    o = mod[:, mg.layer, 4 * (mg.g0 + g):4 * (mg.g0 + g) + 4, :]
                    step(nc.vector.tensor_tensor(o, mg.bank(g)[:, 0:8].rearrange("p (j s) -> p j s", s=2),
                                                 vec[:, b0:b0 + 4].rearrange("p (j o) -> p j o", o=1).to_broadcast([P, 4, 2]),
                                                 ALU.add), s_mod)
                    mg.stored += 1
                if last:
                    dve.sem_inc(post, mg.tiles)
                    C.next(post, mg.tiles)
                    end = mg.g0 + mg.n
                    for half in range(2):
                        if not mg.g0 < 4 + 6 * half <= end:
                            continue
                        for s in range(2):
                            sc = (3 * half + 1) * KB
                            g = VCOL[f"g{half + 1}_{mg.layer}"][0]
                            step(nc.vector.scalar_tensor_tensor(gain[:, mg.layer, half, s, :],
                                                                mod[:, mg.layer, sc:sc + KB, s],
                                                                1.0, vec[:, g:g + KB], ALU.add, ALU.mult))

            def z_tiles(stream, first, n):
                T = length(stream)

                def body(c, u, off):
                    dve.wait_ge(evac, C.next(evac))
                    posted()
                grouped(dve, n, first, body, C, {evac: R, post: R})
                c = first + n
                kt = 0 if stream == "main" else SEQ // P
                dve.wait_ge(evac, C.next(evac))
                step(nc.vector.tensor_tensor(v_lo[:, kt:kt + T // P, :, 0:HEAD].rearrange("p k g d -> p (k g) d"),
                                        ring[:, c % R, :T].rearrange("p (k d) -> p k d", d=HEAD),
                                        f(v_hi[:, kt:kt + T // P, :, 0:HEAD].rearrange("p k g d -> p (k g) d")),
                                        ALU.subtract), post)

            def fourier(stream, first):
                T = length(stream)
                for fb in range(2):
                    both(z[:, Z_F + fb, :T], y_hi[:, 2 + fb, :T], y_lo[:, 2 + fb, :T])
                for tt in range(T // P):
                    dve.wait_ge(hi_ready, C.next(hi_ready))
                    step(nc.vector.tensor_tensor(y_lo[:, 4 + tt, :], bank[tt][:, :], f(y_hi[:, 4 + tt, :]),
                                            ALU.subtract), lo_ready)
                posted()
                n = 4 if T == SEQ else 1
                for c in range(first + 1, first + 1 + n):
                    done(c)
                    posted()
                for fb in range(2):
                    dve.wait_ge(hi_ready, C.next(hi_ready))
                    step(nc.vector.tensor_tensor(y_lo[:, 2 + fb, :T], bank[fb][:, :T], f(y_hi[:, 2 + fb, :T]),
                                            ALU.subtract), lo_ready)

            def conv(layer, stream):
                T = length(stream)
                for b in range(2):
                    step(nc.vector.tensor_tensor(z[:, Z_C + b, :T], z[:, Z_C + b, :T], z[:, Z_X + b, :T], ALU.mult))
                wv = lambda j, b: v(f"w_conv{layer}", 2 * j + b)
                for b in range(2):
                    step(nc.vector.tensor_scalar(scr[:, b, :T], z[:, Z_C + b, :T], wv(1, b), None, ALU.mult))
                for b in range(2):
                    step(nc.vector.scalar_tensor_tensor(scr[:, b, 1:T], z[:, Z_C + b, 0:T - 1], wv(0, b),
                                                       scr[:, b, 1:T], ALU.mult, ALU.add))
                for b in range(2):
                    step(nc.vector.scalar_tensor_tensor(scr[:, b, 0:T - 1], z[:, Z_C + b, 1:T], wv(2, b),
                                                       scr[:, b, 0:T - 1], ALU.mult, ALU.add))
                for b in range(2):
                    step(nc.vector.tensor_tensor(scr[:, b, :T], scr[:, b, :T], z[:, Z_B + b, :T], ALU.mult))
                for b in range(2):
                    both(scr[:, b, :T], y_hi[:, b, :T], y_lo[:, b, :T])
                dve.sem_inc(s_free, 1)

            def qk(layer, stream, blocks, first):
                T = length(stream)
                mg = ModGroups("qk", layer, stream, first)
                if stream == "main":
                    dve.wait_ge(s_rope, C.next(s_rope, 16))
                for n, b in enumerate(blocks):
                    g = v(f"gk{layer}" if b == Z_K else f"gq{layer}")
                    dve.wait_ge(root_ready, C.next(root_ready))
                    step(nc.vector.reciprocal(scr[:, 3, :T], scr[:, 2, :T]))
                    step(nc.vector.scalar_tensor_tensor(z[:, b, :T], z[:, b, :T], g, scr[:, 3, :T],
                                                   ALU.mult, ALU.mult), s_qn)
                    if stream == "main":
                        dve.wait_ge(s_rot, C.next(s_rot))
                        step(nc.vector.tensor_tensor(z[:, 13, :T], bank[2 + n % 2][:, :T], z[:, 15, :T], ALU.mult))
                        step(nc.vector.tensor_tensor(z[:, b, :T], z[:, b, :T], z[:, 14, :T], ALU.mult))
                        step(nc.vector.tensor_tensor(z[:, b, :T], z[:, b, :T], z[:, 13, :T], ALU.add))
                    if n + 1 < len(blocks):
                        mod_store(mg, mg.share(2 * n, 2 * len(blocks)).stop)
                c0 = 0 if stream == "main" else SEQ
                cols = slice(c0, c0 + T)
                step(nc.vector.tensor_copy(y_hi[:, 4, :T], z[:, Z_K, :T]))
                step(nc.vector.tensor_tensor(y_lo[:, 4, :T], z[:, Z_K, :T], f(y_hi[:, 4, :T]), ALU.subtract))
                for g in range(2):
                    s = slice(g * HEAD, (g + 1) * HEAD)
                    step(nc.vector.tensor_copy(k_pair[0:HEAD, g, cols], f(y_hi[s, 4, :T])))
                    step(nc.vector.tensor_copy(k_one[0:HEAD, g, cols], f(y_hi[s, 4, :T])))
                    step(nc.vector.tensor_copy(k_pair[HEAD:P, g, cols], f(y_lo[s, 4, :T])))
                mod_store(mg, mg.tiles)

            def attention(layer, stream, first):
                T = length(stream)
                mg = ModGroups("attn", layer, stream, first)
                step_banks = 2 if stream == "main" else 1
                n_kt = KT_ALL if stream == "main" else CTX // P
                nq = T // P

                q_own = [0]

                def queries(h):
                    b, s = h // 2, slice(h % 2 * HEAD, (h % 2 + 1) * HEAD)
                    nc.vector.tensor_copy(y_hi[s, 6 + h % 2, :T], z[s, Z_Q + b, :T]).then_inc(dve_own, 1)
                    q_own[0] = C.next(dve_own)

                def query_parts(h):
                    b, s = h // 2, slice(h % 2 * HEAD, (h % 2 + 1) * HEAD)
                    other, slot = slice(HEAD - h % 2 * HEAD, P - h % 2 * HEAD), 6 + h % 2
                    dve.wait_ge(dve_own, q_own[0])
                    nc.vector.tensor_copy(y_hi[other, slot, :T], f(y_hi[s, slot, :T])).then_inc(s_q, 1)
                    nc.vector.tensor_tensor(y_lo[0:HEAD, slot, :T], z[s, Z_Q + b, :T], f(y_hi[s, slot, :T]),
                                            ALU.subtract).then_inc(s_q, 1)
                    C.next(s_q, 2)

                def maxima(h, qts):
                    for qt in qts:
                        n = C.next(s_score)
                        dve.wait_ge(s_score, n)
                        slot = (n - 1) % 2
                        view = ring[:, step_banks * slot:step_banks * (slot + 1), :].rearrange("p a b -> p (a b)")
                        view = view[:, 0:n_kt * P]
                        nc.vector.reduce_max(mx[:, h % 2, qt:qt + 1], view, AX_X).then_inc(s_max, 1)
                        C.next(s_max)

                def parts():
                    dve.wait_ge(s_exp, C.next(s_exp, 2))
                    k = C.next(s_p)
                    if k > 2:
                        dve.wait_ge(s_pv, k - 2)
                    src, b = z[:, 13 + (k - 1) % 2, :T], 4 + (k - 1) % 2
                    nc.vector.tensor_tensor(y_lo[:, b, :T], src, f(y_hi[:, b, :T]), ALU.subtract).then_inc(s_p, 1)

                def reciprocals(half):
                    dve.wait_ge(s_on, C.next(s_on, 8))
                    step(nc.vector.reciprocal(scr[:, 2 + half, :T], scr[:, 2 + half, :T]), s_recip)

                step(nc.vector.memset(scr[:, 2:4, :], 1.0))
                queries(0)
                query_parts(0)
                maxima(0, range(nq))
                for h in range(N_HEADS):
                    if h + 1 < N_HEADS:
                        queries(h + 1)
                    parts()
                    if h + 1 < N_HEADS:
                        query_parts(h + 1)
                    parts()
                    if h + 1 < N_HEADS:
                        maxima(h + 1, (0,) if n_kt > 2 else range(nq))
                    for n in range(2, n_kt):
                        parts()
                        if h + 1 < N_HEADS:
                            maxima(h + 1, ((1, 2), (3,), (), ())[n - 2])
                    if h == 5:
                        reciprocals(0)
                    if h + 1 < N_HEADS:
                        mod_store(mg, mg.share(2 * h, 2 * N_HEADS).stop)
                reciprocals(1)
                mod_store(mg, mg.tiles)
                C.next(s_st, N_HEADS * n_kt)
                C.next(s_pv, N_HEADS * n_kt)

                def normed(b):
                    dve.wait_ge(s_spread, C.next(s_spread))
                    step(nc.vector.tensor_tensor(z[:, Z_Q + b, :T], z[:, Z_Q + b, :T], bank[b][:, :T], ALU.mult),
                         t_ready)
                lower(4, lambda k: z[:, Z_Q + k, :T], lambda k: y_lo[:, 4 + k, :T], lambda k: y_hi[:, 4 + k, :T],
                      before=normed)

            def merge(stream, first):
                T = length(stream)

                def body(c, u, off):
                    if u % R < 3:
                        dve.wait_ge(evac, C.next(evac))
                        posted()
                        return
                    done(c, off)
                    for g, ps in enumerate((ring[:, c % R, :T], bank[0][:, :T], bank[1][:, :T])):
                        step(nc.vector.tensor_tensor(scr[:, g, :T], ps, scr[:, g, :T], ALU.mult))
                    step(nc.vector.tensor_tensor(scr[:, 0, :T], scr[:, 0, :T], scr[:, 1, :T], ALU.add))
                    m = u // R
                    o = z[:, m, :T] if isinstance(off, int) else at(z[:, :, :T], m, turn[0])
                    step(nc.vector.tensor_tensor(o, scr[:, 0, :T], scr[:, 2, :T], ALU.add), post)
                grouped(dve, 32, first, body, C, {evac: 3, dve_own: 4, post: R})
                dve.sem_inc(t_ready, KB)
                C.next(t_ready, KB)
                lower(KB, lambda k: z[:, k, :T], lambda k: h_lo[:, k, :T], lambda k: h_hi[:, k, :T])

            def residual(c, m, off, m_off, layer, stream, part):
                T, xs, s = length(stream), x_of(stream), int(stream == "ctx")
                done(c, off)
                g = part * KB + m
                g = mod[:, layer, g, s:s + 1] if isinstance(m_off, int) else \
                    mod[:, layer, bass.ds(m_off + g, 1), s:s + 1].rearrange("p o n -> p (o n)")
                o = at(xs[:, :, :T], m, m_off)
                return nc.vector.scalar_tensor_tensor(o, ring[:, c % R, :T], g, o, ALU.mult, ALU.add)

            def w_o(layer, stream, first):
                def body(c, u, off):
                    step(residual(c, u, off, off, layer, stream, 2), post)
                grouped(dve, KB, first, body, C, {post: R})

            def ff(layer, stream, first):
                T = length(stream)

                def body(c, u, off):
                    m = u % 16
                    if m < KB:
                        dve.wait_ge(evac, C.next(evac))
                        step(nc.vector.tensor_tensor(z[:, m % 2, :T], scr[:, m % 2, :T], scr[:, m % 2, :T], ALU.mult))
                        step(nc.vector.tensor_copy(y_hi[:, m, :T], z[:, m % 2, :T]))
                        step(nc.vector.tensor_tensor(y_lo[:, m, :T], z[:, m % 2, :T], f(y_hi[:, m, :T]),
                                                ALU.subtract), post)
                    else:
                        step(residual(c, m - KB, off, 0, layer, stream, 5), post)
                grouped(dve, 64, first, body, C, {evac: KB, dve_own: 2 * KB, post: 2 * KB}, size=16)

            def rms(part_gain, n=KB):
                dve.wait_ge(root_ready, C.next(root_ready))
                step(nc.vector.reciprocal(scr[:, 3, :], scr[:, 2, :]))

                def scaled(k):
                    step(nc.vector.scalar_tensor_tensor(scr[:, k % 2, :], x[:, k, :], part_gain(k), scr[:, 3, :],
                                                        ALU.mult, ALU.mult), t_ready)
                lower(n, lambda k: scr[:, k % 2, :], lambda k: h_lo[:, k, :], lambda k: h_hi[:, k, :], before=scaled)

            def post_norm(gain_of):
                dve.wait_ge(root_ready, C.next(root_ready))
                step(nc.vector.reciprocal(scr[:, 3, :], scr[:, 2, :]))
                for k in range(KB):
                    step(nc.vector.scalar_tensor_tensor(z[:, k, :], z[:, k, :], gain_of(k), scr[:, 3, :],
                                                        ALU.mult, ALU.mult))
                    step(nc.vector.tensor_tensor(x[:, k, :], x[:, k, :], z[:, k, :], ALU.add))
                dve.sem_inc(s_x, 1)

            def passed(n, first):
                def body(c, u, off):
                    dve.wait_ge(evac, C.next(evac))
                    posted()
                grouped(dve, n, first, body, C, {evac: R, post: R})

            def ab_conf(first):
                for n in range(8):
                    dve.wait_ge(evac, C.next(evac))
                    if n % 2 == 0:
                        posted()
                    else:
                        b = n // 2
                        step(nc.vector.tensor_tensor(z[:, b, :], z[:, b, :], scr[:, b % 2, :], ALU.mult), post)

            def ab_lru(first):
                width = 31
                n = 0
                for b in range(4):
                    o = z[:, 4 + b, :]
                    for j in range(width - 1, -1, -1):
                        w_col = v("conf_w", 4 * j + b)
                        back = width - 1 - j
                        if back == 0:
                            ins = nc.vector.tensor_scalar(o, z[:, b, :], w_col, v("conf_b", b), ALU.mult, ALU.add)
                        else:
                            ins = nc.vector.scalar_tensor_tensor(o[:, back:], z[:, b, 0:SEQ - back], w_col, o[:, back:],
                                                                 ALU.mult, ALU.add)
                        step(ins, s_conv if j == 0 else dve_own)
                        if j % 8 == 0 and n < 8:
                            n += 1
                            dve.wait_ge(evac, C.next(evac))
                            posted()
                assert n == 8

            def lru(first):
                for b in range(4):
                    o = xv[:, b, :]
                    for back in range(4):
                        w_col = v("lru_w", 4 * (3 - back) + b)
                        if back == 0:
                            step(nc.vector.tensor_scalar(o, z[:, 8 + b, :], w_col, v("lru_b", b), ALU.mult, ALU.add))
                        else:
                            step(nc.vector.scalar_tensor_tensor(o[:, back:], z[:, 8 + b, 0:SEQ - back], w_col,
                                                                o[:, back:], ALU.mult, ALU.add))
                    both(o, y_hi[:, 4 + b, :], y_lo[:, 4 + b, :])
                dve.wait_ge(root_ready, C.next(root_ready))
                for b in range(4):
                    step(nc.vector.tensor_tensor(z[:, 4 + b, :], z[:, 4 + b, :], scr[:, 2, :], ALU.subtract), t_ready)
                dve.wait_ge(root_ready, C.next(root_ready))
                step(nc.vector.reciprocal(scr[:, 3, :], scr[:, 2, :]))
                for b in range(4):
                    step(nc.vector.scalar_tensor_tensor(z[:, 4 + b, :], z[:, 4 + b, :], v("ln_g", b), scr[:, 3, :],
                                                        ALU.mult, ALU.mult), t_ready)
                for b in range(4):
                    dve.wait_ge(s_act, C.next(s_act))
                    both(z[:, 4 + b, :], y_hi[:, b, :], y_lo[:, b, :])
                dve.sem_inc(s_free, 1)
                for b in range(4):
                    dve.wait_ge(s_act, C.next(s_act))
                    step(nc.vector.tensor_scalar(z[:, 4 + b, :], scr[:, b, :], -1.0, 1.0, ALU.mult, ALU.add))
                    step(nc.vector.reciprocal(z[:, 4 + b, :], z[:, 4 + b, :]))
                    step(nc.vector.scalar_tensor_tensor(scr[:, b, :], scr[:, b, :], -2.0, z[:, 4 + b, :],
                                                        ALU.mult, ALU.mult), t_ready)
                dve.wait_ge(s_act, C.next(s_act, 4))
                for b in range(4):
                    step(nc.vector.tensor_tensor(z[:, b, :], z[:, b, :], xv[:, b, :], ALU.mult))
                    dve.wait_ge(s_act, C.next(s_act))
                    step(nc.vector.tensor_tensor(z[:, b, :], z[:, b, :], scr[:, b, :], ALU.mult))
                    step(nc.vector.tensor_tensor_scan(xv[:, b, :], z[:, 8 + b, :], z[:, b, :], 0.0, ALU.mult, ALU.add))
                    step(nc.vector.tensor_tensor(xv[:, b, :], xv[:, b, :], z[:, 12 + b, :], ALU.mult))
                    if b == 0:
                        done(first)
                    both(xv[:, b, :], y_hi[:, 4 + b, :], y_lo[:, 4 + b, :])
                posted()

            def ffn(first):
                step(nc.vector.memset(z[:, 0:KB, :], 0.0))

                def body(c, u, off):
                    pos, n = (u % 24, 8) if u < 48 else (u - 48, 6)
                    if pos < 2 * n:
                        if pos % 2 == 0:
                            dve.wait_ge(evac, C.next(evac))
                            posted()
                            return
                        m = pos // 2
                        done(c, off)
                        step(nc.vector.tensor_tensor(z[:, 8 + m % 2, :], ring[:, c % R, :], scr[:, m % 2, :], ALU.mult))
                        step(nc.vector.tensor_copy(y_hi[:, m, :], z[:, 8 + m % 2, :]))
                        step(nc.vector.tensor_tensor(y_lo[:, m, :], z[:, 8 + m % 2, :], f(y_hi[:, m, :]),
                                                     ALU.subtract), post)
                    else:
                        m = pos - 2 * n
                        done(c, off)
                        step(nc.vector.tensor_tensor(z[:, m, :], z[:, m, :], ring[:, c % R, :], ALU.add), post)
                grouped(dve, FFN_TILES, first, body, C, {evac: 8, dve_own: 16, post: 24}, size=24)

            def ml_gates(first):
                dve.wait_ge(evac, C.next(evac))
                posted()
                dve.sem_inc(s_row, 1)
                dve.wait_ge(s_act, C.next(s_act))
                g, low, run = scr[0:8, 0, :], scr[32:40, :, :], xv[0:8, 2, :]
                step(nc.vector.memset(scr[0:8, 3, :], 0.0))
                step(nc.vector.scalar_tensor_tensor(scr[0:8, 2, :], low[:, 0, :], 0.0, low[:, 1, :],
                                                    ALU.min, ALU.subtract))
                step(nc.vector.tensor_tensor_scan(run, scr[0:8, 2, :], scr[0:8, 3, :], 0.0, ALU.add, ALU.add))
                step(nc.vector.tensor_tensor(xv[0:8, 3, :], g, run, ALU.subtract))
                step(nc.vector.tensor_tensor_scan(scr[0:8, 2, :], scr[0:8, 3, :], xv[0:8, 3, :], 0.0, ALU.add, ALU.max))
                step(nc.vector.tensor_scalar(row[0], scr[0:8, 2, :], -1.0, None, ALU.mult))
                step(nc.vector.scalar_tensor_tensor(row[1], scr[0:8, 2, :], -1.0, run, ALU.mult, ALU.subtract))
                dve.sem_inc(s_row, 1)

            def ml_v(first):
                for half in range(2):
                    for tt in range(4):
                        dve.wait_ge(hi_ready, C.next(hi_ready))
                        b = 2 * tt + half
                        step(nc.vector.tensor_tensor(y_lo[:, b, :], bank[tt][:, :], f(y_hi[:, b, :]), ALU.subtract),
                             lo_ready)
                    for n in range(4):
                        posted()

            def mlstm():
                dve.wait_ge(s_col, C.next(s_col))
                step(nc.vector.tensor_copy(small[:, 0:32], bank[0][:, 0:32]), s_col)

                def queries_keys(h):
                    b, lo0 = 4 * (h % 2), h % 2 * HEAD
                    s, other = slice(lo0, lo0 + HEAD), slice(HEAD - lo0, P - lo0)
                    q, k = z[s, h // 2, :], z[s, 4 + h // 2, :]
                    step(nc.vector.tensor_copy(kv[s, b, :], q))
                    step(nc.vector.tensor_copy(kv[other, b, :], f(kv[s, b, :])))
                    step(nc.vector.tensor_tensor(kv[0:HEAD, b + 1, :], q, f(kv[s, b, :]), ALU.subtract))
                    step(nc.vector.tensor_scalar(kv[s, b + 2, :], k, HEAD ** -0.5, None, ALU.mult))
                    step(nc.vector.scalar_tensor_tensor(kv[other, b + 2, :], k, HEAD ** -0.5, f(kv[s, b + 2, :]),
                                                        ALU.mult, ALU.subtract))
                    step(nc.vector.tensor_copy(kv[0:HEAD, b + 3, :], f(kv[s, b + 2, :])), s_q)

                def diagonal(h, n):
                    if n == 0:
                        dve.wait_ge(s_act, C.next(s_act))
                    j = slice(n * P, (n + 1) * P)
                    step(nc.vector.tensor_tensor(scr[:, n % 2, j], xv[:, h % 2, j], causal, ALU.add), s_diag)

                def parts(h, n):
                    dve.wait_ge(s_exp, C.next(s_exp))
                    dve.wait_ge(s_st, C.next(s_st))
                    j = slice(n * P, SEQ)
                    k = C.now(s_st) - st0
                    step(nc.vector.tensor_tensor(scr[:, 2, j], ring[:, (k - 1) % 2, j], scr[:, n % 2, j], ALU.mult))
                    if k > 2:
                        dve.wait_ge(s_pv, pv0 + k - 2)
                    b = 8 + 2 * ((k - 1) % 2)
                    step(nc.vector.tensor_copy(kv[:, b, j], scr[:, 2, j]))
                    step(nc.vector.tensor_tensor(kv[:, b + 1, j], scr[:, 2, j], f(kv[:, b, j]), ALU.subtract), s_p)

                st0, pv0 = C.now(s_st), C.now(s_pv)
                queries_keys(0)
                for h in range(N_HEADS):
                    diagonal(h, 0)
                    diagonal(h, 1)
                    if h + 1 < N_HEADS:
                        queries_keys(h + 1)
                    for n in range(4):
                        parts(h, n)
                        if n + 2 < 4:
                            diagonal(h, n + 2)
                    dve.wait_ge(s_pv, C.next(s_pv, 4))
                    dve.wait_ge(s_thr, C.next(s_thr))
                    step(nc.vector.tensor_tensor(scr[:, 3, :], ring[:, 3, :], scr[:, 3, :], ALU.max))
                    step(nc.vector.scalar_tensor_tensor(scr[:, 3, :], ring[:, 3, :], -1.0, scr[:, 3, :],
                                                        ALU.mult, ALU.max))
                    step(nc.vector.reciprocal(scr[:, 3, :], scr[:, 3, :]))
                    step(nc.vector.tensor_tensor(head_out(h), ring[:, 2, :], scr[:, 3, :], ALU.mult), s_on)
                for h in range(N_HEADS):
                    dve.wait_ge(root_ready, C.next(root_ready))
                    step(nc.vector.reciprocal(scr[:, 3, :], scr[:, 2, :]))
                    step(nc.vector.scalar_tensor_tensor(head_out(h), head_out(h), v("head_g", h), scr[:, 3, :],
                                                        ALU.mult, ALU.mult), s_qn)
                    step(nc.vector.tensor_tensor(head_out(h), head_out(h), z[:, 8 + h, :], ALU.mult))
                    both(head_out(h), h_hi[:, h, :], h_lo[:, h, :])

            dve.sem_inc(post, R)
            C.next(post, R)
            step(nc.vector.memset(eps[:, :], EPS), consts)
            step(nc.vector.memset(f(k_one[HEAD:HEAD + 1, :, :]), 1.0))
            step(nc.vector.memset(f(v_hi[:, :, :, HEAD:P]), 1.0))
            step(nc.vector.memset(f(v_lo[:, :, :, HEAD:P]), 0.0))
            dve.wait_ge(s_silu, 1)
            c_in = c_act[:, :].rearrange("p (s k) -> p k s", s=2)
            both(c_in, c_parts[:, :, 0:2], c_parts[:, :, 2:4])
            dve.wait_ge(s_mat, 16)
            step(nc.vector.tensor_tensor(pair[:, :], ident[0:4, 0:2], ident[0:4, 2:4], ALU.add), consts)
            step(nc.vector.tensor_copy(ones_r[:, :], ones))
            dve.wait_ge(s_vec, 16)
            dve.wait_ge(s_lam, 1)
            lam = vec[:, VCOL["lru_lam"][0]:VCOL["lru_lam"][0] + 4]
            e_, r_, q_, a_ = (small[:, i:i + 4] for i in (4, 8, 12, 16))
            step(nc.vector.tensor_scalar(r_, e_, 2.0, None, ALU.add))
            step(nc.vector.reciprocal(r_, r_))
            step(nc.vector.tensor_tensor(r_, r_, e_, ALU.mult))
            step(nc.vector.tensor_tensor(q_, r_, r_, ALU.mult))
            step(nc.vector.tensor_scalar(a_, q_, 1.0 / 17, 1.0 / 15, ALU.mult, ALU.add))
            for odd in (13, 11, 9, 7, 5, 3, 1):
                step(nc.vector.tensor_tensor(a_, a_, q_, ALU.mult))
                step(nc.vector.tensor_scalar(a_, a_, 1.0 / odd, None, ALU.add))
            step(nc.vector.scalar_tensor_tensor(a_, a_, 2.0, r_, ALU.mult, ALU.mult))
            step(nc.vector.tensor_scalar(r_, lam, -1.0, 0.0, ALU.mult, ALU.max))
            step(nc.vector.tensor_tensor(a_, a_, r_, ALU.add))
            step(nc.vector.tensor_scalar(decay[:, :], a_, -8.0, None, ALU.mult))
            for kind, layer, stream, first in steps:
                if kind == "mod":
                    mg = ModGroups(kind, layer, stream, first)
                    mod_store(mg, mg.tiles)
                    dve.wait_ge(s_in, 16)
                    dve.wait_ge(s_ctx, 16)
                elif kind == "norm1":
                    norm(layer, stream, 0)
                elif kind == "norm2":
                    norm(layer, stream, 3)
                elif kind == "z":
                    z_tiles(stream, first, 13)
                elif kind == "z_kv":
                    z_tiles(stream, first, 1)
                elif kind == "fourier":
                    fourier(stream, first)
                elif kind == "conv":
                    conv(layer, stream)
                elif kind == "qk":
                    qk(layer, stream, [Z_K] if (layer, stream) == (1, "ctx") else list(range(Z_Q, Z_K + 1)), first)
                elif kind == "attn":
                    attention(layer, stream, first)
                elif kind == "merge":
                    merge(stream, first)
                elif kind == "w_o":
                    w_o(layer, stream, first)
                elif kind == "pre_mix":
                    rms(lambda k: v(f"pre_mix{layer}", k))
                elif kind == "pre_ffn":
                    rms(lambda k: v(f"pre_ffn{layer}", k))
                elif kind == "post_mix":
                    post_norm(lambda k: v(f"post_mix{layer}", k))
                elif kind == "post_ffn":
                    post_norm(lambda k: v(f"post_ffn{layer}", k))
                elif kind == "ab_conf":
                    ab_conf(first)
                elif kind == "ab_lru":
                    ab_lru(first)
                elif kind == "lru_gate":
                    lru(first)
                elif kind == "mix_out":
                    passed(KB, first)
                elif kind == "ffn":
                    ffn(first)
                elif kind == "ml_qk":
                    passed(8, first)
                    passed(8, first + 8)
                elif kind == "ml_gates":
                    ml_gates(first)
                elif kind == "ml_v":
                    ml_v(first)
                elif kind == "mlstm":
                    mlstm()
                elif kind == "ff":
                    ff(layer, stream, first)
            dve.sem_inc(s_final, 1)


def arrays_of(inputs):
    w = {k: np.asarray(a) for k, a in inputs.items()}
    mats, ropes = shape_tables()
    return {
        "ws": stream_tiles(w), "vecs": vector_table(w), "mats": mats, "ropes": ropes,
        "x_t": np.ascontiguousarray(w["x"][0].T), "ctx_t": np.ascontiguousarray(w["ctx"][0].T),
        "bv": np.ascontiguousarray(w["ml_b_in_2"][:, D:2 * D]),
    }


def kernel(**inputs):
    import concourse.bacc as bacc
    from concourse.bass_utils import run_bass_kernel_spmd

    nc = bacc.Bacc("TRN2", target_bir_lowering=False, num_devices=1)
    arrays = arrays_of(inputs)
    aps = [nc.dram_tensor(n, a.shape, mybir.dt.from_np(a.dtype), kind="ExternalInput").ap() for n, a in arrays.items()]
    out = nc.dram_tensor("out_t", (D, SEQ), F32, kind="ExternalOutput").ap()
    build(nc, *aps, out)
    r = run_bass_kernel_spmd(nc, [arrays], core_ids=[0])
    return np.ascontiguousarray(r.results[0]["out_t"].T).reshape(1, SEQ, D)
```

```python
from contextlib import ExitStack

import numpy as np
import concourse.bass as bass
from concourse import mybir

F32 = mybir.dt.float32
F32R = mybir.dt.float32r
ALU = mybir.AluOpType
ACT = mybir.ActivationFunctionType
AX_X = mybir.AxisListType.X

P = 128
D = 1024
KB = D // P
SEQ = 512
CTX = 256
DEPTH = 2
HEAD = 64
N_HEADS = 8
N_MOD = 6
FF = 4096
FF2 = 2816
EPS = 1e-6
R = 4
TILE = KB * P
LEAD = 3
FFN_GROUPS = ((0, 8), (8, 8), (16, 6))
FFN_TILES = sum(2 * n + KB for _, n in FFN_GROUPS)
KT_ALL = (SEQ + CTX) // P

Z_B, Z_C, Z_X, Z_F, Z_Q, Z_K = 0, 2, 4, 6, 8, 12

MOD_GROUPS = {
    ("mod", 0, "main"): (0, 0, 4), ("qk", 0, "ctx"): (0, 4, 3), ("attn", 0, "ctx"): (0, 7, 5),
    ("qk", 0, "main"): (1, 0, 6), ("qk", 1, "ctx"): (1, 6, 1), ("qk", 1, "main"): (1, 7, 5),
}


def vector_columns():
    cols, at = {}, 0
    for name, n in (
        ("c", 8), ("c_ctx", 8), ("b_mod0", 48), ("b_mod1", 48),
        ("g1_0", 8), ("g1_1", 8), ("g2_0", 8), ("g2_1", 8),
        ("w_conv0", 6), ("w_conv1", 6), ("gq0", 1), ("gq1", 1), ("gk0", 1), ("gk1", 1),
        ("pre_mix0", 8), ("pre_mix1", 8), ("post_mix0", 8), ("post_mix1", 8),
        ("pre_ffn0", 8), ("pre_ffn1", 8), ("post_ffn0", 8), ("post_ffn1", 8),
        ("ab_b", 16), ("conf_w", 31 * 4), ("conf_b", 4), ("ln_g", 4), ("ln_b", 4),
        ("lru_w", 16), ("lru_b", 4), ("lru_ba", 4), ("lru_bx", 4), ("lru_lam", 4),
        ("ml_b", 16), ("ml_bg", 1), ("head_g", 8),
    ):
        cols[name] = (at, n)
        at += n
    return cols, at


VCOL, N_VCOL = vector_columns()


def plan():
    steps, at = [], 0

    def add(kind, n, layer=0, stream="main"):
        nonlocal at
        steps.append((kind, layer, stream, at))
        at += n + 4 * MOD_GROUPS.get((kind, layer, stream), (0, 0, 0))[2]

    def block(layer, stream):
        add("norm1", 0, layer, stream)
        add("z", 14, layer, stream)
        add("fourier", 5 if stream == "main" else 2, layer, stream)
        add("qk", 0, layer, stream)
        add("attn", 0, layer, stream)
        add("merge", 32, layer, stream)
        add("w_o", 8, layer, stream)
        add("norm2", 0, layer, stream)
        add("ff", 64, layer, stream)
        if layer == 0:
            add("roots", 0, 1, stream)

    add("mod", 0, 0)
    add("roots", 0, 0, "ctx")
    add("roots", 0, 0, "main")
    block(0, "ctx")
    block(0, "main")
    add("norm1", 0, 1, "ctx")
    add("z_kv", 2, 1, "ctx")
    add("qk", 0, 1, "ctx")
    block(1, "main")
    add("pre_mix", 0, 0)
    add("ab_conf", 8)
    add("ab_lru", 8)
    add("lru_gate", 1)
    add("mix_out", 8, 0)
    add("post_mix", 0, 0)
    add("pre_ffn", 0, 0)
    add("ffn", FFN_TILES, 0)
    add("post_ffn", 0, 0)
    add("pre_mix", 0, 1)
    add("ml_qk", 16)
    add("ml_gates", 1)
    add("ml_v", 8)
    add("mlstm", 0)
    add("mix_out", 8, 1)
    add("post_mix", 0, 1)
    add("pre_ffn", 0, 1)
    add("ffn", FFN_TILES, 1)
    add("post_ffn", 0, 1)
    return steps, at


def stream_tiles(w):
    out = []

    def cols(m, first, n):
        part = m[:, first:first + n * P].reshape(KB, P, n, P)
        out.extend(part.transpose(2, 1, 0, 3).reshape(n, P, TILE))

    def fourier(length):
        k = np.arange(HEAD)
        ang = 2 * np.pi * np.outer(k, k) / HEAD
        t = np.zeros((P, TILE), np.float32)
        for i, fn in enumerate((np.cos, np.sin)):
            for g in range(2):
                t[g * HEAD:(g + 1) * HEAD, i * P + g * HEAD:i * P + (g + 1) * HEAD] = fn(ang) / 8.0
        out.append(t)
        k = np.arange(length)
        ang = 2 * np.pi * (np.outer(k, k) % length) / length
        big = np.stack([np.cos(ang), -np.sin(ang)]) / np.sqrt(length)
        big = big.astype(np.float32).reshape(2, length // P, P, length)
        rows = big.reshape(2 * (length // P), P, length)
        per = TILE // length
        for i in range(0, rows.shape[0], per):
            out.append(rows[i:i + per].transpose(1, 0, 2).reshape(P, TILE))

    def ffn(gate, up, down):
        for first, n in FFN_GROUPS:
            for m in range(first, first + n):
                cols(gate, m * P, 1)
                cols(up, m * P, 1)
            for m in range(KB):
                t = np.zeros((P, TILE), np.float32)
                part = down[first * P:(first + n) * P, m * P:(m + 1) * P]
                t[:, :n * P] = part.reshape(n, P, P).transpose(1, 0, 2).reshape(P, n * P)
                out.append(t)

    for kind, layer, stream, at in plan()[0]:
        assert at == len(out), (kind, at, len(out))
        if (kind, layer, stream) in MOD_GROUPS:
            of, g0, n = MOD_GROUPS[kind, layer, stream]
            for g in range(g0, g0 + n):
                for kk in range(0, KB, 2):
                    part = w["w_mod"][of][kk * P:(kk + 2) * P, g * 512:(g + 1) * 512]
                    out.append(part.reshape(2, P, 512).transpose(1, 0, 2).reshape(P, TILE))
        if kind == "z":
            cols(w["w_in"][layer], 0, 14)
        elif kind == "z_kv":
            cols(w["w_in"][layer], 12 * P, 2)
        elif kind == "fourier":
            fourier(SEQ if stream == "main" else CTX)
        elif kind == "merge":
            branch = np.concatenate([w["w_conv_out"][layer], w["w_four_out"][layer], w["w_attn_out"][layer]])
            for m in range(KB):
                for g in range(3):
                    cols(w["w_in"][layer], 14 * P + g * D + m * P, 1)
                cols(branch, m * P, 1)
        elif kind == "w_o":
            cols(w["w_o"][layer], 0, 8)
        elif kind == "ff":
            for g in range(4):
                cols(w["w_ff1"][layer], g * D, 8)
                cols(w["w_ff2"][layer][g * D:(g + 1) * D], 0, 8)
        elif kind == "ab_conf":
            for b in range(4):
                cols(w["ab_w_in_2"][0], b * P, 1)
                cols(w["ab_w_in_2"][0], (4 + b) * P, 1)
        elif kind == "ab_lru":
            cols(w["ab_w_in_2"][0], 12 * P, 4)
            cols(w["ab_w_in_2"][0], 8 * P, 4)
        elif kind == "lru_gate":
            t = np.zeros((P, 2, 4, P), np.float32)
            for i, name in enumerate(("lru_w_a_2", "lru_w_x_2")):
                for h in range(8):
                    o = (h % 2) * HEAD
                    t[o:o + HEAD, i, h // 2, o:o + HEAD] = w[name][0, h]
            out.append(t.reshape(P, TILE))
        elif kind == "mix_out":
            cols(w["ml_w_out_2"][0] if layer else w["ab_w_out_2"][0], 0, 8)
        elif kind == "ffn":
            ffn(w["ffn_w_gate_2"][layer], w["ffn_w_up_2"][layer], w["ffn_w_down_2"][layer])
        elif kind == "ml_qk":
            cols(w["ml_w_in_2"][0], 0, 8)
            cols(w["ml_w_in_2"][0], 2 * D, 8)
        elif kind == "ml_gates":
            t = np.zeros((D, P), np.float32)
            t[:, 0:8] = w["ml_w_in_2"][0][:, 3 * D:3 * D + 8]
            t[:, 32:40] = w["ml_w_in_2"][0][:, 3 * D + 8:3 * D + 16]
            cols(t, 0, 1)
        elif kind == "ml_v":
            v = w["ml_w_in_2"][0][:, D:2 * D]
            for half in range(2):
                for kk in range(0, KB, 2):
                    part = v[kk * P:(kk + 2) * P, half * 512:(half + 1) * 512]
                    out.append(part.reshape(2, P, 512).transpose(1, 0, 2).reshape(P, TILE))
    return np.ascontiguousarray(np.stack(out), dtype=np.float32)


def vector_table(w):
    t = np.zeros((P, N_VCOL), np.float32)

    def put(name, v):
        at, n = VCOL[name]
        t[:, at:at + n] = np.asarray(v).reshape(n, P).T

    put("c", w["c"])
    put("c_ctx", w["c_ctx"])
    for i in range(2):
        put(f"b_mod{i}", w["b_mod"][i])
        put(f"g1_{i}", w["g_norm1"][i])
        put(f"g2_{i}", w["g_norm2"][i])
        put(f"w_conv{i}", w["w_conv"][i])
        put(f"gq{i}", np.tile(w["g_q"][i], 2))
        put(f"gk{i}", np.tile(w["g_k"][i], 2))
        for n in ("pre_mix", "post_mix", "pre_ffn", "post_ffn"):
            put(f"{n}{i}", w[f"{n}_g_2"][i])
    put("ab_b", w["ab_b_in_2"])
    put("conf_w", w["conf_conv_w_2"])
    put("conf_b", w["conf_conv_b_2"])
    put("ln_g", w["conf_ln_g_2"])
    put("ln_b", w["conf_ln_b_2"])
    put("lru_w", w["lru_conv_w_2"])
    put("lru_b", w["lru_conv_b_2"])
    put("lru_ba", w["lru_b_a_2"])
    put("lru_bx", w["lru_b_x_2"])
    put("lru_lam", w["lru_lambda_2"])
    b = w["ml_b_in_2"][0]
    put("ml_b", np.concatenate([b[:D], b[2 * D:3 * D]]))
    gb = np.zeros(P, np.float32)
    gb[0:8], gb[32:40] = b[3 * D:3 * D + 8], b[3 * D + 8:]
    put("ml_bg", gb)
    put("head_g", w["ml_head_g_2"])
    return t


def shape_tables():
    m = np.zeros((P, 5, P), np.float32)
    m[:, 0] = 1.0
    m[:, 1] = np.eye(P)
    for g in range(2):
        s = slice(g * HEAD, (g + 1) * HEAD)
        m[s, 2, s] = 1.0
    for p in range(P):
        lower = p % HEAD < HEAD // 2
        m[p + 32 if lower else p - 32, 3, p] = -1.0 if lower else 1.0
    m[:, 4] = np.where(np.arange(P)[:, None] <= np.arange(P)[None, :], 0.0, -1e30)
    n_freq = HEAD // 4
    inv = (np.float32(10000.0) ** (-np.arange(n_freq, dtype=np.float32) / n_freq)).astype(np.float32)
    t = np.arange(SEQ)
    ang = np.concatenate([(t // 64).astype(np.float32)[:, None] * inv, (t % 64).astype(np.float32)[:, None] * inv], -1)
    ang = np.tile(ang.T, (4, 1)).astype(np.float32)
    rope = np.stack([np.cos(ang), np.sin(ang)], axis=1).astype(np.float32)
    return m.reshape(P, 5 * P), rope.reshape(P, 2 * SEQ)


class Counts:

    def __init__(self):
        self.n, self.i, self.per, self.at = {}, None, {}, {}

    def now(self, sem, more=0):
        n = self.n.get(id(sem), 0) + more
        if self.i is not None and id(sem) in self.per:
            return self.i * self.per[id(sem)] + n
        assert self.i is None or n - more == self.at.get(id(sem), 0), "a count that changes in a loop"
        return n

    def next(self, sem, n=1):
        self.n[id(sem)] = self.n.get(id(sem), 0) + n
        return self.now(sem)

    def enter(self, i, per):
        self.at = dict(self.n)
        self.i, self.per = i, {id(k): n for k, n in per.items()}

    def leave(self, turns):
        for k, n in self.n.items():
            one = n - self.at.get(k, 0)
            assert one == self.per.get(k, 0), ("increments of one turn", one, self.per.get(k, 0))
            self.n[k] = self.at.get(k, 0) + turns * one
        self.i, self.per = None, {}


def build(nc, ws, vecs, mats, ropes, x_in, ctx_in, bv_in, out, upto=None):
    steps, n_tiles = plan()
    if upto is not None:
        n_tiles = steps[upto][3]
        steps = steps[:upto]

    with ExitStack() as stack:
        def sb(name, shape, dt=F32):
            return stack.enter_context(nc.sbuf_tensor(name, shape, dt))

        def sem(name):
            return stack.enter_context(nc.semaphore(name))

        raw = sb("raw", [P, R, TILE])
        w_hi = sb("w_hi", [P, R, TILE], F32R)
        w_lo = sb("w_lo", [P, R, TILE], F32R)
        x = sb("x", [P, KB, SEQ])
        xc = sb("xc", [P, KB, CTX])
        h_hi = sb("h_hi", [P, KB, SEQ], F32R)
        h_lo = sb("h_lo", [P, KB, SEQ], F32R)
        y_hi = sb("y_hi", [P, KB, SEQ], F32R)
        y_lo = sb("y_lo", [P, KB, SEQ], F32R)
        z = sb("z", [P, 16, SEQ])
        kv = sb("kv", [P, 12, SEQ], F32R)
        scr = sb("scr", [P, 4, SEQ])
        vec = sb("vec", [P, N_VCOL])
        mat = sb("mat", [P, 5 * P])
        mod = sb("mod", [P, DEPTH, N_MOD * KB, 2])
        gain = sb("gain", [P, DEPTH, 2, 2, KB])
        c_act = sb("c_act", [P, 16])
        c_parts = sb("c_parts", [P, KB, 4], F32R)
        pair = sb("pair", [4, 2])
        mx = sb("mx", [P, 2, 4])
        small = sb("small", [P, 64])
        eps = sb("eps", [P, 1])
        decay = sb("decay", [P, 4])
        ones_r = sb("ones_r", [P, P], F32R)
        bank = [stack.enter_context(nc.psum_tensor(f"bank{i}", [P, SEQ], F32)) for i in range(4, 8)]
        ring = stack.enter_context(nc.psum_tensor("ring", [P, R, SEQ], F32))

        ones, ident, head_ones, rot = (mat[:, i * P:(i + 1) * P] for i in range(4))
        causal = mat[:, 4 * P:5 * P]
        kvf = kv[:, :, :].rearrange("p a b -> p (a b)")
        nk = SEQ + CTX
        k_pair = kvf[:, 0:2 * nk].rearrange("p (g k) -> p g k", g=2)
        k_one = kvf[:, 2 * nk:4 * nk].rearrange("p (g k) -> p g k", g=2)
        v_hi = kvf[:, 4 * nk:6 * nk].rearrange("p (k g d) -> p k g d", k=KT_ALL, g=2)
        v_lo = kvf[:, 6 * nk:8 * nk].rearrange("p (k g d) -> p k g d", k=KT_ALL, g=2)


        xv = xc[:, :, :].rearrange("p a b -> p (a b)").rearrange("p (a b) -> p a b", b=SEQ)
        gate_rows = slice(32, 40)
        row = (xv[gate_rows, 2, :], xv[gate_rows, 3, :])

        thr_row, den_row, den_sq_row = xv[96:97, 2, :], xv[96:97, 3, :], xv[HEAD:HEAD + 1, 3, :]

        def head_out(h):
            return z[:, h // 2 + 4 * (h % 2), :]

        def v(name, i=0):
            return vec[:, VCOL[name][0] + i:VCOL[name][0] + i + 1]

        loaded = [sem(f"loaded{i}") for i in range(R)]
        s_mat = sem("matrices_loaded")
        s_in = sem("x_loaded")
        s_ctx = sem("ctx_loaded")
        s_rope = sem("rope_loaded")
        s_bv = sem("v_bias_loaded")
        w_hi_ready = sem("w_hi_ready")
        w_ready = sem("w_ready")
        tile_done = sem("tile_done")
        post = sem("post")
        evac = sem("evac")
        sq_ready = sem("sq_ready")
        ss_ready = sem("ss_ready")
        root_ready = sem("root_ready")
        t_ready = sem("t_ready")
        hi_ready = sem("hi_ready")
        lo_ready = sem("lo_ready")
        consts = sem("constants_ready")
        dve_own = sem("vector_own")
        act_own = sem("scalar_own")
        s_score = sem("scores_ready")
        s_max = sem("max_ready")
        s_mrow = sem("max_row_ready")
        s_shift = sem("shift_ready")
        s_q = sem("q_ready")
        s_st = sem("scores_t_ready")
        s_exp = sem("exp_ready")
        s_p = sem("p_ready")
        s_pv = sem("pv_done")
        s_on = sem("o_read")
        s_recip = sem("reciprocals_ready")
        s_spread = sem("reciprocals_spread")
        s_vec = sem("vectors_loaded")
        s_silu = sem("conditions_activated")
        s_free = sem("scratch_free")
        s_qn = sem("q_normed")
        s_rot = sem("rotated")
        s_x = sem("residual_ready")
        s_conv = sem("conv_ready")
        s_gate = sem("lru_gates_ready")
        s_gread = sem("lru_gates_read")
        s_act = sem("activated")
        s_lam = sem("decay_ready")
        s_row = sem("gate_rows_ready")
        s_col = sem("gate_columns_ready")
        s_bc = sem("row_spread")
        s_diag = sem("diagonal_ready")
        s_thr = sem("threshold_ready")
        s_qk_hi = sem("qk_upper_ready")
        s_prod = sem("weights_ready")
        s_prod_hi = sem("weights_upper_ready")
        s_den = sem("denominator_ready")
        s_den_sq = sem("denominator_squared")
        s_total = sem("head_total_ready")
        s_acc = sem("squares_summed")
        s_rstd = sem("rstd_ready")
        s_rspread = sem("rstd_spread")
        s_mod_rows = sem("mod_rows_ready")
        s_mod_cols = sem("mod_columns_ready")
        s_mod = sem("mod_ready")
        s_final = sem("result_ready")
        s_out = sem("stored")

        block = stack.enter_context(nc.Block())

        def length(stream):
            return SEQ if stream == "main" else CTX

        def x_of(stream):
            return x if stream == "main" else xc

        class ModGroups:

            def __init__(self, kind, layer, stream, first):
                self.layer, self.g0, self.n = MOD_GROUPS.get((kind, layer, stream), (0, 0, 0))
                self.first, self.tiles = first, 4 * self.n
                self.free = (2, 3) if kind == "attn" else (0, 1, 2, 3)
                self.stored = 0

            def share(self, i, of):
                return range(self.tiles * i // of, self.tiles * (i + 1) // of)

            def bank(self, g):
                return ring[:, self.free[g % len(self.free)], :]

            def rows(self, g):
                return z[0:4, Z_X + g % 2, :]

        def summed(kind, layer, stream):
            return kind in ("roots", "norm2", "post_mix", "post_ffn") or (kind, layer) == ("pre_mix", 0)

        def first_roots(stream):
            return small[:, 56:60] if stream == "main" else small[:, 60:64]

        def summed_at(kind, layer, stream):
            return 0 if (kind, layer, stream) == ("roots", 0, "ctx") else 2

        root_cols, rstd_cols = small[:, 48:52], small[:, 52:56]

        def max_rows(stream):
            n, per = (2, 2) if stream == "main" else (1, 1)
            return ring[0:1, per - 1:n * per:per, CTX:SEQ]

        turn = [None]

        def grouped(eng, n, first, body, C, per=None, size=R):
            turns = n // size
            turn[0] = None
            if first + turns * size + LEAD > n_tiles:
                turns -= 1
            if turns > 1:
                with eng.Fori(0, turns, 1) as i:
                    C.enter(i, per or {})
                    turn[0] = i
                    for u in range(size):
                        body(first + u, u, i * size)
                    C.leave(turns)
                turn[0] = None
            else:
                turns = 0
            for u in range(turns * size, n):
                body(first + u, u, 0)

        def at(ap, block, off):
            if isinstance(off, int):
                return ap[:, block, :]
            return ap[:, bass.ds(off + block, 1), :].rearrange("p o n -> p (o n)")

        @block.sync
        def _(sp):
            sp.dma_start(vec[:, :], vecs).then_inc(s_vec, 16)
            sp.dma_start(raw[:, 0, :], ws[0]).then_inc(loaded[0], 16)
            sp.dma_start(mat[:, :], mats).then_inc(s_mat, 16)
            for t in range(1, R):
                sp.dma_start(raw[:, t, :], ws[t]).then_inc(loaded[t], 16)
            sp.dma_start(xc[:, :, :], ctx_in.rearrange("(k p) t -> p k t", p=P)).then_inc(s_ctx, 16)
            sp.dma_start(x[:, :, :], x_in.rearrange("(k p) t -> p k t", p=P)).then_inc(s_in, 16)
            groups = n_tiles // R - 1
            with sp.Fori(0, groups, 1) as i:
                for u in range(R):
                    sp.wait_ge(w_ready, i * R + (u + 1))
                    sp.dma_start(raw[:, u, :], ws[bass.ds(i * R + (R + u), 1)].rearrange("o p n -> (o p) n"))\
                        .then_inc(loaded[u], 16)
            for t in range((groups + 1) * R, n_tiles):
                sp.wait_ge(w_ready, t - R + 1)
                sp.dma_start(raw[:, t % R, :], ws[t]).then_inc(loaded[t % R], 16)
            sp.wait_ge(s_final, 1)
            sp.dma_start(out.rearrange("(k p) t -> p k t", p=P), x[:, :, :]).then_inc(s_out, 16)
            sp.wait_ge(s_out, 16)

        @block.gpsimd
        def _(pool):
            def lower(u, n):
                pool.wait_ge(w_hi_ready, n)
                nc.gpsimd.tensor_tensor(w_lo[:, u, :], raw[:, u, :], w_hi[:, u, :].bitcast(F32),
                                        ALU.subtract).then_inc(w_ready, 1)

            with pool.Fori(0, n_tiles // R, 1) as i:
                for u in range(R):
                    lower(u, i * R + (u + 1))
            for t in range(n_tiles // R * R, n_tiles):
                lower(t % R, t + 1)

        @block.scalar
        def _(act):
            C = Counts()

            def split(c, off=0):
                t = c + LEAD
                if isinstance(off, int) and t >= n_tiles:
                    return
                act.wait_ge(loaded[t % R], off * (16 // R) + 16 * (t // R + 1))
                act.wait_ge(tile_done, off + (t + 1))
                nc.scalar.activation(w_hi[:, t % R, :], raw[:, t % R, :], ACT.Copy).then_inc(w_hi_ready, 1)

            def done(c, off=0):
                act.wait_ge(tile_done, off + (c + 1 + R))

            def begun(at_tile):
                act.wait_ge(post, at_tile + R)

            def squares(src, n, T, residual=False):
                for k in range(n):
                    if residual:
                        act.wait_ge(s_x, C.next(s_x))
                    if k >= 2:
                        act.wait_ge(ss_ready, C.next(ss_ready))
                    nc.scalar.activation(scr[:, k % 2, :T], src(k), ACT.Square).then_inc(sq_ready, 1)
                act.wait_ge(ss_ready, C.next(ss_ready, min(n, 2)))

            def root(ps, T, count):
                nc.scalar.activation(scr[:, 2, :T], ps[:, :T], ACT.Sqrt, bias=eps[:, 0:1], scale=1.0 / count)\
                    .then_inc(root_ready, 1)

            def upper(n, src, dst, bias=None):
                for k in range(n):
                    act.wait_ge(t_ready, C.next(t_ready))
                    if bias is None:
                        nc.scalar.activation(dst(k), src(k), ACT.Copy).then_inc(hi_ready, 1)
                    else:
                        nc.scalar.activation(dst(k), src(k), ACT.Identity, bias=bias(k)).then_inc(hi_ready, 1)

            def column_roots(T, cols=root_cols):
                for tt in range(T // P):
                    nc.scalar.activation(cols[:, tt:tt + 1], bank[tt][:, 0:1], ACT.Sqrt, bias=eps[:, 0:1],
                                         scale=1.0 / D).then_inc(root_ready, 1)

            def gain_norm(first, is_summed):
                begun(first)
                if is_summed:
                    act.wait_ge(ss_ready, C.next(ss_ready))
                else:
                    squares(lambda k: x[:, k, :], KB, SEQ, residual=True)
                column_roots(SEQ)
                upper(KB, lambda k: scr[:, k % 4, :], lambda k: h_hi[:, k, :])

            def post_norm(first):
                act.wait_ge(ss_ready, C.next(ss_ready))
                column_roots(SEQ)

            def biased(c, off, o, func, column):
                nc.scalar.activation(o, ring[:, c % R, :], func, bias=column).then_inc(evac, 1)

            def col(name, i, off):
                at0 = VCOL[name][0] + i
                return vec[:, at0:at0 + 1] if isinstance(off, int) else vec[:, bass.ds(off + at0, 1)]

            def ab_conf(first):
                for n in range(8):
                    c, b = first + n, n // 2
                    split(c)
                    done(c)
                    if n % 2 == 0:
                        biased(c, 0, z[:, b, :], ACT.Identity, col("ab_b", b, 0))
                    else:
                        act.wait_ge(post, c - 3 + R)
                        biased(c, 0, scr[:, b % 2, :], ACT.Sigmoid, col("ab_b", 4 + b, 0))

            def ab_lru(first):
                for n in range(8):
                    split(first + n)
                    done(first + n)
                    if n < 4:
                        biased(first + n, 0, z[:, 8 + n, :], ACT.Identity, col("ab_b", 12 + n, 0))
                    else:
                        biased(first + n, 0, z[:, 8 + n, :], ACT.Gelu_apprx_tanh, col("ab_b", 8 + n - 4, 0))

            def lru(first):
                split(first)
                act.wait_ge(ss_ready, C.next(ss_ready, 4))
                nc.scalar.activation(scr[:, 2, :], bank[0][:, :], ACT.Copy, scale=1.0 / (4 * P)).then_inc(root_ready, 1)
                act.wait_ge(t_ready, C.next(t_ready, 4))
                squares(lambda k: z[:, 4 + k, :], 4, SEQ)
                root(bank[0], SEQ, 4 * P)
                for b in range(4):
                    act.wait_ge(t_ready, C.next(t_ready))
                    nc.scalar.activation(z[:, 4 + b, :], z[:, 4 + b, :], ACT.Silu, bias=v("ln_b", b)).then_inc(s_act, 1)
                for b in range(4):
                    act.wait_ge(s_gate, C.next(s_gate))
                    nc.scalar.activation(z[:, 8 + b, :], bank[2][:, :], ACT.Sigmoid, bias=v("lru_ba", b))\
                        .then_inc(s_gread, 1)
                    nc.scalar.activation(z[:, b, :], bank[3][:, :], ACT.Sigmoid, bias=v("lru_bx", b))\
                        .then_inc(s_gread, 1)
                act.wait_ge(s_free, C.next(s_free))
                act.wait_ge(s_gread, C.next(s_gread, 8))
                for b in range(4):
                    nc.scalar.activation(scr[:, b, :], z[:, 8 + b, :], ACT.Tanh, scale=decay[:, b:b + 1])\
                        .then_inc(s_act, 1)
                for b in range(4):
                    act.wait_ge(s_act, 5 + b)
                    nc.scalar.activation(z[:, 8 + b, :], z[:, 8 + b, :], ACT.Exp, scale=decay[:, b:b + 1])\
                        .then_inc(s_act, 1)
                for b in range(4):
                    act.wait_ge(t_ready, C.next(t_ready))
                    nc.scalar.activation(scr[:, b, :], scr[:, b, :], ACT.Sqrt).then_inc(s_act, 1)

            def mix_out(first):
                def body(c, u, off):
                    split(c, off)
                    done(c, off)
                    nc.scalar.activation(at(z, u, off), ring[:, c % R, :], ACT.Copy).then_inc(evac, 1)
                grouped(act, KB, first, body, C)

            def ffn(first):
                def body(c, u, off):
                    pos, n = (u % 24, 8) if u < 48 else (u - 48, 6)
                    split(c, off)
                    if pos >= 2 * n or pos % 2:
                        return
                    done(c, off)
                    act.wait_ge(post, off + (c - 2 + R))
                    nc.scalar.activation(scr[:, pos // 2 % 2, :], ring[:, c % R, :], ACT.Silu).then_inc(evac, 1)
                grouped(act, FFN_TILES, first, body, C, size=24)

            def ml_qk(first):
                act.dma_start(xv[0:1, 0:2, :], bv_in.rearrange("o (a n) -> o a n", a=2)).then_inc(s_bv, 16)

                def qk_body(c, u, off):
                    split(c, off)
                    done(c, off)
                    biased(c, off, at(z, u, off), ACT.Identity, col("ml_b", u, off))

                def o_body(c, u, off):
                    split(c, off)
                    done(c, off)
                    biased(c, off, at(z, 8 + u, off), ACT.Sigmoid, col("ml_b", 8 + u, off))
                grouped(act, 8, first, qk_body, C)
                grouped(act, 8, first + 8, o_body, C)

            def ml_gates(first):
                split(first)
                done(first)
                biased(first, 0, scr[:, 0, :], ACT.Identity, v("ml_bg"))
                own_wait()
                f_rows = slice(32, 40)
                step(nc.scalar.activation(scr[f_rows, 1, :], scr[f_rows, 0, :], ACT.Abs))
                step(nc.scalar.activation(scr[f_rows, 1, :], scr[f_rows, 1, :], ACT.Exp, scale=-1.0))
                nc.scalar.activation(scr[f_rows, 1, :], scr[f_rows, 1, :], ACT.Ln, bias=mat[f_rows, 0:1])\
                    .then_inc(s_act, 1)

            def own_wait():
                act.wait_ge(s_row, C.next(s_row))

            def step(ins):
                ins.then_inc(act_own, 1)
                act.wait_ge(act_own, C.next(act_own))

            def ml_v(first):
                for half in range(2):
                    for n in range(4):
                        split(first + 4 * half + n)
                    done(first + 4 * half + 3)
                    for tt in range(4):
                        nc.scalar.activation(y_hi[:, 2 * tt + half, :], bank[tt][:, :], ACT.Copy).then_inc(hi_ready, 1)

            def mlstm():
                e0, prod0 = C.now(s_exp), C.now(s_prod)

                def query_key_parts(h):
                    b, lo0 = 4 * (h % 2), h % 2 * HEAD
                    s, other = slice(lo0, lo0 + HEAD), slice(HEAD - lo0, P - lo0)
                    q, k = z[s, h // 2, :], z[s, 4 + h // 2, :]
                    for o, src, scale in ((kv[s, b, :], q, 1.0), (kv[other, b, :], q, 1.0),
                                          (kv[s, b + 2, :], k, HEAD ** -0.5), (kv[0:HEAD, b + 3, :], k, HEAD ** -0.5)):
                        nc.scalar.activation(o, src, ACT.Copy, scale=scale).then_inc(s_qk_hi, 1)

                def exponentials(h, n):
                    act.wait_ge(s_diag, C.next(s_diag))
                    j = n * P
                    a_col, e = small[:, n * 8 + h:n * 8 + h + 1], scr[:, n % 2, :]
                    nc.scalar.activation(e[:, j:j + P], e[:, j:j + P], ACT.Exp, bias=a_col).then_inc(s_exp, 1)
                    if n < 3:
                        nc.scalar.activation(e[:, j + P:], bank[2 * (h % 2)][:, j + P:], ACT.Exp, bias=a_col)\
                            .then_inc(s_exp, 1)

                def upper_part(n):
                    act.wait_ge(s_prod, C.next(s_prod))
                    k = C.now(s_prod) - prod0 - 1
                    if k >= 2:
                        act.wait_ge(s_pv, C.now(s_pv) + k - 1)
                    j = slice(n * P, SEQ)
                    nc.scalar.activation(kv[:, 8 + 2 * (k % 2), j], scr[:, 2 + k % 2, j], ACT.Copy).then_inc(s_prod_hi, 1)

                def numerator(h):
                    act.wait_ge(s_pv, C.now(s_pv) + 4 * (h + 1))
                    act.wait_ge(s_q, C.now(s_q) + 2 * min(h + 2, N_HEADS))
                    nc.scalar.activation(head_out(h), ring[:, 2, :], ACT.Copy).then_inc(s_on, 1)
                    nc.scalar.activation(xv[:, h % 2, :], ring[:, 2, :], ACT.Square).then_inc(s_on, 1)

                def denominator(h):
                    act.wait_ge(s_den, h + 1)
                    if h:
                        act.wait_ge(s_total, h)
                    nc.scalar.activation(den_sq_row, den_row, ACT.Square, scale=float(np.sqrt(P * EPS)))\
                        .then_inc(s_den_sq, 1)

                def row_copy(h):
                    act.wait_ge(s_bc, C.next(s_bc))
                    if h >= 2:
                        act.wait_ge(s_total, h - 1)
                    nc.scalar.activation(xv[:, h % 2, :], bank[2 * (h % 2)][:, :], ACT.Copy).then_inc(s_act, 1)

                query_key_parts(0)
                row_copy(0)
                exponentials(0, 0)
                exponentials(0, 1)
                for h in range(N_HEADS):
                    for n in range(4):
                        if n == 0 and h:
                            numerator(h - 1)
                        if n == 2 and h + 1 < N_HEADS:
                            row_copy(h + 1)
                        upper_part(n)
                        if n < 2:
                            exponentials(h, n + 2)
                        elif h + 1 < N_HEADS:
                            exponentials(h + 1, n - 2)
                        if n == 0:
                            if h:
                                denominator(h - 1)
                            nc.scalar.activation(thr_row, bank[3][96:97, :], ACT.Exp).then_inc(s_thr, 1)
                        if n == 1 and h + 1 < N_HEADS:
                            query_key_parts(h + 1)
                numerator(N_HEADS - 1)
                denominator(N_HEADS - 1)
                C.next(s_q, 2 * N_HEADS)
                C.next(s_pv, 4 * N_HEADS)
                act.wait_ge(s_total, N_HEADS)
                nc.scalar.activation(small[:, 32:64], bank[1][:, 0:32], ACT.Sqrt, scale=1.0 / P)\
                    .then_inc(root_ready, 1)
                upper(N_HEADS, head_out, lambda k: h_hi[:, k, :])

            def norm(layer, stream, first, part):
                T, src, s = length(stream), x_of(stream), int(stream == "ctx")
                begun(first)
                if part == 0 and stream == "main":
                    act.dma_start(z[:, 14:16, :], ropes.rearrange("p (a t) -> p a t", a=2)).then_inc(s_rope, 16)
                if part:
                    act.wait_ge(ss_ready, C.next(ss_ready))
                    column_roots(T)
                upper(KB, lambda k: scr[:, k % 4, :T], lambda k: h_hi[:, k, :T],
                      lambda k: mod[:, layer, part * KB + k, s:s + 1])

            def mod_tiles(mg, numbers):
                for i in numbers:
                    split(mg.first + i)
                    if i % 4 == 0 and i:
                        mod_rows(mg, i // 4 - 1)
                if len(numbers) and numbers.stop == mg.tiles:
                    mod_rows(mg, mg.n - 1)

            def mod_rows(mg, g):
                done(mg.first + 4 * g + 3)
                if g >= 2:
                    act.wait_ge(s_mod_cols, C.now(s_mod_rows) - 1)
                nc.scalar.activation(mg.rows(g), mg.bank(g)[0:4, :], ACT.Copy).then_inc(s_mod_rows, 1)
                C.next(s_mod_rows)

            def z_tiles(layer, stream, first, n):
                T = length(stream)

                def body(c, u, off):
                    split(c, off)
                    done(c, off)
                    nc.scalar.activation(at(z[:, :, :T], (Z_K if n == 0 else 0) + u, off), ring[:, c % R, :T],
                                         ACT.Copy).then_inc(evac, 1)
                grouped(act, max(n, 1), first, body, C)
                c = first + max(n, 1)
                split(c)
                done(c)
                kt = 0 if stream == "main" else SEQ // P
                nc.scalar.activation(v_hi[:, kt:kt + T // P, :, 0:HEAD].rearrange("p k g d -> p (k g) d"),
                                     ring[:, c % R, :T].rearrange("p (k d) -> p k d", d=HEAD),
                                     ACT.Copy).then_inc(evac, 1)

            def fourier(layer, stream, first):
                T = length(stream)
                split(first)
                done(first)
                for tt in range(T // P):
                    nc.scalar.activation(y_hi[:, 4 + tt, :], bank[tt][:, :], ACT.Copy).then_inc(hi_ready, 1)
                n = 4 if T == SEQ else 1
                for c in range(first + 1, first + 1 + n):
                    split(c)
                done(first + n)
                for fb in range(2):
                    nc.scalar.activation(y_hi[:, 2 + fb, :T], bank[fb][:, :T], ACT.Copy).then_inc(hi_ready, 1)

            def qk(layer, stream, blocks, first):
                T = length(stream)
                mg = ModGroups("qk", layer, stream, first)
                begun(first)
                if len(blocks) > 1:
                    act.wait_ge(s_free, C.next(s_free))

                def square(n):
                    if n >= 2:
                        act.wait_ge(ss_ready, ss0 + n - 1)
                    nc.scalar.activation(scr[:, n % 2, :T], z[:, blocks[n], :T], ACT.Square).then_inc(sq_ready, 1)

                ss0 = C.now(ss_ready)
                square(0)
                for n in range(len(blocks)):
                    if n + 1 < len(blocks):
                        square(n + 1)
                    act.wait_ge(ss_ready, ss0 + n + 1)
                    if n:
                        act.wait_ge(s_qn, C.next(s_qn))
                    root(bank[n % 2], T, HEAD)
                    if n:
                        mod_tiles(mg, mg.share(2 * n - 1, 2 * len(blocks)))
                    mod_tiles(mg, mg.share(2 * n, 2 * len(blocks)))
                mod_tiles(mg, mg.share(2 * len(blocks) - 1, 2 * len(blocks)))
                C.next(ss_ready, len(blocks))
                C.next(s_qn)

            def attention(layer, stream, first):
                T = length(stream)
                mg = ModGroups("attn", layer, stream, first)
                kts = range(0 if stream == "main" else SEQ // P, KT_ALL)
                pv0 = C.now(s_st)

                def unnormed(h):
                    b, s = h // 2, slice(h % 2 * HEAD, (h % 2 + 1) * HEAD)
                    act.wait_ge(s_pv, pv0 + (h + 1) * len(kts))
                    r, ps = h % 4 * 32, bank[2 + h % 2]
                    nc.scalar.activation(z[s, Z_Q + b, :T], ps[0:HEAD, :T], ACT.Copy).then_inc(s_on, 1)
                    nc.scalar.activation(scr[r:r + 1, 2 + h // 4, :T], ps[HEAD:HEAD + 1, :T], ACT.Copy)\
                        .then_inc(s_on, 1)

                def shift(h):
                    act.wait_ge(s_mrow, C.next(s_mrow))
                    act.wait_ge(s_q, C.next(s_q, 2))
                    nc.scalar.activation(y_lo[HEAD:HEAD + 1, 6 + h % 2, :T].rearrange("p (a b) -> p a b", b=CTX),
                                         max_rows(stream), ACT.Copy, scale=-1.0).then_inc(s_shift, 1)

                shift(0)
                for h in range(N_HEADS):
                    for n, kt in enumerate(kts):
                        act.wait_ge(s_st, C.next(s_st))
                        k = C.now(s_st) - 1
                        if k >= 2:
                            act.wait_ge(s_p, k - 1)
                        nc.scalar.activation(z[:, 13 + k % 2, :T], bank[k % 2][:, :T], ACT.Exp, scale=HEAD ** -0.5)\
                            .then_inc(s_exp, 1)
                        if k >= 2:
                            act.wait_ge(s_pv, k - 1)
                        nc.scalar.activation(y_hi[:, 4 + k % 2, :T], bank[k % 2][:, :T], ACT.Exp, scale=HEAD ** -0.5)\
                            .then_inc(s_exp, 1)
                        if n == 1 and h:
                            unnormed(h - 1)
                        if stream == "main" and n == len(kts) - 2 and h + 1 < N_HEADS:
                            shift(h + 1)
                    mod_tiles(mg, mg.share(2 * h, 2 * N_HEADS))
                    if stream == "ctx" and h + 1 < N_HEADS:
                        shift(h + 1)
                    mod_tiles(mg, mg.share(2 * h + 1, 2 * N_HEADS))
                unnormed(N_HEADS - 1)
                C.next(s_on, 2 * N_HEADS)
                C.next(s_pv, N_HEADS * len(kts))
                upper(4, lambda k: z[:, Z_Q + k, :T], lambda k: y_hi[:, 4 + k, :T])

            def merge(layer, stream, first):
                T = length(stream)

                def body(c, u, off):
                    split(c, off)
                    if u % R == 3:
                        return
                    done(c, off)
                    g = u % R
                    act.wait_ge(post, off + (c - g + R))
                    nc.scalar.activation(scr[:, g, :T], ring[:, c % R, :T], ACT.Sigmoid).then_inc(evac, 1)
                grouped(act, 32 - R, first, body, C)
                for u in range(32 - R, 32):
                    body(first + u, u, 0)
                upper(KB, lambda k: z[:, k, :T], lambda k: h_hi[:, k, :T])

            def ff(layer, stream, first):
                T = length(stream)

                def body(c, u, off):
                    split(c, off)
                    if u % 16 >= KB:
                        return
                    done(c, off)
                    act.wait_ge(post, off + (c - 1 + R))
                    nc.scalar.activation(scr[:, u % 2, :T], ring[:, c % R, :T], ACT.Relu).then_inc(evac, 1)
                grouped(act, 64, first, body, C, size=16)

            act.wait_ge(s_vec, 16)
            act.wait_ge(consts, 1)
            nc.scalar.activation(c_act[:, :], vec[:, 0:16], ACT.Silu).then_inc(s_silu, 1)
            for t in range(-LEAD, 0):
                split(t)
            lam = vec[:, VCOL["lru_lam"][0]:VCOL["lru_lam"][0] + 4]
            step(nc.scalar.activation(small[:, 0:4], lam, ACT.Abs))
            nc.scalar.activation(small[:, 4:8], small[:, 0:4], ACT.Exp, scale=-1.0).then_inc(s_lam, 1)
            for n, (kind, layer, stream, first) in enumerate(steps):
                if kind == "mod":
                    mg = ModGroups(kind, layer, stream, first)
                    mod_tiles(mg, mg.share(0, 1))
                elif kind == "roots":
                    act.wait_ge(ss_ready, C.next(ss_ready))
                    column_roots(length(stream), first_roots(stream))
                elif kind == "norm1":
                    norm(layer, stream, first, 0)
                elif kind == "z":
                    z_tiles(layer, stream, first, 13)
                elif kind == "z_kv":
                    z_tiles(layer, stream, first, 0)
                elif kind == "fourier":
                    fourier(layer, stream, first)
                elif kind == "qk":
                    qk(layer, stream, [Z_K] if (layer, stream) == (1, "ctx") else list(range(Z_Q, Z_K + 1)), first)
                elif kind == "attn":
                    attention(layer, stream, first)
                elif kind == "merge":
                    merge(layer, stream, first)
                elif kind == "w_o":
                    for c in range(first, first + KB):
                        split(c)
                elif kind == "norm2":
                    norm(layer, stream, first, 3)
                elif kind == "pre_mix":
                    gain_norm(first, layer == 0)
                elif kind == "pre_ffn":
                    gain_norm(first, False)
                elif kind in ("post_mix", "post_ffn"):
                    post_norm(first)
                elif kind == "ab_conf":
                    ab_conf(first)
                elif kind == "ab_lru":
                    ab_lru(first)
                elif kind == "lru_gate":
                    lru(first)
                elif kind == "mix_out":
                    mix_out(first)
                elif kind == "ffn":
                    ffn(first)
                elif kind == "ml_qk":
                    ml_qk(first)
                elif kind == "ml_gates":
                    ml_gates(first)
                elif kind == "ml_v":
                    ml_v(first)
                elif kind == "mlstm":
                    mlstm()
                elif kind == "ff":
                    ff(layer, stream, first)

        @block.tensor
        def _(pe):
            C = Counts()

            def three(o, a_hi, a_lo, b_hi, b_lo, start, stop):
                nc.tensor.matmul(o, a_hi, b_hi, start=start, stop=False)
                nc.tensor.matmul(o, a_hi, b_lo, start=False, stop=False)
                return nc.tensor.matmul(o, a_lo, b_hi, start=False, stop=stop)

            def ready(c, off=0):
                pe.wait_ge(w_ready, off + (c + 1))
                pe.wait_ge(post, off + (c + 1))

            def w(c, k, n=P):
                return w_hi[:, c % R, k * n:(k + 1) * n], w_lo[:, c % R, k * n:(k + 1) * n]

            def product(c, T, a_hi, a_lo, blocks=range(KB), o=None, last=True, first_k=0, before=None):
                o = ring[:, c % R, :T] if o is None else o
                for n, k in enumerate(blocks):
                    if before:
                        before(k)
                    m = three(o, *w(c, k), a_hi[:, k, :T], a_lo[:, k, :T], n == 0, n == len(blocks) - 1)
                if last:
                    m.then_inc(tile_done, 1)

            def sums(n, T, lhs, ps):
                for k in range(n):
                    pe.wait_ge(sq_ready, C.next(sq_ready))
                    nc.tensor.matmul(ps(k)[:, :T], lhs, scr[:, k % 2, :T], start=(k == 0), stop=(k == n - 1))\
                        .then_inc(ss_ready, 1)

            def column_norm(T, is_summed, spread):
                column_sums(T, is_summed, 2)
                C.next(root_ready, T // P)
                spread_rstd(T, spread)

            def column_sums(T, is_summed, at_block):
                for k in range(1 if is_summed else KB):
                    if is_summed:
                        pe.wait_ge(s_acc, C.next(s_acc))
                    else:
                        pe.wait_ge(sq_ready, C.next(sq_ready))
                    src = scr[:, at_block if is_summed else k % 2, :]
                    for tt in range(T // P):
                        m = nc.tensor.matmul(bank[tt][:, 0:1], src[:, tt * P:(tt + 1) * P], ones[:, 0:1],
                                             start=k == 0, stop=is_summed or k == KB - 1)
                    m.then_inc(ss_ready, 1)

            def spread_rstd(T, spread):
                pe.wait_ge(s_rstd, C.next(s_rstd))
                for tt in range(T // P):
                    m = nc.tensor.matmul(spread[:, tt * P:(tt + 1) * P], rstd_cols[:, tt:tt + 1].to_broadcast([P, P]),
                                         ident, start=True, stop=True)
                m.then_inc(s_rspread, 1)

            def blocks_ready(k0):
                return lambda k: pe.wait_ge(lo_ready, k0 + k + 1)

            def mod_tiles(mg, numbers):
                for i in numbers:
                    g, c = i // 4, mg.first + i
                    pe.wait_ge(w_ready, c + 1)
                    if i == 0:
                        pe.wait_ge(post, c + R)
                        mod0[0] = C.now(s_mod)
                    if i % 4 == 0 and g >= len(mg.free):
                        pe.wait_ge(s_mod, mod0[0] + g - len(mg.free) + 1)
                    o = mg.bank(g)[0:4, :]
                    for r in range(2):
                        a = c_parts[:, 2 * (i % 4) + r, :]
                        hi, lo = w(c, r, SEQ)
                        nc.tensor.matmul(o, a, hi, start=i % 4 == 0 and r == 0, stop=False)
                        m = nc.tensor.matmul(o, a, lo, start=False, stop=i % 4 == 3 and r == 1)
                    m.then_inc(tile_done, 1)
                    if i % 4 == 1 and g:
                        mod_columns(mg, g - 1)
                if len(numbers) and numbers.stop == mg.tiles:
                    mod_columns(mg, mg.n - 1)
                    C.next(s_mod, mg.n)

            def mod_columns(mg, g):
                pe.wait_ge(s_mod_rows, C.next(s_mod_rows))
                for j in range(4):
                    m = nc.tensor.matmul(mg.bank(g)[:, 2 * j:2 * j + 2], mg.rows(g)[:, j * P:(j + 1) * P], pair[:, :],
                                         start=True, stop=True)
                m.then_inc(s_mod_cols, 1)

            mod0 = [0]

            def z_tiles(stream, first, n):
                T = length(stream)
                k0 = C.now(lo_ready)
                C.next(lo_ready, KB)

                def body(c, u, off):
                    ready(c, off)
                    product(c, T, h_hi, h_lo, before=blocks_ready(k0) if u == 0 else None)
                grouped(pe, n, first, body, C)
                c = first + n
                ready(c)
                for tt in range(T // P):
                    s = slice(tt * P, (tt + 1) * P)
                    for k in range(KB):
                        m = three(ring[:, c % R, s], h_hi[:, k, s], h_lo[:, k, s], *w(c, k), k == 0, k == KB - 1)
                m.then_inc(tile_done, 1)

            def fourier(stream, first):
                T = length(stream)
                pe.wait_ge(lo_ready, C.next(lo_ready, 2))
                ready(first)
                for tt in range(T // P):
                    s = slice(tt * P, (tt + 1) * P)
                    for fb in range(2):
                        m = three(bank[tt][:, fb * 256:(fb + 1) * 256], y_hi[:, 2 + fb, s], y_lo[:, 2 + fb, s],
                                  *w(first, 0, 256), True, True)
                m.then_inc(tile_done, 1)
                pe.wait_ge(lo_ready, C.next(lo_ready, T // P))
                per, nkt = TILE // T, T // P
                total = 2 * nkt
                for idx in range(total):
                    c = first + 1 + idx // per
                    cs, kt = divmod(idx, nkt)
                    if idx % per == 0:
                        ready(c)
                    for fb in range(2):
                        a = slice(fb * 256 + cs * P, fb * 256 + (cs + 1) * P)
                        m = three(bank[fb][:, :T], y_hi[:, 4 + kt, a], y_lo[:, 4 + kt, a],
                                  *w(c, idx % per, T), idx == 0, idx == total - 1)
                    if idx % per == per - 1:
                        m.then_inc(tile_done, 1)

            def qk(layer, stream, n_blocks, first):
                T = length(stream)
                mg = ModGroups("qk", layer, stream, first)

                def total(n):
                    pe.wait_ge(sq_ready, C.next(sq_ready))
                    if n >= 2:
                        pe.wait_ge(root_ready, root0 + n - 1)
                    nc.tensor.matmul(bank[n % 2][:, :T], head_ones, scr[:, n % 2, :T], start=True, stop=True)\
                        .then_inc(ss_ready, 1)

                if n_blocks > 1:
                    pe.wait_ge(lo_ready, C.now(lo_ready, 4))
                root0 = C.now(root_ready)
                C.next(root_ready, n_blocks)
                total(0)
                for n in range(n_blocks):
                    if n + 1 < n_blocks:
                        total(n + 1)
                    mod_tiles(mg, mg.share(2 * n, 2 * n_blocks))
                    pe.wait_ge(s_qn, C.next(s_qn))
                    if stream == "main":
                        b = n if n_blocks > 1 else Z_K - Z_Q
                        nc.tensor.matmul(bank[2 + n % 2][:, :T], rot, z[:, Z_Q + b, :T], start=True, stop=True)\
                            .then_inc(s_rot, 1)
                    mod_tiles(mg, mg.share(2 * n + 1, 2 * n_blocks))

            def attention(layer, stream, first):
                T = length(stream)
                mg = ModGroups("attn", layer, stream, first)
                step_banks = 2 if stream == "main" else 1
                pe.wait_ge(post, first + R)
                kts = list(range(0 if stream == "main" else SEQ // P, KT_ALL))
                c0, n_k = kts[0] * P, len(kts) * P
                nq = T // P
                e0, e1 = C.now(s_exp), C.now(s_st)

                def scores(h, qts):
                    g, s = h // 4, 6 + h % 2
                    for qt in qts:
                        if qt == 0:
                            pe.wait_ge(s_q, C.next(s_q, 2))
                        n = C.next(s_score)
                        if n > 2:
                            pe.wait_ge(s_max, n - 2)
                        q = slice(qt * P, (qt + 1) * P)
                        slot = (n - 1) % 2
                        for a in range(0, n_k, SEQ):
                            e = min(a + SEQ, n_k)
                            o = ring[:, step_banks * slot + a // SEQ, 0:e - a]
                            nc.tensor.matmul(o, y_hi[:, s, q], k_pair[:, g, c0 + a:c0 + e], start=True, stop=False)
                            m = nc.tensor.matmul(o, y_lo[0:HEAD, s, q], k_one[0:HEAD, g, c0 + a:c0 + e],
                                                 start=False, stop=True)
                        m.then_inc(s_score, 1)

                def max_row(h):
                    pe.wait_ge(s_max, C.next(s_max, nq))
                    for qt in range(nq):
                        m = nc.tensor.matmul(max_rows(stream)[:, qt // 2, qt % 2 * P:(qt % 2 + 1) * P],
                                             mx[:, h % 2, qt:qt + 1], ident, start=True, stop=True)
                    m.then_inc(s_mrow, 1)

                def score_t(h, n):
                    g, s = h // 4, 6 + h % 2
                    if n == 0:
                        pe.wait_ge(s_shift, C.next(s_shift))
                    k = C.next(s_st) - 1
                    if k >= 2:
                        pe.wait_ge(s_exp, e0 + 2 * (k - e1 - 1))
                    keys = slice(kts[n] * P, (kts[n] + 1) * P)
                    nc.tensor.matmul(bank[k % 2][:, :T], k_pair[:, g, keys], y_hi[:, s, :T], start=True, stop=False)
                    nc.tensor.matmul(bank[k % 2][:, :T], k_one[0:HEAD + 1, g, keys], y_lo[0:HEAD + 1, s, :T],
                                     start=False, stop=True).then_inc(s_st, 1)

                def values(h, n):
                    g = h // 4
                    k = C.next(s_p)
                    pe.wait_ge(s_p, k)
                    if n == 0 and h >= 2:
                        pe.wait_ge(s_on, C.next(s_on, 2))
                    b = 4 + (k - 1) % 2
                    m = three(bank[2 + h % 2][:, :T], v_hi[:, kts[n], g, :], v_lo[:, kts[n], g, :],
                              y_hi[:, b, :T], y_lo[:, b, :T], n == 0, n == len(kts) - 1)
                    m.then_inc(s_pv, 1)

                scores(0, range(nq))
                max_row(0)
                score_t(0, 0)
                score_t(0, 1)
                for h in range(N_HEADS):
                    more = h + 1 < N_HEADS
                    if stream == "ctx":
                        if more:
                            scores(h + 1, range(nq))
                        mod_tiles(mg, mg.share(2 * h, 2 * N_HEADS))
                        values(h, 0)
                        values(h, 1)
                        if more:
                            max_row(h + 1)
                        mod_tiles(mg, mg.share(2 * h + 1, 2 * N_HEADS))
                        if more:
                            score_t(h + 1, 0)
                            score_t(h + 1, 1)
                        continue
                    for n in range(len(kts)):
                        if n + 2 < len(kts):
                            score_t(h, n + 2)
                        elif more:
                            if n + 2 == len(kts):
                                max_row(h + 1)
                            score_t(h + 1, n + 2 - len(kts))
                        if more:
                            scores(h + 1, ((), (0, 1), (2,), (3,), (), ())[n])
                        values(h, n)
                C.next(s_on, 4)
                C.next(s_exp, 2 * N_HEADS * len(kts))
                for b in range(4):
                    if b % 2 == 0:
                        pe.wait_ge(s_recip, C.next(s_recip))
                    for i in range(2):
                        r = (2 * b + i) % 4 * 32
                        m = nc.tensor.matmul(bank[b][i * HEAD:(i + 1) * HEAD, :T],
                                             ident[:, r:r + 1].to_broadcast([P, HEAD]), scr[:, 2 + b // 2, :T],
                                             start=True, stop=True)
                    m.then_inc(s_spread, 1)

            def merge(stream, first):
                T = length(stream)
                y_all = C.next(lo_ready, 2 + 2 + 4)

                def body(c, u, off):
                    ready(c, off)
                    if u % R < 3:
                        product(c, T, h_hi, h_lo)
                        return
                    pe.wait_ge(lo_ready, y_all)
                    product(c, T, y_hi, y_lo, range(0, 2), last=False)
                    product(c, T, y_hi, y_lo, range(2, 4), o=bank[0][:, :T], last=False)
                    product(c, T, y_hi, y_lo, range(4, 8), o=bank[1][:, :T])
                grouped(pe, 32, first, body, C)

            def w_o(T, first):
                k0 = C.now(lo_ready)
                C.next(lo_ready, KB)

                def body(c, u, off):
                    ready(c, off)
                    product(c, T, h_hi, h_lo, before=blocks_ready(k0) if u == 0 else None)
                grouped(pe, KB, first, body, C)

            def ff(stream, first):
                T = length(stream)
                k0 = C.now(lo_ready)
                C.next(lo_ready, KB)

                def body(c, u, off):
                    ready(c, off)
                    if u % 16 < KB:
                        product(c, T, h_hi, h_lo, before=blocks_ready(k0) if u % 16 == 0 else None)
                    else:
                        def hidden(k):
                            if u % 16 == KB and k > KB - R:
                                pe.wait_ge(post, off + (c - KB + k + 1 + R))
                        product(c, T, y_hi, y_lo, before=hidden)
                grouped(pe, 64, first, body, C, size=16)

            def plain(n, first, a_hi, a_lo, split_first=KB):
                k0 = C.now(lo_ready)
                C.next(lo_ready, split_first)

                def body(c, u, off):
                    ready(c, off)
                    product(c, SEQ, a_hi, a_lo, before=blocks_ready(k0) if u == 0 and split_first else None)
                grouped(pe, n, first, body, C)

            def lru(first):
                for b in range(4):
                    pe.wait_ge(s_conv, C.next(s_conv))
                    nc.tensor.matmul(bank[0][:, :], ones, z[:, 4 + b, :], start=b == 0, stop=b == 3)\
                        .then_inc(ss_ready, 1)
                pe.wait_ge(root_ready, C.next(root_ready))
                sums(4, SEQ, ones, lambda k: bank[0])
                C.next(root_ready)
                pe.wait_ge(lo_ready, C.next(lo_ready, 4))
                ready(first)
                for b in range(4):
                    if b:
                        pe.wait_ge(s_gread, C.next(s_gread, 2))
                    for i in range(2):
                        m = three(bank[2 + i][:, :], *w(first, 4 * i + b), y_hi[:, 4 + b, :], y_lo[:, 4 + b, :],
                                  True, True)
                    m.then_inc(s_gate, 1)
                pe.wait_ge(s_gread, C.next(s_gread, 2))
                pe.sem_inc(tile_done, 1)

            def ffn(first):
                k0 = C.now(lo_ready)
                C.next(lo_ready, KB)

                def body(c, u, off):
                    pos, n = (u % 24, 8) if u < 48 else (u - 48, 6)
                    ready(c, off)
                    if pos < 2 * n:
                        product(c, SEQ, h_hi, h_lo, before=blocks_ready(k0) if u == 0 else None)
                        return

                    def hidden(k):
                        if pos == 2 * n and k >= n - 2:
                            pe.wait_ge(post, off + (c - 2 * (n - k) + 2 + R))
                    product(c, SEQ, y_hi, y_lo, range(n), before=hidden)
                grouped(pe, FFN_TILES, first, body, C, size=24)

            def ml_v(first):
                pe.wait_ge(s_bv, 16)
                for half in range(2):
                    if half:
                        pe.wait_ge(lo_ready, C.next(lo_ready, 4))
                    for n in range(4):
                        c = first + 4 * half + n
                        ready(c)
                        for tt in range(4):
                            s = slice(tt * P, (tt + 1) * P)
                            if n == 0:
                                nc.tensor.matmul(bank[tt][:, :], ones[0:1, :], xv[0:1, half, :], start=True, stop=False)
                            for r in range(2):
                                m = three(bank[tt][:, :], h_hi[:, 2 * n + r, s], h_lo[:, 2 * n + r, s],
                                          *w(c, r, SEQ), False, n == 3 and r == 1)
                        m.then_inc(tile_done, 1)

            def mlstm(first):
                pe.wait_ge(lo_ready, C.next(lo_ready, 4))
                pe.wait_ge(post, first + R)
                pe.wait_ge(s_row, C.next(s_row, 2))
                for tt in range(4):
                    m = nc.tensor.matmul(bank[0][:, tt * 8:tt * 8 + 8], xv[0:8, 3, tt * P:(tt + 1) * P],
                                         ident[0:8, 0:8], start=True, stop=True)
                m.then_inc(s_col, 1)
                pe.wait_ge(s_col, C.next(s_col, 2))

                def spread(h):
                    if h:
                        pe.wait_ge(s_thr, C.next(s_thr))
                    if h >= 2:
                        pe.wait_ge(s_exp, e0 + 7 * (h - 1))
                    for i in range(2):
                        m = nc.tensor.matmul((bank[2 * (h % 2)], bank[3])[i][:, :],
                                             ident[gate_rows, 32 + h:33 + h].to_broadcast([8, P]), row[i],
                                             start=True, stop=True)
                    m.then_inc(s_bc, 1)

                def score_t(h, n):
                    b = 4 * (h % 2)
                    if n == 0:
                        pe.wait_ge(s_qk_hi, 4 * (h + 1))
                        pe.wait_ge(s_q, C.next(s_q, 2))
                    k = C.next(s_st) - st0 - 1
                    if k >= 2:
                        pe.wait_ge(s_prod, k - 1)
                    keys, o = slice(n * P, (n + 1) * P), ring[:, k % 2, n * P:]
                    nc.tensor.matmul(o, kv[:, b + 2, keys], kv[:, b, n * P:], start=True, stop=False)
                    nc.tensor.matmul(o, kv[0:HEAD, b + 3, keys], kv[0:HEAD, b + 1, n * P:], start=False, stop=True)\
                        .then_inc(s_st, 1)

                def values(h, n):
                    k = C.next(s_p)
                    pe.wait_ge(s_prod_hi, k - p0)
                    pe.wait_ge(s_p, k)
                    if n == 0 and h:
                        pe.wait_ge(s_on, C.next(s_on, 2))
                        pe.wait_ge(s_den, h)
                    b = 8 + 2 * ((k - p0 - 1) % 2)
                    vb, vc = 2 * n + h // 4, slice(h % 4 * P, (h % 4 + 1) * P)
                    j = slice(n * P, SEQ)
                    three(ring[:, 2, j], y_hi[:, vb, vc], y_lo[:, vb, vc], kv[:, b, j], kv[:, b + 1, j], n == 0, n == 3)
                    nc.tensor.matmul(ring[:, 3, j], ones_r[:, :], kv[:, b, j], start=n == 0, stop=False)
                    nc.tensor.matmul(ring[:, 3, j], ones_r[:, :], kv[:, b + 1, j], start=False, stop=n == 3)\
                        .then_inc(s_pv, 1)

                def total(h):
                    pe.wait_ge(s_den_sq, h + 1)
                    for tt in range(4):
                        o, t = bank[1][:, 4 * h + tt:4 * h + tt + 1], slice(tt * P, (tt + 1) * P)
                        nc.tensor.matmul(o, xv[:, h % 2, t], ones[:, 0:1], start=True, stop=False)
                        m = nc.tensor.matmul(o, den_sq_row[:, t], ones[HEAD:HEAD + 1, 0:1], start=False, stop=True)
                    m.then_inc(s_total, 1)

                st0, p0, e0 = C.now(s_st), C.now(s_p), C.now(s_exp)
                spread(0)
                score_t(0, 0)
                score_t(0, 1)
                for h in range(N_HEADS):
                    for n in range(4):
                        if n < 2:
                            score_t(h, n + 2)
                        elif h + 1 < N_HEADS:
                            score_t(h + 1, n - 2)
                        if n == 1 and h:
                            total(h - 1)
                        values(h, n)
                        if n == 0 and h + 1 < N_HEADS:
                            spread(h + 1)
                pe.wait_ge(s_on, C.next(s_on, 2))
                total(N_HEADS - 1)
                C.next(s_thr)
                C.next(s_exp, 7 * N_HEADS)
                C.next(root_ready)
                pe.wait_ge(s_rstd, C.next(s_rstd))
                for h in range(N_HEADS):
                    if h >= 4:
                        pe.wait_ge(s_qn, C.now(s_qn) + h - 3)
                    for tt in range(4):
                        m = nc.tensor.matmul(bank[h % 4][:, tt * P:(tt + 1) * P],
                                             small[:, 4 * h + tt:4 * h + tt + 1].to_broadcast([P, P]), ident,
                                             start=True, stop=True)
                    m.then_inc(s_rspread, 1)
                C.next(s_qn, N_HEADS)

            pe.sem_inc(tile_done, R)
            pe.wait_ge(s_mat, 16)
            pe.wait_ge(lo_ready, C.next(lo_ready))
            pe.wait_ge(consts, 2)
            for kind, layer, stream, first in steps:
                if kind == "mod":
                    mg = ModGroups(kind, layer, stream, first)
                    mod_tiles(mg, mg.share(0, 1))
                elif kind == "roots":
                    pe.wait_ge(root_ready, C.now(root_ready))
                    column_sums(length(stream), True, summed_at(kind, layer, stream))
                    C.next(root_ready, length(stream) // P)
                elif kind == "norm1":
                    spread_rstd(length(stream), bank[0])
                elif kind in ("norm2", "pre_mix", "pre_ffn", "post_mix", "post_ffn"):
                    column_norm(length(stream), summed(kind, layer, stream),
                                ring[:, 0, :] if kind in ("post_mix", "post_ffn") else bank[0])
                elif kind == "z":
                    z_tiles(stream, first, 13)
                elif kind == "z_kv":
                    z_tiles(stream, first, 1)
                elif kind == "fourier":
                    fourier(stream, first)
                elif kind == "qk":
                    qk(layer, stream, 1 if (layer, stream) == (1, "ctx") else 5, first)
                elif kind == "attn":
                    attention(layer, stream, first)
                elif kind == "merge":
                    merge(stream, first)
                elif kind == "w_o":
                    w_o(length(stream), first)
                elif kind == "ab_conf":
                    plain(8, first, h_hi, h_lo)
                elif kind == "ab_lru":
                    plain(8, first, h_hi, h_lo, 0)
                elif kind == "lru_gate":
                    lru(first)
                elif kind == "mix_out":
                    plain(8, first, *((h_hi, h_lo) if layer else (y_hi, y_lo)))
                elif kind == "ffn":
                    ffn(first)
                elif kind == "ml_qk":
                    plain(8, first, h_hi, h_lo)
                    plain(8, first + 8, h_hi, h_lo, 0)
                elif kind == "ml_gates":
                    plain(1, first, h_hi, h_lo, 0)
                elif kind == "ml_v":
                    ml_v(first)
                elif kind == "mlstm":
                    mlstm(first)
                elif kind == "ff":
                    ff(stream, first)

        @block.vector
        def _(dve):
            C = Counts()

            def step(ins, sem=dve_own):
                ins.then_inc(sem, 1)
                dve.wait_ge(sem, C.next(sem))

            def issue(ins, sem=dve_own):
                ins.then_inc(sem, 1)
                return C.next(sem)

            def posted():
                dve.sem_inc(post, 1)
                C.next(post)

            def done(c, off=0):
                dve.wait_ge(tile_done, off + (c + 1 + R))

            def f(ap):
                return ap.bitcast(F32)

            def lower(n, src, dst, hi, bias=None, before=None):
                if before:
                    before(0)
                for k in range(n):
                    if before and k + 1 < n:
                        before(k + 1)
                    dve.wait_ge(hi_ready, C.next(hi_ready))
                    step(nc.vector.scalar_tensor_tensor(dst(k), src(k), bias(k) if bias else 0.0, f(hi(k)),
                                                   ALU.add, ALU.subtract), lo_ready)

            def both(src, hi, lo):
                step(nc.vector.tensor_copy(hi, src))
                step(nc.vector.tensor_tensor(lo, src, f(hi), ALU.subtract), lo_ready)

            def norm(layer, stream, part):
                T, src, s = length(stream), x_of(stream), int(stream == "ctx")
                normed_parts(T, src, lambda k: gain[:, layer, part // 3, s, k:k + 1],
                             lambda k: mod[:, layer, part * KB + k, s:s + 1], None if part else first_roots(stream))

            def column_rstd(T, kept=None):
                if kept is None:
                    dve.wait_ge(root_ready, C.next(root_ready, T // P))
                else:
                    dve.wait_ge(root_ready, C.now(root_ready))
                roots = root_cols if kept is None else kept
                nc.vector.reciprocal(rstd_cols[:, :T // P], roots[:, :T // P]).then_inc(s_rstd, 1)
                C.next(s_rstd)
                dve.wait_ge(s_rspread, C.next(s_rspread))

            def normed_parts(T, src, gain_of, shift_of=None, kept=None):
                column_rstd(T, kept)
                l0 = C.now(lo_ready)
                for k in range(KB + 1):
                    if k < KB:
                        if k >= 4:
                            dve.wait_ge(lo_ready, l0 + k - 3)
                        nc.vector.scalar_tensor_tensor(scr[:, k % 4, :T], src[:, k, :T], gain_of(k), bank[0][:, :T],
                                                       ALU.mult, ALU.mult).then_inc(t_ready, 1)
                        C.next(t_ready)
                    if k:
                        n = k - 1
                        dve.wait_ge(hi_ready, C.next(hi_ready))
                        nc.vector.scalar_tensor_tensor(h_lo[:, n, :T], scr[:, n % 4, :T], shift_of(n) if shift_of else 0.0,
                                                       f(h_hi[:, n, :T]), ALU.add, ALU.subtract).then_inc(lo_ready, 1)
                        C.next(lo_ready)

            def add_squares(src, T, start=False, at_block=2):
                total = scr[:, at_block, :T]
                if start:
                    step(nc.vector.tensor_tensor(total, src, src, ALU.mult))
                    return
                step(nc.vector.tensor_tensor(scr[:, 3, :T], src, src, ALU.mult))
                step(nc.vector.tensor_tensor(total, total, scr[:, 3, :T], ALU.add))

            def squares_done():
                dve.sem_inc(s_acc, 1)

            def mod_store(mg, tiles):
                if not mg.n:
                    return
                last = tiles >= mg.tiles
                while mg.stored < mg.n and (last or 4 * mg.stored + 5 < tiles):
                    g = mg.stored
                    dve.wait_ge(s_mod_cols, C.next(s_mod_cols))
                    b0 = VCOL[f"b_mod{mg.layer}"][0] + 4 * (mg.g0 + g)
                    o = mod[:, mg.layer, 4 * (mg.g0 + g):4 * (mg.g0 + g) + 4, :]
                    step(nc.vector.tensor_tensor(o, mg.bank(g)[:, 0:8].rearrange("p (j s) -> p j s", s=2),
                                                 vec[:, b0:b0 + 4].rearrange("p (j o) -> p j o", o=1).to_broadcast([P, 4, 2]),
                                                 ALU.add), s_mod)
                    mg.stored += 1
                if last:
                    dve.sem_inc(post, mg.tiles)
                    C.next(post, mg.tiles)
                    end = mg.g0 + mg.n
                    for half in range(2):
                        if not mg.g0 < 4 + 6 * half <= end:
                            continue
                        for s in range(2):
                            sc = (3 * half + 1) * KB
                            g = VCOL[f"g{half + 1}_{mg.layer}"][0]
                            step(nc.vector.scalar_tensor_tensor(gain[:, mg.layer, half, s, :],
                                                                mod[:, mg.layer, sc:sc + KB, s],
                                                                1.0, vec[:, g:g + KB], ALU.add, ALU.mult))

            def z_tiles(stream, first, n):
                T = length(stream)

                def body(c, u, off):
                    dve.wait_ge(evac, C.next(evac))
                    posted()
                grouped(dve, n, first, body, C, {evac: R, post: R})
                c = first + n
                kt = 0 if stream == "main" else SEQ // P
                dve.wait_ge(evac, C.next(evac))
                step(nc.vector.tensor_tensor(v_lo[:, kt:kt + T // P, :, 0:HEAD].rearrange("p k g d -> p (k g) d"),
                                        ring[:, c % R, :T].rearrange("p (k d) -> p k d", d=HEAD),
                                        f(v_hi[:, kt:kt + T // P, :, 0:HEAD].rearrange("p k g d -> p (k g) d")),
                                        ALU.subtract), post)

            def fourier(layer, stream, first):
                T = length(stream)
                for fb in range(2):
                    both(z[:, Z_F + fb, :T], y_hi[:, 2 + fb, :T], y_lo[:, 2 + fb, :T])
                for tt in range(T // P):
                    dve.wait_ge(hi_ready, C.next(hi_ready))
                    step(nc.vector.tensor_tensor(y_lo[:, 4 + tt, :], bank[tt][:, :], f(y_hi[:, 4 + tt, :]),
                                            ALU.subtract), lo_ready)
                posted()
                conv(layer, stream)
                n = 4 if T == SEQ else 1
                for c in range(first + 1, first + 1 + n):
                    done(c)
                    posted()
                for fb in range(2):
                    dve.wait_ge(hi_ready, C.next(hi_ready))
                    step(nc.vector.tensor_tensor(y_lo[:, 2 + fb, :T], bank[fb][:, :T], f(y_hi[:, 2 + fb, :T]),
                                            ALU.subtract), lo_ready)

            def conv(layer, stream):
                T = length(stream)
                for b in range(2):
                    step(nc.vector.tensor_tensor(z[:, Z_C + b, :T], z[:, Z_C + b, :T], z[:, Z_X + b, :T], ALU.mult))
                wv = lambda j, b: v(f"w_conv{layer}", 2 * j + b)
                for b in range(2):
                    step(nc.vector.tensor_scalar(scr[:, b, :T], z[:, Z_C + b, :T], wv(1, b), None, ALU.mult))
                for b in range(2):
                    step(nc.vector.scalar_tensor_tensor(scr[:, b, 1:T], z[:, Z_C + b, 0:T - 1], wv(0, b),
                                                       scr[:, b, 1:T], ALU.mult, ALU.add))
                for b in range(2):
                    step(nc.vector.scalar_tensor_tensor(scr[:, b, 0:T - 1], z[:, Z_C + b, 1:T], wv(2, b),
                                                       scr[:, b, 0:T - 1], ALU.mult, ALU.add))
                for b in range(2):
                    step(nc.vector.tensor_tensor(scr[:, b, :T], scr[:, b, :T], z[:, Z_B + b, :T], ALU.mult))
                for b in range(2):
                    both(scr[:, b, :T], y_hi[:, b, :T], y_lo[:, b, :T])
                dve.sem_inc(s_free, 1)

            def qk(layer, stream, blocks, first):
                T = length(stream)
                mg = ModGroups("qk", layer, stream, first)
                if stream == "main":
                    dve.wait_ge(s_rope, C.next(s_rope, 16))
                for n, b in enumerate(blocks):
                    g = v(f"gk{layer}" if b == Z_K else f"gq{layer}")
                    dve.wait_ge(root_ready, C.next(root_ready))
                    step(nc.vector.reciprocal(scr[:, 3, :T], scr[:, 2, :T]))
                    step(nc.vector.scalar_tensor_tensor(z[:, b, :T], z[:, b, :T], g, scr[:, 3, :T],
                                                   ALU.mult, ALU.mult), s_qn)
                    if stream == "main":
                        dve.wait_ge(s_rot, C.next(s_rot))
                        step(nc.vector.tensor_tensor(z[:, 13, :T], bank[2 + n % 2][:, :T], z[:, 15, :T], ALU.mult))
                        step(nc.vector.tensor_tensor(z[:, b, :T], z[:, b, :T], z[:, 14, :T], ALU.mult))
                        step(nc.vector.tensor_tensor(z[:, b, :T], z[:, b, :T], z[:, 13, :T], ALU.add))
                    if n + 1 < len(blocks):
                        mod_store(mg, mg.share(2 * n, 2 * len(blocks)).stop)
                c0 = 0 if stream == "main" else SEQ
                cols = slice(c0, c0 + T)
                step(nc.vector.tensor_copy(y_hi[:, 4, :T], z[:, Z_K, :T]))
                step(nc.vector.tensor_tensor(y_lo[:, 4, :T], z[:, Z_K, :T], f(y_hi[:, 4, :T]), ALU.subtract))
                for g in range(2):
                    s = slice(g * HEAD, (g + 1) * HEAD)
                    step(nc.vector.tensor_copy(k_pair[0:HEAD, g, cols], f(y_hi[s, 4, :T])))
                    step(nc.vector.tensor_copy(k_one[0:HEAD, g, cols], f(y_hi[s, 4, :T])))
                    step(nc.vector.tensor_copy(k_pair[HEAD:P, g, cols], f(y_lo[s, 4, :T])))
                mod_store(mg, mg.tiles)

            def attention(layer, stream, first):
                T = length(stream)
                mg = ModGroups("attn", layer, stream, first)
                step_banks = 2 if stream == "main" else 1
                n_kt = KT_ALL if stream == "main" else CTX // P
                nq = T // P

                q_own = [0]

                def queries(h):
                    b, s = h // 2, slice(h % 2 * HEAD, (h % 2 + 1) * HEAD)
                    nc.vector.tensor_copy(y_hi[s, 6 + h % 2, :T], z[s, Z_Q + b, :T]).then_inc(dve_own, 1)
                    q_own[0] = C.next(dve_own)

                def query_parts(h):
                    b, s = h // 2, slice(h % 2 * HEAD, (h % 2 + 1) * HEAD)
                    other, slot = slice(HEAD - h % 2 * HEAD, P - h % 2 * HEAD), 6 + h % 2
                    dve.wait_ge(dve_own, q_own[0])
                    nc.vector.tensor_copy(y_hi[other, slot, :T], f(y_hi[s, slot, :T])).then_inc(s_q, 1)
                    nc.vector.tensor_tensor(y_lo[0:HEAD, slot, :T], z[s, Z_Q + b, :T], f(y_hi[s, slot, :T]),
                                            ALU.subtract).then_inc(s_q, 1)
                    C.next(s_q, 2)

                def maxima(h, qts):
                    for qt in qts:
                        n = C.next(s_score)
                        dve.wait_ge(s_score, n)
                        slot = (n - 1) % 2
                        view = ring[:, step_banks * slot:step_banks * (slot + 1), :].rearrange("p a b -> p (a b)")
                        view = view[:, 0:n_kt * P]
                        nc.vector.reduce_max(mx[:, h % 2, qt:qt + 1], view, AX_X).then_inc(s_max, 1)
                        C.next(s_max)

                def parts():
                    dve.wait_ge(s_exp, C.next(s_exp, 2))
                    k = C.next(s_p)
                    if k > 2:
                        dve.wait_ge(s_pv, k - 2)
                    src, b = z[:, 13 + (k - 1) % 2, :T], 4 + (k - 1) % 2
                    nc.vector.tensor_tensor(y_lo[:, b, :T], src, f(y_hi[:, b, :T]), ALU.subtract).then_inc(s_p, 1)

                def reciprocals(half):
                    dve.wait_ge(s_on, C.next(s_on, 8))
                    step(nc.vector.reciprocal(scr[:, 2 + half, :T], scr[:, 2 + half, :T]), s_recip)

                step(nc.vector.memset(scr[:, 2:4, :], 1.0))
                queries(0)
                query_parts(0)
                maxima(0, range(nq))
                for h in range(N_HEADS):
                    if h + 1 < N_HEADS:
                        queries(h + 1)
                    if h:
                        mod_store(mg, min(mg.share(2 * h - 1, 2 * N_HEADS).stop, mg.tiles - 1))
                    parts()
                    if h + 1 < N_HEADS:
                        query_parts(h + 1)
                    parts()
                    if h + 1 < N_HEADS:
                        maxima(h + 1, (0,) if n_kt > 2 else range(nq))
                    for n in range(2, n_kt):
                        parts()
                        if h + 1 < N_HEADS:
                            maxima(h + 1, ((1, 2), (3,), (), ())[n - 2])
                    if h == 5:
                        reciprocals(0)
                reciprocals(1)
                mod_store(mg, mg.tiles)
                C.next(s_st, N_HEADS * n_kt)
                C.next(s_pv, N_HEADS * n_kt)

                def normed(b):
                    dve.wait_ge(s_spread, C.next(s_spread))
                    step(nc.vector.tensor_tensor(z[:, Z_Q + b, :T], z[:, Z_Q + b, :T], bank[b][:, :T], ALU.mult),
                         t_ready)
                lower(4, lambda k: z[:, Z_Q + k, :T], lambda k: y_lo[:, 4 + k, :T], lambda k: y_hi[:, 4 + k, :T],
                      before=normed)

            def merge(stream, first):
                T = length(stream)

                def body(c, u, off):
                    if u % R < 3:
                        dve.wait_ge(evac, C.next(evac))
                        posted()
                        return
                    done(c, off)
                    for g, ps in enumerate((ring[:, c % R, :T], bank[0][:, :T], bank[1][:, :T])):
                        step(nc.vector.tensor_tensor(scr[:, g, :T], ps, scr[:, g, :T], ALU.mult))
                    step(nc.vector.tensor_tensor(scr[:, 0, :T], scr[:, 0, :T], scr[:, 1, :T], ALU.add))
                    m = u // R
                    o = z[:, m, :T] if isinstance(off, int) else at(z[:, :, :T], m, turn[0])
                    step(nc.vector.tensor_tensor(o, scr[:, 0, :T], scr[:, 2, :T], ALU.add), post)
                grouped(dve, 32 - R, first, body, C, {evac: 3, dve_own: 4, post: R})
                for u in range(32 - R, 31):
                    body(first + u, u, 0)
                for k in range(KB):
                    if k == 0:
                        dve.sem_inc(t_ready, KB - 1)
                    if k == KB - 1:
                        body(first + 31, 31, 0)
                        dve.sem_inc(t_ready, 1)
                    dve.wait_ge(hi_ready, C.next(hi_ready))
                    issue(nc.vector.tensor_tensor(h_lo[:, k, :T], z[:, k, :T], f(h_hi[:, k, :T]), ALU.subtract), lo_ready)
                C.next(t_ready, KB)

            def residual(c, m, off, m_off, layer, stream, part):
                T, xs, s = length(stream), x_of(stream), int(stream == "ctx")
                done(c, off)
                g = part * KB + m
                g = mod[:, layer, g, s:s + 1] if isinstance(m_off, int) else \
                    mod[:, layer, bass.ds(m_off + g, 1), s:s + 1].rearrange("p o n -> p (o n)")
                o = at(xs[:, :, :T], m, m_off)
                step(nc.vector.scalar_tensor_tensor(o, ring[:, c % R, :T], g, o, ALU.mult, ALU.add), post)
                return o

            def w_o(layer, stream, first):
                T = length(stream)
                step(nc.vector.memset(scr[:, 2, :T], 0.0))

                def body(c, u, off):
                    add_squares(residual(c, u, off, off, layer, stream, 2), T)
                grouped(dve, KB, first, body, C, {post: R, dve_own: 2 * R})
                squares_done()

            def ff(layer, stream, first):
                T = length(stream)

                def body(c, u, off):
                    m = u % 16
                    if m < KB:
                        dve.wait_ge(evac, C.next(evac))
                        step(nc.vector.tensor_tensor(z[:, m % 2, :T], scr[:, m % 2, :T], scr[:, m % 2, :T], ALU.mult))
                        step(nc.vector.tensor_copy(y_hi[:, m, :T], z[:, m % 2, :T]))
                        step(nc.vector.tensor_tensor(y_lo[:, m, :T], z[:, m % 2, :T], f(y_hi[:, m, :T]),
                                                ALU.subtract), post)
                    else:
                        o = residual(c, m - KB, off, 0, layer, stream, 5)
                        add_squares(o, T, start=m == KB)
                grouped(dve, 64, first, body, C, {evac: KB, dve_own: 4 * KB - 1, post: 2 * KB}, size=16)
                squares_done()

            def post_norm(gain_of):
                column_rstd(SEQ)
                for k in range(KB + 1):
                    if k < KB:
                        nc.vector.scalar_tensor_tensor(z[:, k, :], z[:, k, :], gain_of(k), ring[:, 0, :],
                                                       ALU.mult, ALU.mult).then_inc(dve_own, 1)
                        C.next(dve_own)
                    if k:
                        dve.wait_ge(dve_own, C.now(dve_own) - (1 if k < KB else 0))
                        nc.vector.tensor_tensor(x[:, k - 1, :], x[:, k - 1, :], z[:, k - 1, :], ALU.add).then_inc(s_x, 1)
                        C.next(s_x)
                dve.wait_ge(s_x, C.now(s_x))

            def mix_out(first):
                step(nc.vector.memset(scr[:, 2, :], 0.0))

                def body(c, u, off):
                    dve.wait_ge(evac, C.next(evac))
                    posted()
                    add_squares(at(z, u, off), SEQ)
                grouped(dve, KB, first, body, C, {evac: R, post: R, dve_own: 2 * R})
                squares_done()

            def passed(n, first):
                def body(c, u, off):
                    dve.wait_ge(evac, C.next(evac))
                    posted()
                grouped(dve, n, first, body, C, {evac: R, post: R})

            def conformer():
                width, seen = 31, [0]

                def tile():
                    n = seen[0]
                    seen[0] += 1
                    dve.wait_ge(evac, C.next(evac))
                    if n < 8 and n % 2:
                        b = n // 2
                        step(nc.vector.tensor_tensor(z[:, b, :], z[:, b, :], scr[:, b % 2, :], ALU.mult), post)
                    else:
                        posted()

                for n in range(4):
                    tile()
                for pair_ in ((0, 1), (2, 3)):
                    written = {}
                    for back in range(width):
                        for b in pair_:
                            o, w_col = z[:, 4 + b, :], v("conf_w", 4 * (width - 1 - back) + b)
                            if back == 0:
                                ins = nc.vector.tensor_scalar(o, z[:, b, :], w_col, v("conf_b", b), ALU.mult, ALU.add)
                            else:
                                dve.wait_ge(dve_own, written[b])
                                ins = nc.vector.scalar_tensor_tensor(o[:, back:], z[:, b, 0:SEQ - back], w_col,
                                                                     o[:, back:], ALU.mult, ALU.add)
                            written[b] = issue(ins, s_conv if back == width - 1 else dve_own)
                        if back % 4 == 3 and seen[0] < 16:
                            tile()
                while seen[0] < 16:
                    tile()

            def lru(first):
                for pair_ in ((0, 1), (2, 3)):
                    written = {}
                    for back in range(4):
                        for b in pair_:
                            o, w_col = xv[:, b, :], v("lru_w", 4 * (3 - back) + b)
                            if back == 0:
                                ins = nc.vector.tensor_scalar(o, z[:, 8 + b, :], w_col, v("lru_b", b), ALU.mult, ALU.add)
                            else:
                                dve.wait_ge(dve_own, written[b])
                                ins = nc.vector.scalar_tensor_tensor(o[:, back:], z[:, 8 + b, 0:SEQ - back], w_col,
                                                                     o[:, back:], ALU.mult, ALU.add)
                            written[b] = issue(ins)
                    for b in pair_:
                        dve.wait_ge(dve_own, written[b])
                        written[b] = issue(nc.vector.tensor_copy(y_hi[:, 4 + b, :], xv[:, b, :]))
                    for b in pair_:
                        dve.wait_ge(dve_own, written[b])
                        issue(nc.vector.tensor_tensor(y_lo[:, 4 + b, :], xv[:, b, :], f(y_hi[:, 4 + b, :]), ALU.subtract),
                              lo_ready)
                dve.wait_ge(root_ready, C.next(root_ready))
                for b in range(4):
                    issue(nc.vector.tensor_tensor(z[:, 4 + b, :], z[:, 4 + b, :], scr[:, 2, :], ALU.subtract), t_ready)
                dve.wait_ge(root_ready, C.next(root_ready))
                step(nc.vector.reciprocal(scr[:, 3, :], scr[:, 2, :]))
                for b in range(4):
                    issue(nc.vector.scalar_tensor_tensor(z[:, 4 + b, :], z[:, 4 + b, :], v("ln_g", b), scr[:, 3, :],
                                                         ALU.mult, ALU.mult), t_ready)
                for b in range(4 + 1):
                    if b < 4:
                        dve.wait_ge(s_act, C.next(s_act))
                        issue(nc.vector.tensor_copy(y_hi[:, b, :], z[:, 4 + b, :]))
                    if b:
                        dve.wait_ge(dve_own, C.now(dve_own) - (1 if b < 4 else 0))
                        low = issue(nc.vector.tensor_tensor(y_lo[:, b - 1, :], z[:, 3 + b, :], f(y_hi[:, b - 1, :]),
                                                            ALU.subtract), lo_ready)
                dve.wait_ge(lo_ready, low)
                dve.sem_inc(s_free, 1)
                for b in range(4 + 1):
                    if b < 4:
                        dve.wait_ge(s_act, C.next(s_act))
                        less = issue(nc.vector.tensor_scalar(z[:, 4 + b, :], scr[:, b, :], -1.0, 1.0, ALU.mult, ALU.add))
                    if b:
                        dve.wait_ge(dve_own, inverse)
                        issue(nc.vector.scalar_tensor_tensor(scr[:, b - 1, :], scr[:, b - 1, :], -2.0, z[:, 3 + b, :],
                                                             ALU.mult, ALU.mult), t_ready)
                    if b < 4:
                        dve.wait_ge(dve_own, less)
                        inverse = issue(nc.vector.reciprocal(z[:, 4 + b, :], z[:, 4 + b, :]))
                dve.wait_ge(s_act, C.next(s_act, 4))
                for b in range(4):
                    x_in_ = issue(nc.vector.tensor_tensor(z[:, b, :], z[:, b, :], xv[:, b, :], ALU.mult))
                for b in range(4 + 1):
                    if b < 4:
                        dve.wait_ge(s_act, C.next(s_act))
                        dve.wait_ge(dve_own, x_in_)
                        drive = issue(nc.vector.tensor_tensor(z[:, b, :], z[:, b, :], scr[:, b, :], ALU.mult))
                    if b:
                        n = b - 1
                        dve.wait_ge(dve_own, scan)
                        gated = issue(nc.vector.tensor_tensor(xv[:, n, :], xv[:, n, :], z[:, 12 + n, :], ALU.mult))
                        if n == 0:
                            done(first)
                    if b < 4:
                        dve.wait_ge(dve_own, drive)
                        scan = issue(nc.vector.tensor_tensor_scan(xv[:, b, :], z[:, 8 + b, :], z[:, b, :], 0.0,
                                                                  ALU.mult, ALU.add))
                    if b:
                        dve.wait_ge(dve_own, gated)
                        both(xv[:, n, :], y_hi[:, 4 + n, :], y_lo[:, 4 + n, :])
                posted()

            def ffn(first):
                step(nc.vector.memset(z[:, 0:KB, :], 0.0))

                def body(c, u, off):
                    pos, n = (u % 24, 8) if u < 48 else (u - 48, 6)
                    if pos < 2 * n:
                        if pos % 2 == 0:
                            dve.wait_ge(evac, C.next(evac))
                            posted()
                            return
                        m = pos // 2
                        done(c, off)
                        step(nc.vector.tensor_tensor(z[:, 8 + m % 2, :], ring[:, c % R, :], scr[:, m % 2, :], ALU.mult))
                        step(nc.vector.tensor_copy(y_hi[:, m, :], z[:, 8 + m % 2, :]))
                        step(nc.vector.tensor_tensor(y_lo[:, m, :], z[:, 8 + m % 2, :], f(y_hi[:, m, :]),
                                                     ALU.subtract), post)
                    else:
                        m = pos - 2 * n
                        done(c, off)
                        step(nc.vector.tensor_tensor(z[:, m, :], z[:, m, :], ring[:, c % R, :], ALU.add), post)
                        if u >= 48:
                            add_squares(z[:, m, :], SEQ, start=m == 0)
                grouped(dve, FFN_TILES, first, body, C, {evac: 8, dve_own: 16, post: 24}, size=24)
                squares_done()

            def ml_gates(first):
                dve.wait_ge(evac, C.next(evac))
                posted()
                dve.sem_inc(s_row, 1)
                dve.wait_ge(s_act, C.next(s_act))
                g, low, run = scr[0:8, 0, :], scr[32:40, :, :], xv[0:8, 2, :]
                step(nc.vector.memset(scr[0:8, 3, :], 0.0))
                step(nc.vector.scalar_tensor_tensor(scr[0:8, 2, :], low[:, 0, :], 0.0, low[:, 1, :],
                                                    ALU.min, ALU.subtract))
                step(nc.vector.tensor_tensor_scan(run, scr[0:8, 2, :], scr[0:8, 3, :], 0.0, ALU.add, ALU.add))
                step(nc.vector.tensor_tensor(xv[0:8, 3, :], g, run, ALU.subtract))
                step(nc.vector.tensor_tensor_scan(scr[0:8, 2, :], scr[0:8, 3, :], xv[0:8, 3, :], 0.0, ALU.add, ALU.max))
                step(nc.vector.tensor_scalar(row[0], scr[0:8, 2, :], -1.0, None, ALU.mult))
                step(nc.vector.scalar_tensor_tensor(row[1], scr[0:8, 2, :], -1.0, run, ALU.mult, ALU.subtract))
                dve.sem_inc(s_row, 1)

            def ml_v(first):
                for half in range(2):
                    for tt in range(4):
                        dve.wait_ge(hi_ready, C.next(hi_ready))
                        b = 2 * tt + half
                        step(nc.vector.tensor_tensor(y_lo[:, b, :], bank[tt][:, :], f(y_hi[:, b, :]), ALU.subtract),
                             lo_ready)
                    for n in range(4):
                        posted()

            def mlstm():
                dve.wait_ge(s_col, C.next(s_col))
                step(nc.vector.tensor_copy(small[:, 0:32], bank[0][:, 0:32]), s_col)

                st0, prod0 = C.now(s_st), C.now(s_prod)

                def query_key_parts(h):
                    b, lo0 = 4 * (h % 2), h % 2 * HEAD
                    s, other = slice(lo0, lo0 + HEAD), slice(HEAD - lo0, P - lo0)
                    dve.wait_ge(s_qk_hi, C.next(s_qk_hi, 4))
                    issue(nc.vector.tensor_tensor(kv[0:HEAD, b + 1, :], z[s, h // 2, :], f(kv[s, b, :]), ALU.subtract), s_q)
                    issue(nc.vector.scalar_tensor_tensor(kv[other, b + 2, :], z[s, 4 + h // 2, :], HEAD ** -0.5,
                                                         f(kv[s, b + 2, :]), ALU.mult, ALU.subtract), s_q)

                def diagonal(h, n):
                    if n == 0:
                        dve.wait_ge(s_act, C.next(s_act))
                    if 4 * h + n >= 2:
                        dve.wait_ge(s_prod, 4 * h + n - 1 + prod0)
                    j = slice(n * P, (n + 1) * P)
                    issue(nc.vector.tensor_tensor(scr[:, n % 2, j], xv[:, h % 2, j], causal, ALU.add), s_diag)

                def weights(h, n):
                    dve.wait_ge(s_exp, C.next(s_exp, 2 if n < 3 else 1))
                    dve.wait_ge(s_st, C.next(s_st))
                    k = 4 * h + n
                    if k >= 2:
                        dve.wait_ge(s_p, p0 + k - 1)
                    j = slice(n * P, SEQ)
                    issue(nc.vector.tensor_tensor(scr[:, 2 + k % 2, j], ring[:, k % 2, j], scr[:, n % 2, j], ALU.mult),
                          s_prod)

                def lower_part(h, n):
                    dve.wait_ge(s_prod_hi, C.next(s_prod_hi))
                    k, j = 4 * h + n, slice(n * P, SEQ)
                    b = 8 + 2 * (k % 2)
                    issue(nc.vector.tensor_tensor(kv[:, b + 1, j], scr[:, 2 + k % 2, j], f(kv[:, b, j]), ALU.subtract), s_p)

                def denominator(h):
                    dve.wait_ge(s_pv, C.next(s_pv, 4))
                    dve.wait_ge(s_thr, C.next(s_thr))
                    if h:
                        dve.wait_ge(s_den_sq, h)
                    total = ring[96:97, 3, :]
                    step(nc.vector.tensor_tensor(den_row, total, thr_row, ALU.max))
                    issue(nc.vector.scalar_tensor_tensor(den_row, total, -1.0, den_row, ALU.mult, ALU.max), s_den)

                p0 = C.now(s_p)
                query_key_parts(0)
                diagonal(0, 0)
                diagonal(0, 1)
                weights(0, 0)
                for k in range(4 * N_HEADS):
                    h, n = divmod(k, 4)
                    if k + 1 < 4 * N_HEADS:
                        weights((k + 1) // 4, (k + 1) % 4)
                    if n == 0 and h:
                        denominator(h - 1)
                    if k + 2 < 4 * N_HEADS:
                        diagonal((k + 2) // 4, (k + 2) % 4)
                    lower_part(h, n)
                    if n == 1 and h + 1 < N_HEADS:
                        query_key_parts(h + 1)
                denominator(N_HEADS - 1)
                dve.wait_ge(root_ready, C.next(root_ready))
                issue(nc.vector.reciprocal(small[:, 0:32], small[:, 32:64]), s_rstd)
                for n in range(N_HEADS + 2):
                    if n < N_HEADS:
                        dve.wait_ge(s_rspread, C.next(s_rspread))
                        o = head_out(n)
                        scaled = issue(nc.vector.scalar_tensor_tensor(o, o, v("head_g", n), bank[n % 4][:, :],
                                                                      ALU.mult, ALU.mult), s_qn)
                    if 1 <= n <= N_HEADS:
                        o = head_out(n - 1)
                        dve.wait_ge(s_qn, scaled - (1 if n < N_HEADS else 0))
                        issue(nc.vector.tensor_tensor(o, o, z[:, 8 + n - 1, :], ALU.mult), t_ready)
                    if n >= 2:
                        dve.wait_ge(hi_ready, C.next(hi_ready))
                        issue(nc.vector.tensor_tensor(h_lo[:, n - 2, :], head_out(n - 2), f(h_hi[:, n - 2, :]),
                                                      ALU.subtract), lo_ready)

            dve.sem_inc(post, R)
            C.next(post, R)
            step(nc.vector.memset(eps[:, :], EPS), consts)
            step(nc.vector.memset(f(k_one[HEAD:HEAD + 1, :, :]), 1.0))
            step(nc.vector.memset(f(v_hi[:, :, :, HEAD:P]), 1.0))
            step(nc.vector.memset(f(v_lo[:, :, :, HEAD:P]), 0.0))
            dve.wait_ge(s_silu, 1)
            c_in = c_act[:, :].rearrange("p (s k) -> p k s", s=2)
            both(c_in, c_parts[:, :, 0:2], c_parts[:, :, 2:4])
            dve.wait_ge(s_mat, 16)
            step(nc.vector.tensor_tensor(pair[:, :], ident[0:4, 0:2], ident[0:4, 2:4], ALU.add), consts)
            step(nc.vector.tensor_copy(ones_r[:, :], ones))
            dve.wait_ge(s_vec, 16)
            dve.wait_ge(s_lam, 1)
            lam = vec[:, VCOL["lru_lam"][0]:VCOL["lru_lam"][0] + 4]
            e_, r_, q_, a_ = (small[:, i:i + 4] for i in (4, 8, 12, 16))
            step(nc.vector.tensor_scalar(r_, e_, 2.0, None, ALU.add))
            step(nc.vector.reciprocal(r_, r_))
            step(nc.vector.tensor_tensor(r_, r_, e_, ALU.mult))
            step(nc.vector.tensor_tensor(q_, r_, r_, ALU.mult))
            step(nc.vector.tensor_scalar(a_, q_, 1.0 / 17, 1.0 / 15, ALU.mult, ALU.add))
            for odd in (13, 11, 9, 7, 5, 3, 1):
                step(nc.vector.tensor_tensor(a_, a_, q_, ALU.mult))
                step(nc.vector.tensor_scalar(a_, a_, 1.0 / odd, None, ALU.add))
            step(nc.vector.scalar_tensor_tensor(a_, a_, 2.0, r_, ALU.mult, ALU.mult))
            step(nc.vector.tensor_scalar(r_, lam, -1.0, 0.0, ALU.mult, ALU.max))
            step(nc.vector.tensor_tensor(a_, a_, r_, ALU.add))
            step(nc.vector.tensor_scalar(decay[:, :], a_, -8.0, None, ALU.mult))
            for kind, layer, stream, first in steps:
                if kind == "mod":
                    dve.wait_ge(s_ctx, 16)
                    for k in range(KB):
                        add_squares(xc[:, k, :], CTX, k == 0, 0)
                    squares_done()
                    dve.wait_ge(s_in, 16)
                    for k in range(KB):
                        add_squares(x[:, k, :], SEQ, k == 0)
                    squares_done()
                    mg = ModGroups(kind, layer, stream, first)
                    mod_store(mg, mg.tiles)
                elif kind == "roots":
                    C.next(root_ready, length(stream) // P)
                elif kind == "norm1":
                    norm(layer, stream, 0)
                elif kind == "norm2":
                    norm(layer, stream, 3)
                elif kind == "z":
                    z_tiles(stream, first, 13)
                elif kind == "z_kv":
                    z_tiles(stream, first, 1)
                elif kind == "fourier":
                    fourier(layer, stream, first)
                elif kind == "qk":
                    qk(layer, stream, [Z_K] if (layer, stream) == (1, "ctx") else list(range(Z_Q, Z_K + 1)), first)
                elif kind == "attn":
                    attention(layer, stream, first)
                elif kind == "merge":
                    merge(stream, first)
                elif kind == "w_o":
                    w_o(layer, stream, first)
                elif kind == "pre_mix":
                    normed_parts(SEQ, x, lambda k: v(f"pre_mix{layer}", k))
                elif kind == "pre_ffn":
                    normed_parts(SEQ, x, lambda k: v(f"pre_ffn{layer}", k))
                elif kind == "post_mix":
                    post_norm(lambda k: v(f"post_mix{layer}", k))
                elif kind == "post_ffn":
                    post_norm(lambda k: v(f"post_ffn{layer}", k))
                elif kind == "ab_conf":
                    conformer()
                elif kind == "lru_gate":
                    lru(first)
                elif kind == "mix_out":
                    mix_out(first)
                elif kind == "ffn":
                    ffn(first)
                elif kind == "ml_qk":
                    passed(8, first)
                    passed(8, first + 8)
                elif kind == "ml_gates":
                    ml_gates(first)
                elif kind == "ml_v":
                    ml_v(first)
                elif kind == "mlstm":
                    mlstm()
                elif kind == "ff":
                    ff(layer, stream, first)
            dve.sem_inc(s_final, 1)


def arrays_of(inputs):
    w = {k: np.asarray(a) for k, a in inputs.items()}
    mats, ropes = shape_tables()
    return {
        "ws": stream_tiles(w), "vecs": vector_table(w), "mats": mats, "ropes": ropes,
        "x_t": np.ascontiguousarray(w["x"][0].T), "ctx_t": np.ascontiguousarray(w["ctx"][0].T),
        "bv": np.ascontiguousarray(w["ml_b_in_2"][:, D:2 * D]),
    }


def kernel(**inputs):
    import concourse.bacc as bacc
    from concourse.bass_utils import run_bass_kernel_spmd

    nc = bacc.Bacc("TRN2", target_bir_lowering=False, num_devices=1)
    arrays = arrays_of(inputs)
    aps = [nc.dram_tensor(n, a.shape, mybir.dt.from_np(a.dtype), kind="ExternalInput").ap() for n, a in arrays.items()]
    out = nc.dram_tensor("out_t", (D, SEQ), F32, kind="ExternalOutput").ap()
    build(nc, *aps, out)
    r = run_bass_kernel_spmd(nc, [arrays], core_ids=[0])
    return np.ascontiguousarray(r.results[0]["out_t"].T).reshape(1, SEQ, D)
```
